# Optimizing a Trainium2 kernel written in Bass

```python
import jax, jax.numpy as jnp
from jax import lax
import numpy as np

D_MODEL = 1024
BATCH = 1
SEQ = 256
DEPTH = 2

N_EVEN = (DEPTH + 1) // 2
N_ODD = DEPTH // 2
D_PLE = 256
EPS = 1e-6

CONV_GROUPS = 8
CONV_GROUP_DIM = 64
CONV_DIM = CONV_GROUPS * CONV_GROUP_DIM
CONV_WIDTH = 3
GMLP_HEADS = 8
GMLP_HEAD_DIM = 64
GMLP_DIM = GMLP_HEADS * GMLP_HEAD_DIM
GMLP_CHUNK = 128
EVEN_IN = 3 * CONV_DIM + 2 * GMLP_DIM
EVEN_MIX = CONV_DIM + GMLP_DIM

MLA_HEADS = 8
MLA_NOPE = 64
MLA_ROPE = 32
MLA_V = 64
MLA_QK = MLA_NOPE + MLA_ROPE
Q_LORA = 384
KV_LORA = 256
ROPE_THETA = 10000.0
ATTN_BLOCK = 128
MLSTM_HEADS = 4
MLSTM_QK = 64
MLSTM_V = 128
MLSTM_CHUNK = 64
ODD_IN = Q_LORA + KV_LORA + MLA_ROPE + 2 * MLSTM_HEADS * MLSTM_QK + 2 * MLSTM_HEADS * MLSTM_V + 2 * MLSTM_HEADS
ODD_MIX = MLA_HEADS * MLA_V + MLSTM_HEADS * MLSTM_V

D_FF = -(-8 * D_MODEL // (3 * 256)) * 256


def rmsnorm(x, g):
    xf = x.astype(jnp.float32)
    y = xf * lax.rsqrt(jnp.mean(xf * xf, axis=-1, keepdims=True) + EPS)
    return (y * g.astype(jnp.float32)).astype(x.dtype)

def swiglu(h, w_gate, w_up, w_down):
    return (jax.nn.silu(h @ w_gate) * (h @ w_up)) @ w_down

def short_gated_conv(b_gate, c_gate, x_in, w_conv):
    z = c_gate * x_in
    conv = lax.conv_general_dilated(
        z, w_conv[:, None, :].astype(z.dtype), window_strides=(1,),
        padding=[(CONV_WIDTH - 1, 0)], dimension_numbers=('NWC', 'WIO', 'NWC'),
        feature_group_count=CONV_DIM)
    return b_gate * conv

def chunked_spatial_gating(u, v, g_v, w_s, b_s):
    bsz, seq, _ = u.shape
    n_chunks = seq // GMLP_CHUNK
    shape5 = (bsz, n_chunks, GMLP_CHUNK, GMLP_HEADS, GMLP_HEAD_DIM)
    u = jax.nn.gelu(u).reshape(shape5)
    v = rmsnorm(jax.nn.gelu(v).reshape(shape5), g_v)
    causal = jnp.tril(jnp.ones((GMLP_CHUNK, GMLP_CHUNK), dtype=w_s.dtype))
    mixed = jnp.einsum('hts,bnshd->bnthd', w_s * causal, v) + b_s.T[:, :, None]
    return (u * mixed).reshape(bsz, seq, GMLP_DIM)

def rope_tables(positions, dim, dtype):
    inv_freq = ROPE_THETA ** (-jnp.arange(0, dim, 2, dtype=jnp.float32) / dim)
    ang = positions.astype(jnp.float32)[..., None] * inv_freq
    return jnp.cos(ang)[:, :, None, :].astype(dtype), jnp.sin(ang)[:, :, None, :].astype(dtype)

def apply_rope(x, cos, sin):
    half = x.shape[-1] // 2
    x1, x2 = x[..., :half], x[..., half:]
    return jnp.concatenate([x1 * cos - x2 * sin, x2 * cos + x1 * sin], axis=-1)

def causal_block_attention(q, k, v):
    bsz, seq, heads, dk = q.shape
    n_blocks = seq // ATTN_BLOCK
    q_blocks = q.reshape(bsz, n_blocks, ATTN_BLOCK, heads, dk).transpose(1, 0, 2, 3, 4)
    k_idx = jnp.arange(seq)
    scale = dk ** -0.5

    def one_block(args):
        qi, bi = args
        s = jnp.einsum('bqhd,bkhd->bhqk', qi, k).astype(jnp.float32) * scale
        q_idx = bi * ATTN_BLOCK + jnp.arange(ATTN_BLOCK)
        s = jnp.where(k_idx[None, :] <= q_idx[:, None], s, -jnp.inf)
        pr = jax.nn.softmax(s, axis=-1).astype(v.dtype)
        return jnp.einsum('bhqk,bkhv->bqhv', pr, v)

    out = lax.map(one_block, (q_blocks, jnp.arange(n_blocks)))
    return out.transpose(1, 0, 2, 3, 4).reshape(bsz, seq, heads, v.shape[-1])

def latent_attention(q_lat, kv_lat, k_pe, positions, g_qa, g_kva, w_q_up, w_kv_up, g_q, g_k):
    bsz, seq, _ = q_lat.shape
    q = (rmsnorm(q_lat, g_qa) @ w_q_up).reshape(bsz, seq, MLA_HEADS, MLA_QK)
    kv = (rmsnorm(kv_lat, g_kva) @ w_kv_up).reshape(bsz, seq, MLA_HEADS, MLA_NOPE + MLA_V)
    k_nope, v = kv[..., :MLA_NOPE], kv[..., MLA_NOPE:]
    cos, sin = rope_tables(positions, MLA_ROPE, q.dtype)
    q_nope = rmsnorm(q[..., :MLA_NOPE], g_q[:MLA_NOPE])
    q_pe = apply_rope(rmsnorm(q[..., MLA_NOPE:], g_q[MLA_NOPE:]), cos, sin)
    k_nope = rmsnorm(k_nope, g_k[:MLA_NOPE])
    k_pe = apply_rope(rmsnorm(k_pe[:, :, None, :], g_k[MLA_NOPE:]), cos, sin)
    q = jnp.concatenate([q_nope, q_pe], axis=-1)
    k = jnp.concatenate([k_nope, jnp.broadcast_to(k_pe, (bsz, seq, MLA_HEADS, MLA_ROPE))], axis=-1)
    return causal_block_attention(q, k, v).reshape(bsz, seq, MLA_HEADS * MLA_V)

def mlstm_chunkwise(q, k, v, i_pre, f_pre):
    out_dtype = v.dtype
    bsz, seq, heads, dk = q.shape
    dv = v.shape[-1]
    L = MLSTM_CHUNK
    nc = seq // L
    f32 = jnp.float32

    def to_chunks(a):
        return a.astype(f32).reshape(bsz, nc, L, heads, -1).transpose(1, 0, 3, 2, 4)

    def gate_chunks(a):
        return a.astype(f32).reshape(bsz, nc, L, heads).transpose(1, 0, 3, 2)

    qc = to_chunks(q) * (dk ** -0.5)
    kc, vc = to_chunks(k), to_chunks(v)
    ic = gate_chunks(i_pre)
    ac = jnp.cumsum(jax.nn.log_sigmoid(gate_chunks(f_pre)), axis=-1)
    causal = jnp.tril(jnp.ones((L, L), dtype=bool))

    def step(carry, xs):
        c_mat, n_vec, m = carry
        qb, kb, vb, ib, ab = xs
        d = jnp.where(causal, ab[..., :, None] - ab[..., None, :] + ib[..., None, :], -jnp.inf)
        inter = ab + m[..., None]
        m_t = jnp.maximum(inter, jnp.max(d, axis=-1))
        w_intra = jnp.exp(d - m_t[..., None])
        w_inter = jnp.exp(inter - m_t)
        s = jnp.einsum('bhtd,bhsd->bhts', qb, kb) * w_intra
        num = jnp.einsum('bhts,bhsv->bhtv', s, vb) + w_inter[..., None] * jnp.einsum('bhtd,bhvd->bhtv', qb, c_mat)
        den = jnp.sum(s, axis=-1) + w_inter * jnp.einsum('bhtd,bhd->bht', qb, n_vec)
        h = num / jnp.maximum(jnp.abs(den), jnp.exp(-m_t))[..., None]
        a_last = ab[..., -1]
        m_new = m_t[..., -1]
        w_s = jnp.exp(a_last[..., None] - ab + ib - m_new[..., None])
        decay = jnp.exp(a_last + m - m_new)
        c_new = decay[..., None, None] * c_mat + jnp.einsum('bhs,bhsv,bhsd->bhvd', w_s, vb, kb)
        n_new = decay[..., None] * n_vec + jnp.einsum('bhs,bhsd->bhd', w_s, kb)
        return (c_new, n_new, m_new), h

    init = (jnp.zeros((bsz, heads, dv, dk), f32), jnp.zeros((bsz, heads, dk), f32), jnp.zeros((bsz, heads), f32))
    _, hs = lax.scan(step, init, (qc, kc, vc, ic, ac))
    return hs.transpose(1, 0, 3, 2, 4).reshape(bsz, seq, heads, dv).astype(out_dtype)

def even_mixer(hn, w_in, w_conv, g_v, w_s, b_s, w_out):
    z = hn @ w_in
    b_gate, c_gate, x_in, u, v = jnp.split(z, [CONV_DIM, 2 * CONV_DIM, 3 * CONV_DIM, 3 * CONV_DIM + GMLP_DIM], axis=-1)
    y_a = short_gated_conv(b_gate, c_gate, x_in, w_conv)
    y_b = chunked_spatial_gating(u, v, g_v, w_s, b_s)
    return jnp.concatenate([y_a, y_b], axis=-1) @ w_out

def odd_mixer(hn, positions, w_in, b_gate, g_qa, g_kva, w_q_up, w_kv_up, g_q, g_k, g_mh, w_out):
    bsz, seq, _ = hn.shape
    z = hn @ w_in
    sizes = [Q_LORA, KV_LORA, MLA_ROPE, MLSTM_HEADS * MLSTM_QK, MLSTM_HEADS * MLSTM_QK,
             MLSTM_HEADS * MLSTM_V, MLSTM_HEADS * MLSTM_V, MLSTM_HEADS, MLSTM_HEADS]
    q_lat, kv_lat, k_pe, mq, mk, mv, mo, mi, mf = jnp.split(z, np.cumsum(sizes)[:-1].tolist(), axis=-1)
    y_c = latent_attention(q_lat, kv_lat, k_pe, positions, g_qa, g_kva, w_q_up, w_kv_up, g_q, g_k)
    h_m = mlstm_chunkwise(mq.reshape(bsz, seq, MLSTM_HEADS, MLSTM_QK),
                          mk.reshape(bsz, seq, MLSTM_HEADS, MLSTM_QK),
                          mv.reshape(bsz, seq, MLSTM_HEADS, MLSTM_V),
                          mi + b_gate[:MLSTM_HEADS], mf + b_gate[MLSTM_HEADS:])
    y_d = jax.nn.sigmoid(mo) * rmsnorm(h_m, g_mh).reshape(bsz, seq, MLSTM_HEADS * MLSTM_V)
    return jnp.concatenate([y_c, y_d], axis=-1) @ w_out

def first_inputs(seed: int = 0) -> dict:
    key = jax.random.key(seed)
    ks = list(jax.random.split(key, 40))
    f32 = jnp.float32

    def normal(shape):
        return jax.random.normal(ks.pop(), shape, f32)

    def dense(shape, fan_in):
        return normal(shape) * fan_in ** -0.5

    def gain(shape):
        return 1.0 + 0.05 * normal(shape)

    x = normal((BATCH, SEQ, D_MODEL))
    p = normal((DEPTH, BATCH, SEQ, D_PLE))
    positions = jnp.arange(SEQ, dtype=jnp.int32)[None, :] + jax.random.randint(ks.pop(), (BATCH, 1), 0, SEQ, dtype=jnp.int32)
    od_b_gate = jnp.concatenate([0.1 * normal((N_ODD, MLSTM_HEADS)), 3.0 + 0.1 * normal((N_ODD, MLSTM_HEADS))], axis=-1)
    return {
        'x': x,
        'p': p,
        'positions': positions,
        'g_mix': gain((DEPTH, D_MODEL)),
        'g_ffn': gain((DEPTH, D_MODEL)),
        'g_ple': gain((DEPTH, D_MODEL)),
        'ev_w_in': dense((N_EVEN, D_MODEL, EVEN_IN), D_MODEL),
        'ev_w_conv': dense((N_EVEN, CONV_WIDTH, CONV_DIM), CONV_WIDTH),
        'ev_g_v': gain((N_EVEN, GMLP_HEADS, GMLP_HEAD_DIM)),
        'ev_w_s': dense((N_EVEN, GMLP_HEADS, GMLP_CHUNK, GMLP_CHUNK), GMLP_CHUNK),
        'ev_b_s': 1.0 + 0.1 * normal((N_EVEN, GMLP_HEADS, GMLP_CHUNK)),
        'ev_w_out': dense((N_EVEN, EVEN_MIX, D_MODEL), EVEN_MIX),
        'od_w_in': dense((N_ODD, D_MODEL, ODD_IN), D_MODEL),
        'od_b_gate': od_b_gate,
        'od_g_qa': gain((N_ODD, Q_LORA)),
        'od_g_kva': gain((N_ODD, KV_LORA)),
        'od_w_q_up': dense((N_ODD, Q_LORA, MLA_HEADS * MLA_QK), Q_LORA),
        'od_w_kv_up': dense((N_ODD, KV_LORA, MLA_HEADS * (MLA_NOPE + MLA_V)), KV_LORA),
        'od_g_q': gain((N_ODD, MLA_QK)),
        'od_g_k': gain((N_ODD, MLA_QK)),
        'od_g_mh': gain((N_ODD, MLSTM_HEADS, MLSTM_V)),
        'od_w_out': dense((N_ODD, ODD_MIX, D_MODEL), ODD_MIX),
        'w_gate': dense((DEPTH, D_MODEL, D_FF), D_MODEL),
        'w_up': dense((DEPTH, D_MODEL, D_FF), D_MODEL),
        'w_down': dense((DEPTH, D_FF, D_MODEL), D_FF),
        'w_ple_proj': dense((DEPTH, D_PLE, D_MODEL), D_PLE),
        'w_ple_gate': dense((DEPTH, D_MODEL, D_MODEL), D_MODEL),
    }

def first_block(x, p, positions, g_mix, g_ffn, g_ple, ev_w_in, ev_w_conv, ev_g_v, ev_w_s, ev_b_s, ev_w_out,
              od_w_in, od_b_gate, od_g_qa, od_g_kva, od_w_q_up, od_w_kv_up, od_g_q, od_g_k, od_g_mh, od_w_out,
              w_gate, w_up, w_down, w_ple_proj, w_ple_gate):
    h = x
    for layer in range(DEPTH):
        j = layer // 2
        hn = rmsnorm(h, g_mix[layer])
        if layer % 2 == 0:
            mix = even_mixer(hn, ev_w_in[j], ev_w_conv[j], ev_g_v[j], ev_w_s[j], ev_b_s[j], ev_w_out[j])
        else:
            mix = odd_mixer(hn, positions, od_w_in[j], od_b_gate[j], od_g_qa[j], od_g_kva[j], od_w_q_up[j],
                            od_w_kv_up[j], od_g_q[j], od_g_k[j], od_g_mh[j], od_w_out[j])
        h = h + mix
        h = h + swiglu(rmsnorm(h, g_ffn[layer]), w_gate[layer], w_up[layer], w_down[layer])
        gate = jax.nn.sigmoid(rmsnorm(h, g_ple[layer]) @ w_ple_gate[layer])
        h = h + gate * (p[layer] @ w_ple_proj[layer])
    return h


DEPTH_2 = 1

N_MIXERS = 4
CONV_WIDTH_2 = 31
HGRN_EXPAND = 128
HGRN_HEADS = D_MODEL // HGRN_EXPAND
HGRN_CHUNK = 64
POOL_WINDOWS = (2, 4, 8, 16)
POOL_GROUPS = len(POOL_WINDOWS)
POOL_DIM = D_MODEL // POOL_GROUPS
SB_HEADS = 16
SB_HEAD_DIM = D_MODEL // SB_HEADS
SB_BLOCK = 128
MOE_GROUPS = 4
MOE_EXPERTS_PER_GROUP = 8
MOE_EXPERTS = MOE_GROUPS * MOE_EXPERTS_PER_GROUP
MOE_TOP_K = 2
MOE_HIDDEN = D_MODEL // 2
MOE_BLOCK = 128


def _n_layers_of(m):
    return (DEPTH_2 - m + N_MIXERS - 1) // N_MIXERS

def rmsnorm_2(x, g):
    xf = x.astype(jnp.float32)
    y = xf * lax.rsqrt(jnp.mean(xf * xf, axis=-1, keepdims=True) + EPS) * g.astype(jnp.float32)
    return y.astype(x.dtype)

def layernorm(x, g, b):
    xf = x.astype(jnp.float32)
    mu = jnp.mean(xf, axis=-1, keepdims=True)
    xc = xf - mu
    y = xc * lax.rsqrt(jnp.mean(xc * xc, axis=-1, keepdims=True) + EPS) * g + b
    return y.astype(x.dtype)

def conformer_conv(h, w_in, b_in, w_dw, b_dw, ln_g, ln_b, w_out):
    u = h @ w_in + b_in
    a, gt = jnp.split(u, 2, axis=-1)
    u = a * jax.nn.sigmoid(gt)
    y = lax.conv_general_dilated(
        u, w_dw[:, None, :], window_strides=(1,),
        padding=[(CONV_WIDTH_2 - 1, 0)],
        dimension_numbers=('NWC', 'WIO', 'NWC'),
        feature_group_count=D_MODEL) + b_dw
    y = jax.nn.silu(layernorm(y, ln_g, ln_b))
    return (y @ w_out).astype(h.dtype)

def hgrn_lower_bounds(logits):
    p = jax.nn.softmax(logits.astype(jnp.float32), axis=0)
    cum = jnp.cumsum(p, axis=0)
    return cum - cum[0:1]

def hgrn2(h, w_in, lb, norm_g, w_out):
    B, S, _ = h.shape
    H, dh, C = HGRN_HEADS, HGRN_EXPAND, HGRN_CHUNK
    n_chunk = S // C
    q, f, i_in, g = jnp.split((h @ w_in).astype(jnp.float32), 4, axis=-1)
    q = jax.nn.silu(q)
    forget = lb + (1.0 - lb) * jax.nn.sigmoid(f)
    log_f = jnp.log(forget)
    k = (1.0 - lb) * jax.nn.sigmoid(-f)

    def chunks(t):
        return t.reshape(B, n_chunk, C, H, dh).transpose(1, 0, 3, 2, 4)

    causal = jnp.tril(jnp.ones((C, C), bool))[:, :, None]

    def step(state, inp):
        qc, kc, vc, lfc = inp
        b = jnp.cumsum(lfc, axis=2)
        o_inter = jnp.einsum('bhtk,bhkv->bhtv', qc * jnp.exp(b), state)
        rel = jnp.where(causal, b[:, :, :, None, :] - b[:, :, None, :, :], -jnp.inf)
        scores = jnp.einsum('bhtk,bhsk,bhtsk->bhts', qc, kc, jnp.exp(rel))
        o_intra = jnp.einsum('bhts,bhsv->bhtv', scores, vc)
        b_end = b[:, :, -1:, :]
        state = (jnp.exp(b_end[:, :, 0, :, None]) * state
                 + jnp.einsum('bhsk,bhsv->bhkv', kc * jnp.exp(b_end - b), vc))
        return state, o_inter + o_intra

    state0 = jnp.zeros((B, H, dh, dh), jnp.float32)
    _, o = lax.scan(step, state0, (chunks(q), chunks(k), chunks(i_in), chunks(log_f)))
    o = o.transpose(1, 0, 3, 2, 4).reshape(B, S, H, dh)
    o = o * lax.rsqrt(jnp.mean(o * o, axis=-1, keepdims=True) + EPS) * norm_g.reshape(H, dh)
    o = o.reshape(B, S, D_MODEL) * jax.nn.silu(g)
    return (o.astype(h.dtype) @ w_out).astype(h.dtype)

def multiscale_pool(h, w_grp, b_grp, ls):
    B, S, _ = h.shape
    hf = h.astype(jnp.float32).reshape(B, S, POOL_GROUPS, POOL_DIM)
    cs0 = jnp.pad(jnp.cumsum(hf, axis=1), ((0, 0), (1, 0), (0, 0), (0, 0)))
    pos = jnp.arange(S)
    outs = []
    for gi, w in enumerate(POOL_WINDOWS):
        c_g = cs0[:, :, gi]
        upper = c_g[:, 1:]
        lower = jnp.pad(c_g, ((0, 0), (w - 1, 0), (0, 0)))[:, :S]
        count = jnp.minimum(pos + 1, w).astype(jnp.float32)[None, :, None]
        outs.append((upper - lower) / count - hf[:, :, gi])
    pooled = jnp.stack(outs, axis=2)
    y = jnp.einsum('bsgc,gcd->bsgd', pooled, w_grp.astype(jnp.float32))
    y = y.reshape(B, S, D_MODEL) + b_grp
    return (y * ls).astype(h.dtype)

def stick_breaking_attention(h, w_qkv, w_out):
    B, S, _ = h.shape
    qkv = (h @ w_qkv).reshape(B, S, 3, SB_HEADS, SB_HEAD_DIM)
    q = qkv[:, :, 0].transpose(0, 2, 1, 3)
    k = qkv[:, :, 1].transpose(0, 2, 1, 3)
    v = qkv[:, :, 2].transpose(0, 2, 1, 3)
    n_blk = S // SB_BLOCK
    q_blocks = q.reshape(B, SB_HEADS, n_blk, SB_BLOCK, SB_HEAD_DIM).transpose(2, 0, 1, 3, 4)
    key_pos = jnp.arange(S)
    scale = SB_HEAD_DIM ** -0.5

    def one_block(args):
        qb, bi = args
        z = jnp.einsum('bhtd,bhsd->bhts', qb, k).astype(jnp.float32) * scale
        q_pos = bi * SB_BLOCK + jnp.arange(SB_BLOCK)
        strict = key_pos[None, :] < q_pos[:, None]
        log_keep = jnp.where(strict, jax.nn.log_sigmoid(-z), 0.0)
        later = lax.cumsum(log_keep, axis=3, reverse=True) - log_keep
        weights = jnp.where(strict, jnp.exp(jax.nn.log_sigmoid(z) + later), 0.0)
        return jnp.einsum('bhts,bhsd->bhtd', weights.astype(v.dtype), v)

    o = lax.map(one_block, (q_blocks, jnp.arange(n_blk)))
    o = o.transpose(1, 0, 3, 2, 4).reshape(B, S, D_MODEL)
    return (o @ w_out).astype(h.dtype)

def hier_moe(h, w_rg, b_rg, w_re, b_re, w_gate, w_up, w_down):
    B, S, D = h.shape
    T = B * S
    xt = h.reshape(T, D)
    grp_logits = (xt @ w_rg + b_rg).astype(jnp.float32)
    grp = jnp.argmax(grp_logits, axis=-1)
    grp_p = jnp.take_along_axis(jax.nn.softmax(grp_logits, axis=-1), grp[:, None], axis=1)[:, 0]
    exp_logits = (xt @ w_re + b_re).astype(jnp.float32).reshape(T, MOE_GROUPS, MOE_EXPERTS_PER_GROUP)
    in_grp = jnp.take_along_axis(exp_logits, grp[:, None, None], axis=1)[:, 0]
    top_val, top_idx = lax.top_k(in_grp, MOE_TOP_K)
    gate = grp_p[:, None] * jax.nn.softmax(top_val, axis=-1)
    expert = grp[:, None] * MOE_EXPERTS_PER_GROUP + top_idx

    n_assign = T * MOE_TOP_K
    e_flat = expert.reshape(n_assign).astype(jnp.int32)
    g_flat = gate.reshape(n_assign)
    t_flat = jnp.repeat(jnp.arange(T, dtype=jnp.int32), MOE_TOP_K)
    order = jnp.argsort(e_flat)
    e_s, t_s, g_s = e_flat[order], t_flat[order], g_flat[order]
    counts = jnp.bincount(e_flat, length=MOE_EXPERTS).astype(jnp.int32)
    padded = ((counts + MOE_BLOCK - 1) // MOE_BLOCK) * MOE_BLOCK
    seg_start = jnp.cumsum(counts) - counts
    pad_end = jnp.cumsum(padded)
    pad_start = pad_end - padded
    dest = pad_start[e_s] + (jnp.arange(n_assign, dtype=jnp.int32) - seg_start[e_s])
    n_slots = n_assign + MOE_EXPERTS * MOE_BLOCK
    n_blk = n_slots // MOE_BLOCK
    slot_tok = jnp.full((n_slots,), T, jnp.int32).at[dest].set(t_s)
    slot_gate = jnp.zeros((n_slots,), jnp.float32).at[dest].set(g_s)
    blk_start = jnp.arange(n_blk, dtype=jnp.int32) * MOE_BLOCK
    blk_expert = jnp.minimum(jnp.searchsorted(pad_end, blk_start, side='right'),
                             MOE_EXPERTS - 1).astype(jnp.int32)
    x_pad = jnp.concatenate([xt, jnp.zeros((1, D), xt.dtype)], axis=0)
    xs = x_pad[slot_tok].reshape(n_blk, MOE_BLOCK, D)

    def run_block(args):
        xb, e = args
        hid = jax.nn.silu(xb @ w_gate[e]) * (xb @ w_up[e])
        return hid @ w_down[e]

    ys = lax.map(run_block, (xs, blk_expert)).reshape(n_slots, D)
    out = jnp.zeros((T + 1, D), jnp.float32).at[slot_tok].add(
        ys.astype(jnp.float32) * slot_gate[:, None])[:T]
    return out.reshape(B, S, D).astype(h.dtype)

def second_inputs(seed: int = 0) -> dict:
    key = jax.random.key(seed)
    ks = iter(jax.random.split(key, 40))

    def nrm(shape, scale):
        return jax.random.normal(next(ks), shape, jnp.float32) * scale

    D = D_MODEL
    NA, NB, NC, ND = (_n_layers_of(m) for m in range(N_MIXERS))
    inv = D ** -0.5
    E, F = MOE_EXPERTS, MOE_HIDDEN
    return {
        "x": nrm((BATCH, SEQ, D), 1.0),
        "c": nrm((BATCH, D), 1.0),
        "ada_w": nrm((DEPTH_2, D, 6 * D), 0.5 * inv),
        "ada_b": nrm((DEPTH_2, 6 * D), 0.02),
        "norm_mix_g": 1.0 + nrm((DEPTH_2, D), 0.05),
        "norm_ffn_g": 1.0 + nrm((DEPTH_2, D), 0.05),
        "final_g": 1.0 + nrm((D,), 0.05),
        "conv_w_in": nrm((NA, D, 2 * D), inv),
        "conv_b_in": nrm((NA, 2 * D), 0.02),
        "conv_w_dw": nrm((NA, CONV_WIDTH_2, D), CONV_WIDTH_2 ** -0.5),
        "conv_b_dw": nrm((NA, D), 0.02),
        "conv_ln_g": 1.0 + nrm((NA, D), 0.05),
        "conv_ln_b": nrm((NA, D), 0.02),
        "conv_w_out": nrm((NA, D, D), inv),
        "hgrn_w_in": nrm((NB, D, 4 * D), inv),
        "hgrn_lb_logits": nrm((DEPTH_2, D), 0.5),
        "hgrn_norm_g": 1.0 + nrm((NB, D), 0.05),
        "hgrn_w_out": nrm((NB, D, D), inv),
        "pool_w": nrm((NC, POOL_GROUPS, POOL_DIM, POOL_DIM), POOL_DIM ** -0.5),
        "pool_b": nrm((NC, D), 0.02),
        "pool_scale": 1.0 + nrm((NC, D), 0.1),
        "sb_w_qkv": nrm((ND, D, 3 * D), inv),
        "sb_w_out": nrm((ND, D, D), inv),
        "moe_w_rg": nrm((DEPTH_2, D, MOE_GROUPS), inv),
        "moe_b_rg": nrm((DEPTH_2, MOE_GROUPS), 0.01),
        "moe_w_re": nrm((DEPTH_2, D, E), inv),
        "moe_b_re": nrm((DEPTH_2, E), 0.01),
        "moe_w_gate": nrm((DEPTH_2, E, D, F), inv),
        "moe_w_up": nrm((DEPTH_2, E, D, F), inv),
        "moe_w_down": nrm((DEPTH_2, E, F, D), F ** -0.5),
    }

def second_block(x, c, ada_w, ada_b, norm_mix_g, norm_ffn_g, final_g,
              conv_w_in, conv_b_in, conv_w_dw, conv_b_dw, conv_ln_g, conv_ln_b, conv_w_out,
              hgrn_w_in, hgrn_lb_logits, hgrn_norm_g, hgrn_w_out,
              pool_w, pool_b, pool_scale,
              sb_w_qkv, sb_w_out,
              moe_w_rg, moe_b_rg, moe_w_re, moe_b_re, moe_w_gate, moe_w_up, moe_w_down):
    c_act = jax.nn.silu(c)
    lb_all = hgrn_lower_bounds(hgrn_lb_logits)
    for i in range(DEPTH_2):
        m, j = i % N_MIXERS, i // N_MIXERS
        mod = c_act @ ada_w[i] + ada_b[i]
        sh1, sc1, g1, sh2, sc2, g2 = [t[:, None, :] for t in jnp.split(mod, 6, axis=-1)]
        h = rmsnorm_2(x, norm_mix_g[i]) * (1 + sc1) + sh1
        if m == 0:
            y = conformer_conv(h, conv_w_in[j], conv_b_in[j], conv_w_dw[j], conv_b_dw[j],
                               conv_ln_g[j], conv_ln_b[j], conv_w_out[j])
        elif m == 1:
            y = hgrn2(h, hgrn_w_in[j], lb_all[i], hgrn_norm_g[j], hgrn_w_out[j])
        elif m == 2:
            y = multiscale_pool(h, pool_w[j], pool_b[j], pool_scale[j])
        else:
            y = stick_breaking_attention(h, sb_w_qkv[j], sb_w_out[j])
        x = x + g1 * y
        h = rmsnorm_2(x, norm_ffn_g[i]) * (1 + sc2) + sh2
        x = x + g2 * hier_moe(h, moe_w_rg[i], moe_b_rg[i], moe_w_re[i], moe_b_re[i],
                              moe_w_gate[i], moe_w_up[i], moe_w_down[i])
    return rmsnorm_2(x, final_g)


def setup_inputs(seed=0):
    out = dict(first_inputs(seed))
    for name, value in second_inputs(seed + 1).items():
        if name != "x":
            out[name + "_2"] = value
    return out


def reference(
    x, p, positions, g_mix, g_ffn, g_ple, ev_w_in, ev_w_conv, ev_g_v, ev_w_s, ev_b_s, ev_w_out,
    od_w_in, od_b_gate, od_g_qa, od_g_kva, od_w_q_up, od_w_kv_up, od_g_q, od_g_k, od_g_mh,
    od_w_out, w_gate, w_up, w_down, w_ple_proj, w_ple_gate, c_2, ada_w_2, ada_b_2, norm_mix_g_2,
    norm_ffn_g_2, final_g_2, conv_w_in_2, conv_b_in_2, conv_w_dw_2, conv_b_dw_2, conv_ln_g_2,
    conv_ln_b_2, conv_w_out_2, hgrn_w_in_2, hgrn_lb_logits_2, hgrn_norm_g_2, hgrn_w_out_2,
    pool_w_2, pool_b_2, pool_scale_2, sb_w_qkv_2, sb_w_out_2, moe_w_rg_2, moe_b_rg_2,
    moe_w_re_2, moe_b_re_2, moe_w_gate_2, moe_w_up_2, moe_w_down_2,
):
    x = first_block(
        x, p, positions, g_mix, g_ffn, g_ple, ev_w_in, ev_w_conv, ev_g_v, ev_w_s, ev_b_s,
        ev_w_out, od_w_in, od_b_gate, od_g_qa, od_g_kva, od_w_q_up, od_w_kv_up, od_g_q, od_g_k,
        od_g_mh, od_w_out, w_gate, w_up, w_down, w_ple_proj, w_ple_gate,
    )
    return second_block(
        x, c_2, ada_w_2, ada_b_2, norm_mix_g_2, norm_ffn_g_2, final_g_2, conv_w_in_2,
        conv_b_in_2, conv_w_dw_2, conv_b_dw_2, conv_ln_g_2, conv_ln_b_2, conv_w_out_2,
        hgrn_w_in_2, hgrn_lb_logits_2, hgrn_norm_g_2, hgrn_w_out_2, pool_w_2, pool_b_2,
        pool_scale_2, sb_w_qkv_2, sb_w_out_2, moe_w_rg_2, moe_b_rg_2, moe_w_re_2, moe_b_re_2,
        moe_w_gate_2, moe_w_up_2, moe_w_down_2,
    )


_drawn_inputs = setup_inputs


def setup_inputs(seed=0):
    import zlib

    import numpy as np

    out = dict(_drawn_inputs(seed))
    spreads = {}
    factors = {'g_ple': 4.353,
     'ev_g_v': 3.758,
     'od_g_qa': 8.0,
     'od_g_kva': 8.0,
     'od_g_q': 8.0,
     'od_g_k': 8.0,
     'od_g_mh': 4.839,
     'ada_b_2': 5.266,
     'norm_mix_g_2': 8.0,
     'norm_ffn_g_2': 5.127,
     'conv_b_in_2': 8.0,
     'conv_b_dw_2': 8.0,
     'conv_ln_g_2': 8.0,
     'conv_ln_b_2': 8.0,
     'moe_b_rg_2': 8.0,
     'moe_b_re_2': 22.256}
    for name, (base, spread) in spreads.items():
        noise = np.random.default_rng([zlib.crc32(name.encode()), seed]).standard_normal(out[name].shape)
        drawn = base * np.exp(spread * noise) if base else spread * noise
        out[name] = __import__('jax').numpy.asarray(drawn.astype(out[name].dtype))
    for name, factor in factors.items():
        out[name] = (out[name] * factor).astype(out[name].dtype)
    return out
```

```python
from contextlib import ExitStack, contextmanager

import numpy as np

import concourse.bass as bass
from concourse import mybir

F32 = mybir.dt.float32
I32 = mybir.dt.int32
ALU = mybir.AluOpType
ACT = mybir.ActivationFunctionType
AX = mybir.AxisListType

P = 128
D = 1024
S = 256
T = S // P
KC = D // P
EPS = 1e-6
NEG = -1e30

CONV_DIM = 512
GM_HEADS, GM_HD = 8, 64
Q_LORA, KV_LORA = 384, 256
HEADS, NOPE, ROPE, VD = 8, 64, 32, 64
QK = NOPE + ROPE
MH, MQK, MV = 4, 64, 128
ROPE_THETA = 10000.0
ODD_IN = Q_LORA + KV_LORA + ROPE + 2 * MH * MQK + 2 * MH * MV + 2 * MH
AT_KPE = Q_LORA + KV_LORA
AT_MQ = AT_KPE + ROPE
AT_MK = AT_MQ + MH * MQK
AT_MV = AT_MK + MH * MQK
AT_MO = AT_MV + MH * MV
AT_MI = AT_MO + MH * MV
D_FF = 2816
TAPS = 31
GROUPS, PER_GROUP = 4, 8
EXPERTS = GROUPS * PER_GROUP
EXPERT_HID = 512

BLK = 256
FF_BLOCKS = D_FF // BLK
HALVES = EXPERT_HID // BLK
MOE_BLOCKS = EXPERTS * HALVES
PLACES = 64
SLOT = 3 * KC * BLK
RING = 4
AT_DOWN = 2 * KC * BLK

ITEMS = [("ev_in", 1, 5), ("ev_out", 1, 2), ("ffn0", 3, FF_BLOCKS), ("ple0", 2, 2),
         ("od_in", 1, 5), ("od_up", 2, 1), ("od_out", 1, 2), ("ffn1", 3, FF_BLOCKS), ("ple1", 2, 2),
         ("conv_in", 2, 4), ("conv_out", 1, 2), ("moe", 3, MOE_BLOCKS)]
FIRST, LANDED = {}, []
_slot_count = [0] * RING
for _name, _dmas, _n in ITEMS:
    FIRST[_name] = len(LANDED)
    for _ in range(_n):
        _s = len(LANDED) % RING
        _slot_count[_s] += 16 * _dmas
        LANDED.append(_slot_count[_s])

ROWS_A, ROWS_B = {}, {}
for _rows, _names in ((ROWS_A, [("g_mix", 16), ("g_ffn", 16), ("g_ple", 16), ("norm_mix_g_2", 8), ("norm_ffn_g_2", 8),
                                ("conv_b_dw_2", 8), ("conv_ln_g_2", 8), ("conv_ln_b_2", 8), ("conv_b_in_2", 16),
                                ("od_g_qa", 3), ("od_g_kva", 2), ("ev_w_conv", 12)]),
                      (ROWS_B, [("ada_b_2", 48), ("ev_b_s", 8), ("c_2", 8)])):
    _at = 0
    for _n, _c in _names:
        _rows[_n] = (_at, _c)
        _at += _c
N_ROWS_A = sum(c for _, c in ROWS_A.values())
N_ROWS_B = sum(c for _, c in ROWS_B.values())


class Own:

    def __init__(self, eng, sem):
        self.eng, self.sem, self.n = eng, sem, 0

    def __call__(self, ins):
        self.n += 1
        ins.then_inc(self.sem, 1)
        self.eng.wait_ge(self.sem, self.n)


def build(nc, a, out, stop_after=None):
    ctx = ExitStack()
    with ctx:
        def sb(name, shape, dt=F32):
            return ctx.enter_context(nc.sbuf_tensor(name, shape, dt))

        def sem(name):
            return ctx.enter_context(nc.semaphore(name))

        ring = [sb(f"weights{s}", [P, SLOT]) for s in range(RING)]
        h = sb("h", [P, T, D])
        hnT = sb("hnT", [P, KC, S])
        xn = sb("xn", [P, T, D])
        mixT = sb("mixT", [P, KC, S])
        ident = sb("ident", [P, P])
        ones = sb("ones", [P, P])
        mean_w = sb("mean_w", [P, P])
        upper = sb("upper", [P, P])
        cmask = sb("cmask", [P, 3 * P])
        wsT = sb("wsT", [P, GM_HEADS, P])
        pT = sb("pT", [P, 2, 2, S])
        cols_a = sb("cols_a", [P, P])
        cols_b = sb("cols_b", [P, P])
        w_dw = sb("w_dw", [P, KC, TAPS])
        g_v = sb("g_v", [P, GM_HEADS * GM_HD])
        g_q = sb("g_q", [P, QK])
        g_k = sb("g_k", [P, QK])
        g_mh = sb("g_mh", [P, MH * MV])
        b_gate = sb("b_gate", [P, 2 * MH])
        b_route = sb("b_route", [P, GROUPS + EXPERTS])
        w_route = sb("w_route", [P, KC, GROUPS + EXPERTS])
        rev = sb("rev", [P, EXPERTS])
        pos_i = sb("pos_i", [P, T], I32)
        ms = sb("ms", [P, 64])
        rs = sb("rs", [P, 64])
        rtmp = sb("rtmp", [P, 2, 64])
        c_act = sb("c_act", [P, KC])
        mod_cols = sb("mod_cols", [P, 4, KC])
        gate_half = sb("gate_half", [P, T, EXPERTS])
        places = sb("places", [P, 2 * PLACES])
        ps = ctx.enter_context(nc.psum_tensor("ps", [P, 8, 512], F32))

        def col(name, c, n=1):
            rows, tile = (ROWS_A, cols_a) if name in ROWS_A else (ROWS_B, cols_b)
            at = rows[name][0] + c
            return tile[:, at:at + n]

        @contextmanager
        def scope():
            with ExitStack() as inner:
                yield lambda name, shape, dt=F32: inner.enter_context(nc.sbuf_tensor(name, shape, dt))

        with scope() as st:
            ws_rows = st("ws_rows", [P, GM_HEADS, P])
            p_rows = st("p_rows", [P, 2, T, 256])
            rows_a = st("rows_a", [P, P])
            rows_b = st("rows_b", [P, P])
            dw_rows = st("dw_rows", [TAPS, D])
            rev_i = st("rev_i", [P, EXPERTS], I32)
            places_i = st("places_i", [P, 2 * PLACES], I32)
        with scope() as st:
            ev_x = st("ev_x", [P, 4, S])
            ev_z = st("ev_z", [P, 4, S + 2])
            ev_y = st("ev_y", [P, 4, S])
            gm_v = st("gm_v", [P, T, 512])
            gm_u = st("gm_u", [P, T, 512])
            gm_t = st("gm_t", [P, T, 512])
            gm_s = st("gm_s", [P, T, 512])
        with scope() as st:
            od_z = st("od_z", [P, T, ODD_IN])
            od_q = st("od_q", [P, T, HEADS, QK])
            od_kv = st("od_kv", [P, T, HEADS, NOPE + VD])
            od_k = st("od_k", [P, T, HEADS, QK])
            mqkT = st("mqkT", [P, 4, S])
            cs = st("cs", [P, 2, T, ROPE // 2])
            ang = st("ang", [P, T, ROPE // 2])
            inv_freq = st("inv_freq", [P, ROPE // 2])
            posf = st("posf", [P, T])
            turns = st("turns", [P, T, ROPE // 2])
            sm = st("sm", [P, 2, 3 * P])
            prob = st("prob", [P, 2, 3 * P])
            probT = st("probT", [P, 2, 3 * P])
            nmax = st("nmax", [P, HEADS + MH, T])
            rsum = st("rsum", [P, T, HEADS])
            gts = st("gts", [P, T, 2 * MH])
            lf = st("lf", [P, 3, T, MH])
            acum = st("acum", [P, T, MH])
            bcol = st("bcol", [P, T, MH])
            emt = st("emt", [P, T, MH])
            den = st("den", [P, 2, T])
        lat = xn[:, :, 0:Q_LORA + KV_LORA]
        latT = mixT[:, 0:5, :]
        qT, kT = hnT, mixT
        v_aug = od_q[:].rearrange("p t h d -> p (t h d)")[:, 0:T * MH * (MV + 1)].rearrange(
            "p (t h d) -> p t h d", t=T, h=MH)
        b_masked = od_k[:].rearrange("p t h d -> p (t h d)").rearrange("p (h n) -> p h n", h=MH)
        diag_b = xn[:].rearrange("p t d -> p (t d)")[:, 0:T * MH * P].rearrange("p (t h n) -> p t h n", t=T, h=MH)
        mix = xn
        y_d = mix[:, :, HEADS * VD:].rearrange("p t (h d) -> p t h d", h=MH)
        with scope() as st:
            g_bc = st("g_bc", [P, 2, D])
            ff_th = st("ff_th", [P, T, BLK])
            ff_a = st("ff_a", [P, T, BLK])
            ff_hid = st("ff_hid", [P, 2, T, BLK])
            ff_hidT = st("ff_hidT", [P, 2, S])
            with scope() as st2:
                ada_acc = st2("ada_acc", [P, 6 * D])
                with scope() as st3:
                    ada_w = st3("ada_w", [P, 2, KC, BLK])
                with scope() as st3:
                    ple_th = st3("ple_th", [P, 2, T, 512])
                    ple_a = st3("ple_a", [P, T, 512])
            with scope() as st2:
                f_bc = st2("f_bc", [P, D])
                place = st2("place", [P, T, EXPERTS])
                crowded = st2("crowded", [P, 1], I32)
                with scope() as st3:
                    u_pad = st3("u_pad", [P, KC, S + TAPS - 1])
                    cf_th = st3("cf_th", [P, 2, S])
                    cf_a = st3("cf_a", [P, 2, S])
                    cf_r = st3("cf_r", [P, 4, S])
                    half = st3("half", [P, 4 * KC])
                with scope() as st3:
                    rt = st3("rt", [P, 9, T, EXPERTS])
                    rts = st3("rts", [P, 11, T])
                with scope() as st3:
                    ge_sel = st3("ge_sel", [P, T, PLACES])
                    ge_share = st3("ge_share", [P, 2, T, 2 * PLACES])
                    ge_xT = st3("ge_xT", [P, KC, PLACES])
                    ge_th = st3("ge_th", [P, BLK])
                    ge_a = st3("ge_a", [P, BLK])
                    ge_hid = st3("ge_hid", [P, BLK])
                    ge_turned = st3("ge_turned", [P, 4, P])
                    ge_y = st3("ge_y", [P, 512])

        landed = [sem(f"weights_landed{s}") for s in range(RING)]
        weights_used = sem("weights_used")
        stage_over = sem("stage_over")
        small_landed = sem("small_landed")
        out_landed = sem("out_landed")
        dve_own = sem("dve_own")
        ada_landed = [sem("ada_landed0"), sem("ada_landed1")]
        ada_used = sem("ada_used")
        ends = {}

        def stage_end(eng):
            ends[id(eng)] = ends.get(id(eng), 0) + 1
            eng.drain().then_inc(stage_over, 1)
            eng.wait_ge(stage_over, 4 * ends[id(eng)])

        def slot(item):
            return ring[item % RING]

        def wait_weights(eng, item, it=None):
            value = LANDED[item] if it is None else LANDED[item] + 48 * it
            eng.wait_ge(landed[item % RING], value)

        def cols8(item, n=512):
            return slot(item)[:, 0:KC * n].rearrange("p (k n) -> p k n", k=KC)

        def weight_stream(sp):
            def free(item, it=None):
                if item >= RING:
                    value = item - RING + 1
                    sp.wait_ge(weights_used, value if it is None else value + 4 * it)

            def load(item, dst, src):
                sp.dma_start(dst, src).then_inc(landed[item % RING], 16)

            def columns(name, w, starts, width):
                wv = w.rearrange("(k p) n -> p k n", p=P)
                for i, c in enumerate(starts):
                    item = FIRST[name] + i
                    free(item)
                    n = min(width, w.shape[1] - c)
                    load(item, slot(item)[:, 0:KC * n].rearrange("p (k n) -> p k n", k=KC), wv[:, :, c:c + n])

            def gated(item, it, gate, up, down):
                free(item, it)
                gu = slot(item)[:, 0:AT_DOWN].rearrange("p (k two n) -> p k two n", k=KC, two=2)
                load(item, gu[:, :, 0, :], gate)
                load(item, gu[:, :, 1, :], up)
                load(item, slot(item)[:, AT_DOWN:SLOT].rearrange("p (c d) -> p c d", c=2), down)

            def ffn(layer):
                g = a["w_gate"][layer].rearrange("(k p) f -> p k f", p=P)
                u = a["w_up"][layer].rearrange("(k p) f -> p k f", p=P)
                d = a["w_down"][layer].rearrange("(n c p) d -> p n c d", p=P, c=2)
                first = FIRST[f"ffn{layer}"]

                def block(n, it):
                    m = n if it is None else n + 4 * it
                    gated(first + n, it, g[:, :, bass.ds(m * BLK, BLK)], u[:, :, bass.ds(m * BLK, BLK)], d[:, m])
                with sp.Fori(0, FF_BLOCKS // 4) as it:
                    for j in range(4):
                        block(j, it)
                for n in range(FF_BLOCKS // 4 * 4, FF_BLOCKS):
                    block(n, None)

            def ple(layer):
                w = a["w_ple_gate"][layer].rearrange("(k p) n -> p k n", p=P)
                q = a["w_ple_proj"][layer].rearrange("(k p) n -> p k n", p=P)
                for i in range(2):
                    item = FIRST[f"ple{layer}"] + i
                    free(item)
                    load(item, cols8(item), w[:, :, i * 512:(i + 1) * 512])
                    load(item, slot(item)[:, KC * 512:(KC + 2) * 512].rearrange("p (k n) -> p k n", k=2),
                         q[:, :, i * 512:(i + 1) * 512])

            columns("ev_in", a["ev_w_in"][0], [2048, 1536, 512, 1024, 0], 512)
            columns("ev_out", a["ev_w_out"][0], [0, 512], 512)
            ffn(0)
            ple(0)
            columns("od_in", a["od_w_in"][0], range(0, ODD_IN, 512), 512)
            item = FIRST["od_up"]
            free(item)
            load(item, slot(item)[:, 0:3 * 768].rearrange("p (k n) -> p k n", k=3),
                 a["od_w_q_up"][0].rearrange("(k p) n -> p k n", p=P))
            load(item, slot(item)[:, 3 * 768:3 * 768 + 2 * 1024].rearrange("p (k n) -> p k n", k=2),
                 a["od_w_kv_up"][0].rearrange("(k p) n -> p k n", p=P))
            columns("od_out", a["od_w_out"][0], [0, 512], 512)
            ffn(1)
            ple(1)
            w = a["conv_w_in_2"][0].rearrange("(k p) n -> p k n", p=P)
            for i in range(4):
                item = FIRST["conv_in"] + i
                free(item)
                ag = slot(item)[:, 0:AT_DOWN].rearrange("p (k two n) -> p k two n", k=KC, two=2)
                for j in range(2):
                    load(item, ag[:, :, j, :], w[:, :, j * D + i * BLK:j * D + (i + 1) * BLK])
            columns("conv_out", a["conv_w_out_2"][0], [0, 512], 512)
            g = a["moe_w_gate_2"][0].rearrange("e (k p) f -> p e k f", p=P)
            u = a["moe_w_up_2"][0].rearrange("e (k p) f -> p e k f", p=P)
            d = a["moe_w_down_2"][0].rearrange("e (c p) d -> p e c d", p=P)
            with sp.Fori(0, MOE_BLOCKS // 4) as it:
                for j in range(4):
                    e, f = it * 2 + j // 2, j % 2
                    gated(FIRST["moe"] + j, it, g[:, e, :, f * BLK:(f + 1) * BLK], u[:, e, :, f * BLK:(f + 1) * BLK],
                          d[:, e, 2 * f:2 * f + 2, :])

        def rsqrt(dve, own, x, y, t0, t1, done=None):
            own(dve.tensor_scalar(x, x, EPS, None, ALU.add))
            own(dve.tensor_scalar(t0.bitcast(I32), x.bitcast(I32), 1, None, ALU.logical_shift_right))
            own(dve.tensor_scalar(y.bitcast(I32), t0.bitcast(I32), -1.0, float(0x5F3759DF), ALU.mult, ALU.add))
            for i in range(3):
                own(dve.tensor_tensor(t0, y, y, ALU.mult))
                own(dve.scalar_tensor_tensor(out=t1, in0=t0, scalar=-0.5, in1=x, op0=ALU.mult, op1=ALU.mult))
                last = dve.scalar_tensor_tensor(out=y, in0=t1, scalar=1.5, in1=y, op0=ALU.add, op1=ALU.mult)
                if i < 2 or done is None:
                    own(last)
            if done is not None:
                last.then_inc(done, 1)

        def rsqrt_ms(dve, own, n, done=None):
            rsqrt(dve, own, ms[:, 0:n], rs[:, 0:n], rtmp[:, 0, 0:n], rtmp[:, 1, 0:n], done)

        class NormStage:
            squares, rstd, scaled, turned = (sem("norm_" + n) for n in ("squares", "rstd", "scaled", "turned"))

            def __init__(self, index, gain, shift=None):
                self.index, self.gain, self.shift = index, gain, shift

            def act(self, act):
                for t in range(T):
                    act.activation(xn[:, t], h[:, t], ACT.Square, scale=float(D) ** -0.5,
                                   accum_out=ms[:, t:t + 1]).then_inc(self.squares, 1)
                act.wait_ge(self.rstd, self.index + 1)
                act.activation(xn[:, 0], h[:, 0], ACT.Copy, scale=rs[:, 0:1]).then_inc(self.scaled, 1)
                for b in (1, 3):
                    act.wait_ge(self.turned, 4 * self.index + b + 1)
                    for c in (2 * b, 2 * b + 1):
                        src = ps[:, b, (c % 2) * S:(c % 2 + 1) * S]
                        bias = 0.0 if self.shift is None else self.shift(c)
                        act.activation(hnT[:, c, :], src, ACT.Identity, scale=self.gain(c), bias=bias)
                stage_end(act)

            def dve(self, dve, own):
                dve.wait_ge(self.squares, T * (self.index + 1))
                rsqrt_ms(dve, own, T, self.rstd)
                dve.wait_ge(self.rstd, self.index + 1)
                dve.tensor_scalar(xn[:, 1], h[:, 1], rs[:, 1:2], None, ALU.mult).then_inc(self.scaled, 1)
                for b in (0, 2):
                    dve.wait_ge(self.turned, 4 * self.index + b + 1)
                    for c in (2 * b, 2 * b + 1):
                        src = ps[:, b, (c % 2) * S:(c % 2 + 1) * S]
                        if self.shift is None:
                            dve.tensor_scalar(hnT[:, c, :], src, self.gain(c), None, ALU.mult)
                        else:
                            dve.tensor_scalar(hnT[:, c, :], src, self.gain(c), self.shift(c), ALU.mult, ALU.add)
                stage_end(dve)

            def pe(self, pe):
                pe.wait_ge(self.scaled, T * (self.index + 1))
                for b in range(4):
                    for c in (2 * b, 2 * b + 1):
                        for t in range(T):
                            at = (c % 2) * S + t * P
                            last = pe.transpose(ps[:, b, at:at + P], xn[:, t, c * P:(c + 1) * P], ident[:])
                    last.then_inc(self.turned, 1)
                stage_end(pe)

        class GatedStage:
            def __init__(self, name, blocks, routed, side=None):
                self.side = side
                self.first, self.blocks, self.routed = FIRST[name], blocks, routed
                self.gate_up = sem(f"{name}_gate_up")
                self.tanh = sem(f"{name}_tanh")
                self.half = sem(f"{name}_half")
                self.hid = sem(f"{name}_hid")
                self.turned = sem(f"{name}_turned")
                self.hidT = sem(f"{name}_hidT")
                self.loops = (blocks - 2) // 4

            def blocks_in_loop(self, eng, step):
                with eng.Fori(0, self.loops) as it:
                    for j in range(4):
                        step(2 + j, it)
                for n in range(2 + 4 * self.loops, self.blocks):
                    step(n, None)

            @staticmethod
            def at(value, per_block, it):
                return value if it is None else value + 4 * per_block * it

            def pe(self, pe):
                at = self.at

                def gate_up(n, it, t):
                    if t == 0:
                        wait_weights(pe, self.first + n, it)
                    if n >= 1:
                        pe.wait_ge(self.hid, at(2 * (n - 1) + t + 1, 2, it))
                    w = cols8(self.first + n)
                    for k in range(KC):
                        last = pe.matmul(ps[:, t, :], hnT[:, k, t * P:(t + 1) * P], w[:, k, :],
                                         start=(k == 0), stop=(k == KC - 1))
                    last.then_inc(self.gate_up, 1)

                def turn(n, it):
                    pe.wait_ge(self.hid, at(2 * n + 2, 2, it))
                    if n >= 1:
                        pe.wait_ge(self.hidT, at(n, 1, it))
                    for c in range(2):
                        for t in range(T):
                            last = pe.transpose(ps[:, 2, c * S + t * P:c * S + (t + 1) * P],
                                                ff_hid[:, n % 2, t, c * P:(c + 1) * P], ident[:])
                    last.then_inc(self.turned, 1)

                def down(n, it):
                    pe.wait_ge(self.hidT, at(n + 1, 1, it))
                    w = slot(self.first + n)[:, AT_DOWN:SLOT].rearrange("p (c d) -> p c d", c=2)
                    for t in range(T):
                        for half in range(2):
                            for c in range(2):
                                last = pe.matmul(ps[:, 4 + 2 * t + half, :], ff_hidT[:, c, t * P:(t + 1) * P],
                                                 w[:, c, half * 512:(half + 1) * 512],
                                                 start=(n == 0 and c == 0), stop=(n == self.blocks - 1 and c == 1))
                    last.then_inc(weights_used, 1)

                def step(n, it):
                    gate_up(n, it, 0)
                    turn(n - 1, it)
                    gate_up(n, it, 1)
                    down(n - 1, it)

                gate_up(0, None, 0)
                gate_up(0, None, 1)
                step(1, None)
                self.blocks_in_loop(pe, step)
                turn(self.blocks - 1, None)
                down(self.blocks - 1, None)
                if not self.routed:
                    stage_end(pe)

            def act(self, act):
                at = self.at

                def tanh(n, it, t):
                    act.wait_ge(self.gate_up, at(2 * n + t + 1, 2, it))
                    act.activation(ff_th[:, t], ps[:, t, 0:BLK], ACT.Tanh, scale=0.5).then_inc(self.tanh, 1)

                def copy(n, it):
                    act.wait_ge(self.turned, at(n + 1, 1, it))
                    act.copy(ff_hidT[:], ps[:, 2, :].rearrange("p (c s) -> p c s", c=2)).then_inc(self.hidT, 1)

                def step(n, it):
                    tanh(n, it, 0)
                    copy(n - 1, it)
                    tanh(n, it, 1)

                tanh(0, None, 0)
                tanh(0, None, 1)
                step(1, None)
                self.blocks_in_loop(act, step)
                copy(self.blocks - 1, None)
                if not self.routed:
                    stage_end(act)

            def dve(self, dve, own):
                at = self.at

                def step(n, it):
                    for t in range(T):
                        dve.wait_ge(self.tanh, at(2 * n + t + 1, 2, it))
                        dve.scalar_tensor_tensor(out=ff_a[:, t], in0=ff_th[:, t], scalar=1.0, in1=ps[:, t, 0:BLK],
                                                 op0=ALU.add, op1=ALU.mult).then_inc(self.half, 1)
                        if n >= 2:
                            dve.wait_ge(self.turned, at(n - 1, 1, it))
                        dve.wait_ge(self.half, at(2 * n + t + 1, 2, it))
                        if self.routed:
                            e = n // HALVES if it is None else n // HALVES + it * (4 // HALVES)
                            share = gate_half[:, t, bass.ds(e, 1)]
                        else:
                            share = 0.5
                        dve.scalar_tensor_tensor(out=ff_hid[:, n % 2, t], in0=ff_a[:, t], scalar=share,
                                                 in1=ps[:, t, BLK:2 * BLK], op0=ALU.mult,
                                                 op1=ALU.mult).then_inc(self.hid, 1)
                    if self.side is not None and it is not None:
                        self.side(dve, n - 2, it)

                step(0, None)
                step(1, None)
                self.blocks_in_loop(dve, step)
                dve.wait_ge(weights_used, self.first + self.blocks)
                if not self.routed:
                    for t in range(T):
                        for half in range(2):
                            o = h[:, t, half * 512:(half + 1) * 512]
                            dve.tensor_tensor(o, o, ps[:, 4 + 2 * t + half, :], ALU.add)
                    stage_end(dve)

        class PleStage:
            def __init__(self, layer):
                self.layer, self.first = layer, FIRST[f"ple{layer}"]
                self.made = sem(f"ple{layer}_made")
                self.tanh = sem(f"ple{layer}_tanh")

            def pe(self, pe):
                for i in range(2):
                    wait_weights(pe, self.first + i)
                    w = cols8(self.first + i)
                    q = slot(self.first + i)[:, KC * 512:(KC + 2) * 512].rearrange("p (k n) -> p k n", k=2)
                    for t in range(T):
                        for k in range(KC):
                            pe.matmul(ps[:, 4 * i + 2 * t, :], hnT[:, k, t * P:(t + 1) * P], w[:, k, :],
                                      start=(k == 0), stop=(k == KC - 1))
                        for k in range(2):
                            last = pe.matmul(ps[:, 4 * i + 2 * t + 1, :], pT[:, self.layer, k, t * P:(t + 1) * P],
                                             q[:, k, :], start=(k == 0), stop=(k == 1))
                        last.then_inc(self.made if t == 0 else weights_used, 1)
                stage_end(pe)

            def act(self, act):
                for i in range(2):
                    for t in range(T):
                        if t == 0:
                            act.wait_ge(self.made, i + 1)
                        else:
                            act.wait_ge(weights_used, self.first + i + 1)
                        act.activation(ple_th[:, i, t], ps[:, 4 * i + 2 * t, :], ACT.Tanh,
                                       scale=0.5).then_inc(self.tanh, 1)
                stage_end(act)

            def dve(self, dve, own):
                for i in range(2):
                    for t in range(T):
                        dve.wait_ge(self.tanh, 2 * i + t + 1)
                        own(dve.scalar_tensor_tensor(out=ple_a[:, t], in0=ple_th[:, i, t], scalar=1.0,
                                                     in1=ps[:, 4 * i + 2 * t + 1, :], op0=ALU.add, op1=ALU.mult))
                        o = h[:, t, i * 512:(i + 1) * 512]
                        own(dve.scalar_tensor_tensor(out=o, in0=ple_a[:, t], scalar=0.5, in1=o,
                                                     op0=ALU.mult, op1=ALU.add))
                stage_end(dve)

        class SetupStage:
            def __init__(self):
                self.consts = sem("consts_made")
                self.own_consts = sem("consts_under_way")
                self.turned = sem("setup_turned")
                self.h_landed = sem("h_landed")
                self.cols = sem("setup_cols")

            def loads(self):
                for name, dst in (("ev_g_v", g_v), ("od_g_mh", g_mh)):
                    yield dst[:], a[name][0].rearrange("h d -> (h d)").partition_broadcast(P)
                yield g_q[:], a["od_g_q"][0].partition_broadcast(P)
                yield g_k[:], a["od_g_k"][0].partition_broadcast(P)
                yield b_gate[:], a["od_b_gate"][0].partition_broadcast(P)
                yield b_route[:, 0:GROUPS], a["moe_b_rg_2"][0].partition_broadcast(P)
                yield b_route[:, GROUPS:], a["moe_b_re_2"][0].partition_broadcast(P)
                yield w_route[:, :, 0:GROUPS], a["moe_w_rg_2"][0].rearrange("(k p) n -> p k n", p=P)
                yield w_route[:, :, GROUPS:], a["moe_w_re_2"][0].rearrange("(k p) n -> p k n", p=P)
                yield pos_i[:], a["positions"].rearrange("b (t p) -> p (b t)", p=P)
                yield ws_rows[:], a["ev_w_s"][0].rearrange("h t s -> t h s")
                for layer in range(2):
                    yield p_rows[:, layer], a["p"][layer, 0].rearrange("(t p) d -> p t d", p=P)
                yield dw_rows[:], a["conv_w_dw_2"][0]
                for rows, tile in ((ROWS_A, rows_a), (ROWS_B, rows_b)):
                    for name, (at, n) in rows.items():
                        v = a[name]
                        flat = v.rearrange(" ".join("abcd"[:len(v.shape)]) + " -> (" + " ".join("abcd"[:len(v.shape)]) + ")")
                        yield tile[at:at + n, :], flat.rearrange("(c p) -> c p", p=P)

            def act(self, act):
                act.dma_start(h[:], a["x"][0].rearrange("(t p) d -> p t d", p=P)).then_inc(self.h_landed, 16)
                n = 0
                for dst, src in self.loads():
                    act.dma_start(dst, src, allow_slow_non_contiguous=dst.dtype == I32).then_inc(small_landed, 16)
                    n += 16
                self.all_landed = n
                act.wait_ge(self.h_landed, 16)
                act.wait_ge(self.turned, 2)
                act.copy(wsT[:, 0:4], ps[:, 0, :].rearrange("p (h n) -> p h n", h=4))
                act.copy(wsT[:, 4:8], ps[:, 1, :].rearrange("p (h n) -> p h n", h=4))
                act.wait_ge(self.turned, 4)
                for layer in range(2):
                    act.copy(pT[:, layer], ps[:, 2 + layer, :].rearrange("p (c s) -> p c s", c=2))
                act.wait_ge(self.turned, 6)
                act.copy(cols_a[:, 0:N_ROWS_A], ps[:, 4, 0:N_ROWS_A])
                act.copy(cols_b[:, 0:N_ROWS_B], ps[:, 5, 0:N_ROWS_B]).then_inc(self.cols, 1)
                act.wait_ge(self.cols, 1)
                act.activation(c_act[:], col("c_2", 0, KC), ACT.Tanh, scale=0.5)
                act.wait_ge(self.turned, 7)
                act.copy(w_dw[:], ps[:, 6, 0:KC * TAPS].rearrange("p (c j) -> p c j", c=KC))
                stage_end(act)

            def pool(self, pool):
                own = Own(pool, self.own_consts)
                pool.memset(ones[:], 1.0)
                pool.memset(mean_w[:], 1.0 / D)
                pool.memset(cmask[:], 0.0)
                pool.iota(rev_i[:], pattern=[[-1, EXPERTS]], base=EXPERTS, channel_multiplier=0)
                pool.iota(places_i[:], pattern=[[0, 2], [1, PLACES]], base=0, channel_multiplier=0)
                pool.memset(ms[:], 0.0)
                own(pool.memset(ident[:], 0.0))
                own(pool.affine_select(out=ident[:], in_=ident[:], compare_op=ALU.not_equal, fill=1.0, base=0,
                                       pattern=[[-1, P]], channel_multiplier=1))
                own(pool.affine_select(out=upper[:], in_=ones[:], compare_op=ALU.is_ge, fill=0.0, base=0,
                                       pattern=[[1, P]], channel_multiplier=-1))
                for at in (0, 2 * P):
                    own(pool.affine_select(out=cmask[:, at:at + P], in_=cmask[:, at:at + P], compare_op=ALU.is_ge,
                                           fill=NEG, base=0, pattern=[[-1, P]], channel_multiplier=1))
                pool.tensor_copy(places[:], places_i[:])
                pool.tensor_copy(rev[:], rev_i[:]).then_inc(self.consts, 1)
                stage_end(pool)

            def pe(self, pe):
                pe.wait_ge(self.consts, 1)
                pe.wait_ge(small_landed, self.all_landed)
                for hd in range(GM_HEADS):
                    last = pe.transpose(ps[:, hd // 4, (hd % 4) * P:(hd % 4 + 1) * P], ws_rows[:, hd], ident[:])
                    if hd % 4 == 3:
                        last.then_inc(self.turned, 1)
                for layer in range(2):
                    for c in range(2):
                        for t in range(T):
                            last = pe.transpose(ps[:, 2 + layer, c * S + t * P:c * S + (t + 1) * P],
                                                p_rows[:, layer, t, c * P:(c + 1) * P], ident[:])
                    last.then_inc(self.turned, 1)
                for tile, n, b in ((rows_a, N_ROWS_A, 4), (rows_b, N_ROWS_B, 5)):
                    pe.transpose(ps[:, b, 0:n], tile[0:n, :], ident[0:n, 0:n]).then_inc(self.turned, 1)
                for c in range(KC):
                    last = pe.transpose(ps[:, 6, c * TAPS:(c + 1) * TAPS], dw_rows[:, c * P:(c + 1) * P],
                                        ident[0:TAPS, 0:TAPS])
                last.then_inc(self.turned, 1)
                stage_end(pe)

            def dve(self, dve, own):
                stage_end(dve)
                own(dve.tensor_tensor(wsT[:], wsT[:], upper[:].unsqueeze(1).to_broadcast([P, GM_HEADS, P]), ALU.mult))
                own(dve.scalar_tensor_tensor(out=c_act[:], in0=c_act[:], scalar=1.0, in1=col("c_2", 0, KC), op0=ALU.add,
                                             op1=ALU.mult))
                own(dve.tensor_scalar(c_act[:], c_act[:], 0.5, None, ALU.mult))

        class EvenStage:
            def __init__(self):
                self.v_copied = sem("ev_v_copied")
                self.u_copied = sem("ev_u_copied")
                self.x_copied = sem("ev_x_copied")
                self.v_tanh_in = sem("ev_v_tanh_in")
                self.v_tanh = sem("ev_v_tanh")
                self.u_tanh_in = sem("ev_u_tanh_in")
                self.u_tanh = sem("ev_u_tanh")
                self.vn = sem("ev_vn")
                self.mixed = sem("ev_mixed")
                self.y_b = sem("ev_y_b")
                self.y_turned = sem("ev_y_turned")
                self.y_copied = sem("ev_y_copied")
                self.mixT_ready = sem("ev_mixT_ready")
                self.first, self.out = FIRST["ev_in"], FIRST["ev_out"]

            def pe(self, pe):
                for i in range(2):
                    wait_weights(pe, self.first + i)
                    w = cols8(self.first + i)
                    for t in range(T):
                        for k in range(KC):
                            last = pe.matmul(ps[:, 2 * i + t, :], hnT[:, k, t * P:(t + 1) * P], w[:, k, :],
                                             start=(k == 0), stop=(k == KC - 1))
                    last.then_inc(weights_used, 1)
                for i in range(3):
                    wait_weights(pe, self.first + 2 + i)
                    w = cols8(self.first + 2 + i)
                    if i == 2:
                        pe.wait_ge(self.v_copied, 1)
                    for f in range(4):
                        b = (4, 6, 0)[i] + f // 2
                        for k in range(KC):
                            last = pe.matmul(ps[:, b, (f % 2) * S:(f % 2 + 1) * S], w[:, k, f * P:(f + 1) * P],
                                             hnT[:, k, :], start=(k == 0), stop=(k == KC - 1))
                    last.then_inc(weights_used, 1)
                pe.wait_ge(self.vn, 1)
                pe.wait_ge(self.u_copied, 1)
                for t in range(T):
                    for hd in range(GM_HEADS):
                        last = pe.matmul(ps[:, 2 + t, hd * GM_HD:(hd + 1) * GM_HD], wsT[:, hd, :],
                                         gm_v[:, t, hd * GM_HD:(hd + 1) * GM_HD], start=True, stop=True)
                last.then_inc(self.mixed, 1)
                pe.wait_ge(self.y_b, 1)
                for c in range(4):
                    for t in range(T):
                        at = (c % 2) * S + t * P
                        last = pe.transpose(ps[:, 4 + c // 2, at:at + P], gm_s[:, t, c * P:(c + 1) * P], ident[:])
                last.then_inc(self.y_turned, 1)
                pe.wait_ge(self.mixT_ready, 1)
                pe.wait_ge(self.y_copied, 1)
                for i in range(2):
                    wait_weights(pe, self.out + i)
                    w = cols8(self.out + i)
                    for t in range(T):
                        b = (6, 7, 0, 1)[2 * i + t]
                        for k in range(KC):
                            last = pe.matmul(ps[:, b, :], mixT[:, k, t * P:(t + 1) * P], w[:, k, :],
                                             start=(k == 0), stop=(k == KC - 1))
                    last.then_inc(weights_used, 1)
                stage_end(pe)

            def act(self, act):
                act.wait_ge(weights_used, self.first + 1)
                act.copy(gm_v[:], ps[:, 0:2, :]).then_inc(self.v_copied, 1)
                act.wait_ge(weights_used, self.first + 2)
                act.copy(gm_u[:], ps[:, 2:4, :]).then_inc(self.u_copied, 1)
                act.wait_ge(self.v_tanh_in, 1)
                act.activation(gm_t[:], gm_t[:], ACT.Tanh, scale=0.7978845608028654).then_inc(self.v_tanh, 1)
                act.wait_ge(weights_used, self.first + 4)
                act.copy(ev_x[:], ps[:, 6:8, :].rearrange("p b (c s) -> p (b c) s", c=2)).then_inc(self.x_copied, 1)
                act.wait_ge(self.u_tanh_in, 1)
                act.activation(gm_s[:], gm_s[:], ACT.Tanh, scale=0.7978845608028654).then_inc(self.u_tanh, 1)
                act.wait_ge(self.y_turned, 1)
                act.copy(mixT[:, 4:8, :], ps[:, 4:6, :].rearrange("p b (c s) -> p (b c) s", c=2)).then_inc(self.y_copied, 1)
                stage_end(act)

            def dve(self, dve, own):
                def gelu_in(x, t, done):
                    own(dve.tensor_tensor(t, x, x, ALU.mult))
                    own(dve.tensor_scalar(t, t, 0.044715, 1.0, ALU.mult, ALU.add))
                    dve.tensor_tensor(t, t, x, ALU.mult).then_inc(done, 1)

                own(dve.memset(ev_z[:, :, 0:2], 0.0))
                dve.wait_ge(self.v_copied, 1)
                gelu_in(gm_v[:], gm_t[:], self.v_tanh_in)
                dve.wait_ge(self.u_copied, 1)
                gelu_in(gm_u[:], gm_s[:], self.u_tanh_in)
                dve.wait_ge(self.v_tanh, 1)
                own(dve.scalar_tensor_tensor(out=gm_v[:], in0=gm_t[:], scalar=1.0, in1=gm_v[:], op0=ALU.add, op1=ALU.mult))
                own(dve.tensor_tensor(gm_t[:], gm_v[:], gm_v[:], ALU.mult))
                n = T * GM_HEADS
                own(dve.tensor_reduce(ms[:, 0:n], gm_t[:].rearrange("p t (h d) -> p (t h) d", d=GM_HD), AX.X, ALU.add))
                own(dve.tensor_scalar(ms[:, 0:n], ms[:, 0:n], 0.25 / GM_HD, None, ALU.mult))
                rsqrt_ms(dve, own, n)
                own(dve.tensor_scalar(rs[:, 0:n], rs[:, 0:n], 0.5, None, ALU.mult))
                v3 = gm_v[:].rearrange("p t (h d) -> p (t h) d", d=GM_HD)
                own(dve.tensor_tensor(v3, v3, rs[:, 0:n].unsqueeze(2).to_broadcast([P, n, GM_HD]), ALU.mult))
                dve.tensor_tensor(gm_v[:], gm_v[:], g_v[:].unsqueeze(1).to_broadcast([P, T, 512]),
                                  ALU.mult).then_inc(self.vn, 1)
                dve.wait_ge(self.u_tanh, 1)
                own(dve.scalar_tensor_tensor(out=gm_u[:], in0=gm_s[:], scalar=1.0, in1=gm_u[:], op0=ALU.add, op1=ALU.mult))
                dve.wait_ge(self.x_copied, 1)
                own(dve.tensor_tensor(ev_z[:, :, 2:], ps[:, 4:6, :].rearrange("p b (c s) -> p (b c) s", c=2), ev_x[:],
                                      ALU.mult))
                for j in range(3):
                    for c in range(4):
                        w = col("ev_w_conv", 4 * j + c)
                        if j == 0:
                            own(dve.tensor_scalar(ev_y[:, c], ev_z[:, c, 0:S], w, None, ALU.mult))
                        else:
                            own(dve.scalar_tensor_tensor(out=ev_y[:, c], in0=ev_z[:, c, j:j + S], scalar=w,
                                                         in1=ev_y[:, c], op0=ALU.mult, op1=ALU.add))
                dve.wait_ge(weights_used, self.first + 5)
                dve.tensor_tensor(mixT[:, 0:4, :], ps[:, 0:2, :].rearrange("p b (c s) -> p (b c) s", c=2), ev_y[:],
                                  ALU.mult).then_inc(self.mixT_ready, 1)
                dve.wait_ge(self.mixed, 1)
                bias = col("ev_b_s", 0, GM_HEADS).unsqueeze(2).to_broadcast([P, GM_HEADS, GM_HD])
                for t in range(T):
                    own(dve.tensor_tensor(gm_t[:, t].rearrange("p (h d) -> p h d", d=GM_HD),
                                          ps[:, 2 + t, :].rearrange("p (h d) -> p h d", d=GM_HD), bias, ALU.add))
                dve.scalar_tensor_tensor(out=gm_s[:], in0=gm_t[:], scalar=0.5, in1=gm_u[:], op0=ALU.mult,
                                         op1=ALU.mult).then_inc(self.y_b, 1)
                for i in range(2):
                    dve.wait_ge(weights_used, self.out + i + 1)
                    for t in range(T):
                        o = h[:, t, i * 512:(i + 1) * 512]
                        dve.tensor_tensor(o, o, ps[:, (6, 7, 0, 1)[2 * i + t], :], ALU.add)
                stage_end(dve)

        class OddIn:
            def __init__(self):
                self.first = FIRST["od_in"]
                self.made = sem("od_z_made")
                self.copied = [sem(f"od_z_copied{t}") for t in range(T)]

            def pe(self, pe):
                for i in range(5):
                    n = min(512, ODD_IN - 512 * i)
                    wait_weights(pe, self.first + i)
                    w = cols8(self.first + i, n)
                    if i == 4:
                        for t in range(T):
                            pe.wait_ge(self.copied[t], 1)
                    for t in range(T):
                        for k in range(KC):
                            last = pe.matmul(ps[:, (2 * i + t) % 8, 0:n], hnT[:, k, t * P:(t + 1) * P], w[:, k, :],
                                             start=(k == 0), stop=(k == KC - 1))
                        last.then_inc(self.made if t == 0 else weights_used, 1)
                stage_end(pe)

            def act(self, act):
                for i in range(5):
                    n = min(512, ODD_IN - 512 * i)
                    act.wait_ge(self.made, i + 1)
                    act.copy(od_z[:, 0, 512 * i:512 * i + n], ps[:, (2 * i) % 8, 0:n]).then_inc(self.copied[0], 1)
                stage_end(act)

            def dve(self, dve, own):
                for i in range(5):
                    n = min(512, ODD_IN - 512 * i)
                    dve.wait_ge(weights_used, self.first + i + 1)
                    dve.tensor_copy(od_z[:, 1, 512 * i:512 * i + n], ps[:, (2 * i + 1) % 8, 0:n]).then_inc(self.copied[1], 1)
                stage_end(dve)

            def pool(self, pool):
                freq = (np.float32(ROPE_THETA) ** (-np.arange(0, ROPE, 2, dtype=np.float32) / np.float32(ROPE))
                        ).astype(np.float32)
                for i in range(ROPE // 2):
                    pool.memset(inv_freq[:, i:i + 1], float(freq[i]))
                stage_end(pool)

        class OddUp:
            def __init__(self):
                self.item = FIRST["od_up"]
                self.squares = sem("od_squares")
                self.rstd = sem("od_rstd")
                self.lat = sem("od_lat")
                self.lat_turned = sem("od_lat_turned")
                self.latT = sem("od_latT")
                self.mqk_turned = sem("od_mqk_turned")
                self.mqk_freed = sem("od_mqk_freed")
                self.angles = sem("od_angles")
                self.trig = sem("od_trig")

            def act(self, act):
                for kind, (at, n) in enumerate(((0, Q_LORA), (Q_LORA, KV_LORA), (AT_KPE, ROPE))):
                    for t in range(T):
                        last = act.activation(xn[:, t, at:at + n], od_z[:, t, at:at + n], ACT.Square, scale=float(n) ** -0.5,
                                              accum_out=ms[:, kind * T + t:kind * T + t + 1])
                last.then_inc(self.squares, 1)
                act.wait_ge(self.rstd, 1)
                for t in range(T):
                    act.activation(lat[:, t, 0:Q_LORA], od_z[:, t, 0:Q_LORA], ACT.Copy,
                                   scale=rs[:, t:t + 1]).then_inc(self.lat, 1)
                act.wait_ge(self.lat_turned, 1)
                for c in range(5):
                    gain = col("od_g_qa", c) if c < 3 else col("od_g_kva", c - 3)
                    last = act.activation(latT[:, c, :], ps[:, c // 2, (c % 2) * S:(c % 2 + 1) * S], ACT.Copy, scale=gain)
                last.then_inc(self.latT, 1)
                act.wait_ge(self.mqk_turned, 1)
                act.copy(mqkT[:], ps[:, 3:5, :].rearrange("p b (c s) -> p (b c) s", c=2)).then_inc(self.mqk_freed, 1)
                act.wait_ge(self.angles, 1)
                act.activation(cs[:], cs[:], ACT.Sin).then_inc(self.trig, 1)
                act.wait_ge(weights_used, self.item + 1)
                act.copy(od_q[:].rearrange("p t h d -> p t (h d)").rearrange("p t (a b) -> p (t a) b", a=2),
                         ps[:, 0:4, 0:384])
                act.copy(od_kv[:].rearrange("p t h d -> p t (h d)").rearrange("p t (a b) -> p (t a) b", a=2),
                         ps[:, 4:8, :])
                stage_end(act)

            def dve(self, dve, own):
                own(dve.tensor_copy(posf[:], pos_i[:]))
                for t in range(T):
                    own(dve.tensor_scalar(ang[:, t], inv_freq[:], posf[:, t:t + 1], None, ALU.mult))
                first_part = 6.25
                second_part = np.floor((2 * np.pi - first_part) * 2.0 ** 19) / 2.0 ** 19
                parts = [first_part, second_part, 2 * np.pi - first_part - second_part]
                big = 1.5 * 2.0 ** 23
                for k, quarter in ((0, 0.25), (1, 0.0)):
                    own(dve.tensor_scalar(turns[:], ang[:], float(1 / (2 * np.pi)), quarter, ALU.mult, ALU.add))
                    own(dve.tensor_scalar(turns[:], turns[:], big, None, ALU.add))
                    own(dve.tensor_scalar(turns[:], turns[:], big, None, ALU.subtract))
                    own(dve.scalar_tensor_tensor(out=cs[:, k], in0=turns[:], scalar=-float(parts[0]), in1=ang[:],
                                                 op0=ALU.mult, op1=ALU.add))
                    for part in parts[1:]:
                        own(dve.scalar_tensor_tensor(out=cs[:, k], in0=turns[:], scalar=-float(part), in1=cs[:, k],
                                                     op0=ALU.mult, op1=ALU.add))
                    if quarter:
                        own(dve.tensor_scalar(cs[:, k], cs[:, k], float(np.pi / 2), None, ALU.add))
                    last = dve.tensor_scalar(cs[:, k], cs[:, k], 3.1415925, -3.1415925, ALU.min, ALU.max)
                    if k == 0:
                        own(last)
                last.then_inc(self.angles, 1)
                dve.wait_ge(self.squares, 1)
                rsqrt_ms(dve, own, 3 * T, self.rstd)
                dve.wait_ge(self.rstd, 1)
                for t in range(T):
                    dve.tensor_scalar(lat[:, t, Q_LORA:], od_z[:, t, Q_LORA:AT_KPE], rs[:, T + t:T + t + 1], None,
                                      ALU.mult).then_inc(self.lat, 1)
                for t in range(T):
                    kp = od_z[:, t, AT_KPE:AT_KPE + ROPE]
                    own(dve.scalar_tensor_tensor(out=kp, in0=kp, scalar=rs[:, 2 * T + t:2 * T + t + 1], in1=g_k[:, NOPE:],
                                                 op0=ALU.mult, op1=ALU.mult))
                stage_end(dve)

            def pe(self, pe):
                for c in range(4):
                    for t in range(T):
                        at = (c % 2) * S + t * P
                        last = pe.transpose(ps[:, 3 + c // 2, at:at + P], od_z[:, t, AT_MQ + c * P:AT_MQ + (c + 1) * P],
                                            ident[:])
                last.then_inc(self.mqk_turned, 1)
                pe.wait_ge(self.lat, 2 * T)
                for c in range(5):
                    for t in range(T):
                        at = (c % 2) * S + t * P
                        last = pe.transpose(ps[:, c // 2, at:at + P], lat[:, t, c * P:(c + 1) * P], ident[:])
                last.then_inc(self.lat_turned, 1)
                pe.wait_ge(self.latT, 1)
                pe.wait_ge(self.mqk_freed, 1)
                wait_weights(pe, self.item)
                wq = slot(self.item)[:, 0:3 * 768].rearrange("p (k n) -> p k n", k=3)
                wkv = slot(self.item)[:, 3 * 768:3 * 768 + 2 * 1024].rearrange("p (k n) -> p k n", k=2)
                for t in range(T):
                    for half_ in range(2):
                        for k in range(3):
                            pe.matmul(ps[:, 2 * t + half_, 0:384], latT[:, k, t * P:(t + 1) * P],
                                      wq[:, k, half_ * 384:(half_ + 1) * 384], start=(k == 0), stop=(k == 2))
                for t in range(T):
                    for half_ in range(2):
                        for k in range(2):
                            last = pe.matmul(ps[:, 4 + 2 * t + half_, :], latT[:, 3 + k, t * P:(t + 1) * P],
                                             wkv[:, k, half_ * 512:(half_ + 1) * 512], start=(k == 0), stop=(k == 1))
                last.then_inc(weights_used, 1)
                stage_end(pe)

        class OddHeads:

            def __init__(self):
                self.sq_k = sem("od_sq_k")
                self.q_ready, self.k_ready = sem("od_q_ready"), sem("od_k_ready")
                self.turned, self.exps, self.logs = sem("od_heads_turned"), sem("od_gate_exp"), sem("od_gate_log")
                self.gate_abs = sem("od_gate_abs")

            def dve(self, dve, own):
                n = T * HEADS
                q3 = od_q[:].rearrange("p t h d -> p (t h) d")
                kv3 = od_kv[:].rearrange("p t h d -> p (t h) d")
                k3 = od_k[:].rearrange("p t h d -> p (t h) d")
                sq = xn[:].rearrange("p t d -> p (t d)")[:, 0:n * QK].rearrange("p (n d) -> p n d", d=QK)
                own(dve.tensor_tensor(sq, q3, q3, ALU.mult))
                own(dve.tensor_reduce(ms[:, 0:n], sq[:, :, 0:NOPE], AX.X, ALU.add))
                own(dve.tensor_reduce(ms[:, n:2 * n], sq[:, :, NOPE:], AX.X, ALU.add))
                own(dve.tensor_tensor(sq[:, :, 0:NOPE], kv3[:, :, 0:NOPE], kv3[:, :, 0:NOPE], ALU.mult))
                own(dve.tensor_reduce(ms[:, 2 * n:3 * n], sq[:, :, 0:NOPE], AX.X, ALU.add))
                own(dve.tensor_scalar(ms[:, 0:n], ms[:, 0:n], 1.0 / NOPE, None, ALU.mult))
                own(dve.tensor_scalar(ms[:, n:2 * n], ms[:, n:2 * n], 1.0 / ROPE, None, ALU.mult))
                own(dve.tensor_scalar(ms[:, 2 * n:3 * n], ms[:, 2 * n:3 * n], 1.0 / NOPE, None, ALU.mult))
                rsqrt_ms(dve, own, 3 * n)

                def per_head(x, at, width):
                    return rs[:, at:at + n].unsqueeze(2).to_broadcast([P, n, width])

                own(dve.tensor_tensor(q3[:, :, 0:NOPE], q3[:, :, 0:NOPE], per_head(rs, 0, NOPE), ALU.mult))
                own(dve.tensor_tensor(q3[:, :, NOPE:], q3[:, :, NOPE:], per_head(rs, n, ROPE), ALU.mult))
                own(dve.tensor_tensor(q3, q3, g_q[:].unsqueeze(1).to_broadcast([P, n, QK]), ALU.mult))
                own(dve.tensor_tensor(k3[:, :, 0:NOPE], kv3[:, :, 0:NOPE], per_head(rs, 2 * n, NOPE), ALU.mult))
                own(dve.tensor_tensor(k3[:, :, 0:NOPE], k3[:, :, 0:NOPE],
                                      g_k[:, 0:NOPE].unsqueeze(1).to_broadcast([P, n, NOPE]), ALU.mult))
                hr = ROPE // 2
                for t in range(T):
                    r1 = sq[:, 0:HEADS, 0:hr]
                    r2 = sq[:, 0:HEADS, hr:2 * hr]
                    cos = cs[:, 0, t].unsqueeze(1).to_broadcast([P, HEADS, hr])
                    sin = cs[:, 1, t].unsqueeze(1).to_broadcast([P, HEADS, hr])
                    x1, x2 = od_q[:, t, :, NOPE:NOPE + hr], od_q[:, t, :, NOPE + hr:]
                    own(dve.tensor_tensor(r1, x2, sin, ALU.mult))
                    own(dve.tensor_tensor(r2, x1, sin, ALU.mult))
                    own(dve.tensor_tensor(x1, x1, cos, ALU.mult))
                    own(dve.tensor_tensor(x2, x2, cos, ALU.mult))
                    own(dve.tensor_tensor(x1, x1, r1, ALU.subtract))
                    last = dve.tensor_tensor(x2, x2, r2, ALU.add)
                    last.then_inc(self.q_ready, 1)
                for t in range(T):
                    k1, k2 = od_z[:, t, AT_KPE:AT_KPE + hr], od_z[:, t, AT_KPE + hr:AT_KPE + ROPE]
                    r1, r2 = sq[:, HEADS, 0:hr], sq[:, HEADS, hr:2 * hr]
                    cos, sin = cs[:, 0, t], cs[:, 1, t]
                    own(dve.tensor_tensor(r1, k2, sin, ALU.mult))
                    own(dve.tensor_tensor(r2, k1, sin, ALU.mult))
                    own(dve.tensor_tensor(k1, k1, cos, ALU.mult))
                    own(dve.tensor_tensor(k2, k2, cos, ALU.mult))
                    own(dve.tensor_tensor(k1, k1, r1, ALU.subtract))
                    own(dve.tensor_tensor(k2, k2, r2, ALU.add))
                    dve.tensor_copy(od_k[:, t, :, NOPE:],
                                    od_z[:, t, AT_KPE:AT_KPE + ROPE].unsqueeze(1).to_broadcast([P, HEADS, ROPE])
                                    ).then_inc(self.k_ready, 1)
                own(dve.tensor_tensor(gts[:], od_z[:, :, AT_MI:], b_gate[:].unsqueeze(1).to_broadcast([P, T, 2 * MH]),
                                      ALU.add))
                f = gts[:, :, MH:]
                own(dve.tensor_scalar(lf[:, 2], f, -1.0, None, ALU.mult))
                dve.tensor_tensor(lf[:, 0], f, lf[:, 2], ALU.max).then_inc(self.gate_abs, 1)
                dve.wait_ge(self.logs, 1)
                own(dve.tensor_scalar(lf[:, 2], f, 0.0, None, ALU.min))
                own(dve.tensor_tensor(lf[:, 2], lf[:, 2], lf[:, 1], ALU.subtract))
                for b in range(0, 8, 2):
                    dve.wait_ge(self.turned, b + 1)
                    dst = (qT if b < 4 else kT)[0:QK, 2 * (b % 4):2 * (b % 4) + 2, :]
                    dve.tensor_copy(dst, ps[0:QK, b, :].rearrange("p (h s) -> p h s", h=2))
                stage_end(dve)

            def act(self, act):
                act.wait_ge(self.gate_abs, 1)
                act.activation(lf[:, 0], lf[:, 0], ACT.Exp, scale=-1.0).then_inc(self.exps, 1)
                act.wait_ge(self.exps, 1)
                act.activation(lf[:, 1], lf[:, 0], ACT.Ln, bias=1.0).then_inc(self.logs, 1)
                for b in range(1, 8, 2):
                    act.wait_ge(self.turned, b + 1)
                    dst = (qT if b < 4 else kT)[0:QK, 2 * (b % 4):2 * (b % 4) + 2, :]
                    act.copy(dst, ps[0:QK, b, :].rearrange("p (h s) -> p h s", h=2))
                stage_end(act)

            def pe(self, pe):
                for b in range(8):
                    ready, src = (self.q_ready, od_q) if b < 4 else (self.k_ready, od_k)
                    if b % 4 == 0:
                        pe.wait_ge(ready, T)
                    for hd in range(2):
                        for t in range(T):
                            at = hd * S + t * P
                            last = pe.transpose(ps[0:QK, b, at:at + P], src[:, t, 2 * (b % 4) + hd, :], ident[:])
                    last.then_inc(self.turned, 1)
                stage_end(pe)

        class OddAttend:

            def __init__(self):
                self.cum = sem("oa_cum")
                self.diag = sem("oa_diag")
                self.rows = sem("oa_rows")
                self.rows_freed = sem("oa_rows_freed")
                self.scores = sem("oa_scores")
                self.masked = sem("oa_masked")
                self.prob = sem("oa_prob")
                self.turned = sem("oa_turned")
                self.probT = sem("oa_probT")
                self.valued = sem("oa_valued")
                self.nm = sem("oa_nm")
                self.w_mem = sem("oa_w_mem")
                self.mx = sem("oa_mx")
                self.v_aug_ready = sem("oa_v_aug_ready")
                self.y_freed = sem("oa_y_freed")

            N = HEADS + MH

            def pe(self, pe):
                for t in range(T):
                    o = ps[:, 5, t * MH:(t + 1) * MH]
                    if t:
                        pe.matmul(o, ones[:], lf[:, 2, 0], start=True, stop=False)
                    last = pe.matmul(o, upper[:], lf[:, 2, t], start=(t == 0), stop=True)
                last.then_inc(self.cum, 1)
                pe.wait_ge(self.diag, T)
                for t in range(T):
                    last = pe.matmul(ps[:, 3 + t, :], ones[:], diag_b[:, t], start=True, stop=True)
                last.then_inc(self.rows, 1)

                def scores(hd):
                    if hd >= 3:
                        pe.wait_ge(self.masked, hd - 2)
                    if hd < HEADS:
                        q, k = qT[0:QK, hd, :], kT[0:QK, hd, :]
                    else:
                        m = hd - HEADS
                        rows = slice((m % 2) * MQK, (m % 2 + 1) * MQK)
                        q, k = mqkT[rows, m // 2, :], mqkT[rows, 2 + m // 2, :]
                    pe.matmul(ps[:, hd % 3, 0:P], q[:, 0:P], k[:, 0:P], start=True, stop=True)
                    pe.matmul(ps[:, hd % 3, P:3 * P], q[:, P:S], k, start=True, stop=True).then_inc(self.scores, 1)

                def turn(hd):
                    if hd == 0:
                        pe.wait_ge(self.rows_freed, 1)
                    if hd < HEADS:
                        pe.wait_ge(self.prob, hd + 1)
                    else:
                        pe.wait_ge(self.masked, hd + 1)
                    if hd >= 2:
                        pe.wait_ge(self.probT, hd - 1)
                    for j in range(3):
                        last = pe.transpose(ps[:, 3 + hd % 2, j * P:(j + 1) * P], prob[:, hd % 2, j * P:(j + 1) * P], ident[:])
                    last.then_inc(self.turned, 1)

                def values(hd):
                    pe.wait_ge(self.probT, hd + 1)
                    if hd == HEADS:
                        pe.wait_ge(self.v_aug_ready, 1)
                        pe.wait_ge(self.y_freed, T)
                    elif hd > HEADS + 1:
                        pe.wait_ge(self.y_freed, T + hd - HEADS - 1)
                    for t in range(T):
                        for j in range(t + 1):
                            w = probT[:, hd % 2, (t + j) * P:(t + j + 1) * P]
                            if hd < HEADS:
                                o, v = ps[:, 6 + t, hd * VD:(hd + 1) * VD], od_kv[:, j, hd, NOPE:]
                            else:
                                m = hd - HEADS
                                o = ps[:, 6 + m % 2, t * (MV + 1):(t + 1) * (MV + 1)]
                                v = v_aug[:, j, m, :]
                            last = pe.matmul(o, w, v, start=(j == 0), stop=(j == t))
                    last.then_inc(self.valued, 1)

                for step in range(self.N + 2):
                    if step < self.N:
                        scores(step)
                    if 1 <= step <= self.N:
                        turn(step - 1)
                    if step >= 2:
                        values(step - 2)
                stage_end(pe)

            def act(self, act):
                def copy(hd):
                    act.wait_ge(self.turned, hd + 1)
                    if hd >= 2:
                        act.wait_ge(self.valued, hd - 1)
                    act.copy(probT[:, hd % 2], ps[:, 3 + hd % 2, 0:3 * P]).then_inc(self.probT, 1)

                act.wait_ge(self.mx, 1)
                for m in range(MH):
                    for t in range(T):
                        b = b_masked[:, m, 0:P] if t == 0 else b_masked[:, m, P:3 * P]
                        act.activation(b, b, ACT.Exp, bias=nmax[:, HEADS + m, t:t + 1])
                act.activation(emt[:], emt[:], ACT.Exp, scale=-1.0).then_inc(self.w_mem, 1)
                for hd in range(HEADS):
                    act.wait_ge(self.nm, hd + 1)
                    if hd >= 2:
                        act.wait_ge(self.turned, hd - 1)
                    for t in range(T):
                        cut = slice(0, P) if t == 0 else slice(P, 3 * P)
                        last = act.activation(prob[:, hd % 2, cut], sm[:, hd % 2, cut], ACT.Exp,
                                              bias=nmax[:, hd, t:t + 1], accum_out=rsum[:, t, hd:hd + 1])
                    last.then_inc(self.prob, 1)
                    copy(hd)
                for hd in range(HEADS, self.N):
                    copy(hd)
                stage_end(act)

            def dve(self, dve, own):
                dve.wait_ge(self.cum, 1)
                own(dve.tensor_copy(acum[:], ps[:, 5, 0:T * MH].rearrange("p (t h) -> p t h", t=T)))
                own(dve.tensor_tensor(bcol[:], gts[:, :, 0:MH], acum[:], ALU.subtract))

                def masked(hd):
                    dve.wait_ge(self.scores, hd + 1)
                    if hd < HEADS:
                        if hd >= 2:
                            dve.wait_ge(self.prob, hd - 1)
                        ins = dve.scalar_tensor_tensor(out=sm[:, hd % 2], in0=ps[:, hd % 3, 0:3 * P], scalar=float(QK) ** -0.5,
                                                       in1=cmask[:], op0=ALU.mult, op1=ALU.add)
                        ins.then_inc(self.masked, 1)
                        dve.wait_ge(self.masked, hd + 1)
                        dve.tensor_reduce(nmax[:, hd, 0:1], sm[:, hd % 2, 0:P], AX.X, ALU.max, negate=True)
                        dve.tensor_reduce(nmax[:, hd, 1:2], sm[:, hd % 2, P:3 * P], AX.X, ALU.max,
                                          negate=True).then_inc(self.nm, 1)
                    else:
                        m = hd - HEADS
                        if m == 0:
                            dve.wait_ge(self.w_mem, 1)
                        dve.wait_ge(self.turned, hd - 1)
                        ins = dve.scalar_tensor_tensor(out=prob[:, hd % 2], in0=ps[:, hd % 3, 0:3 * P],
                                                       scalar=float(MQK) ** -0.5, in1=b_masked[:, m, :],
                                                       op0=ALU.mult, op1=ALU.mult)
                        ins.then_inc(self.masked, 1)

                for t in range(T):
                    dve.tensor_tensor(diag_b[:, t], ident[:].unsqueeze(1).to_broadcast([P, MH, P]),
                                      bcol[:, t].unsqueeze(2).to_broadcast([P, MH, P]), ALU.mult).then_inc(self.diag, 1)
                dve.wait_ge(self.rows, 1)
                tri = cmask[:, 0:P].unsqueeze(1).to_broadcast([P, MH, P])
                row = [ps[:, 3 + t, :].rearrange("p (h n) -> p h n", h=MH) for t in range(T)]
                own(dve.tensor_tensor(b_masked[:, :, 0:P], row[0], tri, ALU.add))
                own(dve.tensor_copy(b_masked[:, :, P:2 * P], row[0]))
                dve.tensor_tensor(b_masked[:, :, 2 * P:3 * P], row[1], tri, ALU.add).then_inc(self.rows_freed, 1)
                dve.wait_ge(self.rows_freed, 1)
                top = nmax[:, HEADS:, :].rearrange("p h t -> p t h")
                own(dve.tensor_reduce(nmax[:, HEADS:, 0:1], b_masked[:, :, 0:P], AX.X, ALU.max))
                own(dve.tensor_reduce(nmax[:, HEADS:, 1:2], b_masked[:, :, P:3 * P], AX.X, ALU.max))
                own(dve.tensor_scalar(nmax[:, HEADS:, :], nmax[:, HEADS:, :], 0.0, None, ALU.max))
                own(dve.tensor_tensor(emt[:], acum[:], top, ALU.add))
                dve.tensor_scalar(nmax[:, HEADS:, :], nmax[:, HEADS:, :], -1.0, None, ALU.mult).then_inc(self.mx, 1)
                own(dve.memset(v_aug[:, :, :, MV:], 1.0))
                dve.tensor_copy(v_aug[:, :, :, 0:MV], od_z[:, :, AT_MV:AT_MO].rearrange("p t (h d) -> p t h d", h=MH)
                                ).then_inc(self.v_aug_ready, 1)
                for hd in range(self.N):
                    masked(hd)
                    if hd == HEADS + 1:
                        dve.wait_ge(self.valued, HEADS)
                        own(dve.reciprocal(rsum[:], rsum[:]))
                        for t in range(T):
                            dve.tensor_tensor(mix[:, t, 0:HEADS * VD].rearrange("p (h d) -> p h d", h=HEADS),
                                              ps[:, 6 + t, :].rearrange("p (h d) -> p h d", h=HEADS),
                                              rsum[:, t].unsqueeze(2).to_broadcast([P, HEADS, VD]),
                                              ALU.mult).then_inc(self.y_freed, 1)
                for m in range(MH):
                    dve.wait_ge(self.valued, HEADS + m + 1)
                    dve.wait_ge(self.y_freed, T + m)
                    num = ps[:, 6 + m % 2, 0:T * (MV + 1)].rearrange("p (t d) -> p t d", t=T)
                    own(dve.tensor_copy(den[:, 0], num[:, :, MV]))
                    own(dve.tensor_scalar(den[:, 1], den[:, 0], -1.0, None, ALU.mult))
                    own(dve.tensor_tensor(den[:, 0], den[:, 0], den[:, 1], ALU.max))
                    own(dve.tensor_tensor(den[:, 0], den[:, 0], emt[:, :, m], ALU.max))
                    own(dve.reciprocal(den[:, 0], den[:, 0]))
                    dve.tensor_tensor(y_d[:, :, m, :], num[:, :, 0:MV], den[:, 0].unsqueeze(2).to_broadcast([P, T, MV]),
                                      ALU.mult).then_inc(self.y_freed, 1)
                stage_end(dve)

        class OddOut:
            def __init__(self):
                self.out = FIRST["od_out"]
                self.tanh, self.y, self.turned, self.mixT = (sem("oo_" + n) for n in ("tanh", "y", "turned", "mixT"))
                self.mixed = sem("oo_mixed")

            def act(self, act):
                mo = od_z[:, :, AT_MO:AT_MI]
                act.activation(od_z[:, :, AT_MV:AT_MO], mo, ACT.Tanh, scale=0.5).then_inc(self.tanh, 1)
                for b in (1, 3):
                    act.wait_ge(self.turned, b + 1)
                    act.copy(mixT[:, 2 * b:2 * b + 2, :], ps[:, b, :].rearrange("p (c s) -> p c s", c=2)
                             ).then_inc(self.mixT, 1)
                stage_end(act)

            def dve(self, dve, own):
                n = T * MH
                sq = od_kv[:].rearrange("p t h d -> p t (h d)")[:, :, 0:MH * MV].rearrange("p t (h d) -> p t h d", h=MH)
                own(dve.tensor_tensor(sq, y_d, y_d, ALU.mult))
                own(dve.tensor_reduce(ms[:, 0:n].rearrange("p (t h) -> p t h", t=T), sq, AX.X, ALU.add))
                own(dve.tensor_scalar(ms[:, 0:n], ms[:, 0:n], 1.0 / MV, None, ALU.mult))
                rsqrt_ms(dve, own, n)
                own(dve.tensor_scalar(rs[:, 0:n], rs[:, 0:n], 0.5, None, ALU.mult))
                for t in range(T):
                    own(dve.tensor_tensor(y_d[:, t], y_d[:, t],
                                          rs[:, t * MH:(t + 1) * MH].unsqueeze(2).to_broadcast([P, MH, MV]), ALU.mult))
                flat = mix[:, :, HEADS * VD:]
                own(dve.tensor_tensor(flat, flat, g_mh[:].unsqueeze(1).to_broadcast([P, T, MH * MV]), ALU.mult))
                dve.wait_ge(self.tanh, 1)
                dve.scalar_tensor_tensor(out=flat, in0=od_z[:, :, AT_MV:AT_MO], scalar=1.0, in1=flat, op0=ALU.add,
                                         op1=ALU.mult).then_inc(self.y, 1)
                for b in (0, 2):
                    dve.wait_ge(self.turned, b + 1)
                    dve.tensor_copy(mixT[:, 2 * b:2 * b + 2, :], ps[:, b, :].rearrange("p (c s) -> p c s", c=2)
                                    ).then_inc(self.mixT, 1)
                for i in range(2):
                    dve.wait_ge(weights_used, self.out + i + 1)
                    for t in range(T):
                        o = h[:, t, i * 512:(i + 1) * 512]
                        dve.tensor_tensor(o, o, ps[:, 4 + 2 * i + t, :], ALU.add)
                stage_end(dve)

            def pe(self, pe):
                for b in range(4):
                    if b == 2:
                        pe.wait_ge(self.y, 1)
                    for c in (2 * b, 2 * b + 1):
                        for t in range(T):
                            at = (c % 2) * S + t * P
                            last = pe.transpose(ps[:, b, at:at + P], mix[:, t, c * P:(c + 1) * P], ident[:])
                    last.then_inc(self.turned, 1)
                pe.wait_ge(self.mixT, 4)
                for i in range(2):
                    wait_weights(pe, self.out + i)
                    w = cols8(self.out + i)
                    for t in range(T):
                        for k in range(KC):
                            last = pe.matmul(ps[:, 4 + 2 * i + t, :], mixT[:, k, t * P:(t + 1) * P], w[:, k, :],
                                             start=(k == 0), stop=(k == KC - 1))
                    last.then_inc(weights_used, 1)
                stage_end(pe)

        ADA_ITEMS = 6 * D // BLK
        ADA_PER_BLOCK = 3
        ada_steps = sem("ada_steps")

        def ada_loads(pool):
            w = a["ada_w_2"][0].rearrange("(k p) n -> p k n", p=P)
            for s in range(2):
                pool.dma_start(ada_w[:, s], w[:, :, s * BLK:(s + 1) * BLK]).then_inc(ada_landed[s], 16)
            with pool.Fori(1, ADA_ITEMS // 2) as it:
                for s in range(2):
                    pool.wait_ge(ada_used, 2 * it + s - 1)
                    pool.dma_start(ada_w[:, s], w[:, :, bass.ds((2 * it + s) * BLK, BLK)]).then_inc(ada_landed[s], 16)
            stage_end(pool)

        def ada_products(dve, block, it):
            for q in range(ADA_PER_BLOCK):
                i = ADA_PER_BLOCK * block + q
                per_loop = 4 * ADA_PER_BLOCK
                dve.wait_ge(ada_landed[i % 2], 16 * (i // 2 + 1) + 8 * per_loop * it)
                acc = ada_acc[:, bass.ds((per_loop * it + i) * BLK, BLK)]
                for k in range(KC):
                    w, c = ada_w[:, i % 2, k], c_act[:, k:k + 1]
                    if k == 0:
                        ins = dve.tensor_scalar(acc, w, c, None, ALU.mult)
                    else:
                        dve.wait_ge(ada_steps, (KC - 1) * i + k + (KC - 1) * per_loop * it)
                        ins = dve.scalar_tensor_tensor(out=acc, in0=w, scalar=c, in1=acc, op0=ALU.mult, op1=ALU.add)
                    ins.then_inc(ada_steps if k < KC - 1 else ada_used, 1)

        class ModStage:
            COLS, ROWS = (0, 1, 3, 4), (2, 5)

            def __init__(self):
                self.summed = sem("mod_summed")
                self.b_landed = sem("mod_b_landed")

            def load(self, act):
                for i, v in enumerate(self.ROWS):
                    act.dma_start(g_bc[:, i], a["ada_b_2"][0, v * D:(v + 1) * D].partition_broadcast(P)
                                  ).then_inc(self.b_landed, 16)

            def pe(self, pe):
                for i, v in enumerate(self.COLS):
                    for c in range(KC):
                        pe.matmul(ps[:, 0, i * KC + c:i * KC + c + 1], ada_acc[:, v * D + c * P:v * D + (c + 1) * P],
                                  ones[:, 0:1], start=True, stop=True)
                for i, v in enumerate(self.ROWS):
                    for j in range(2):
                        last = pe.matmul(ps[:, 1 + 2 * i + j, :], ones[:], ada_acc[:, v * D + j * 512:v * D + (j + 1) * 512],
                                         start=True, stop=True)
                last.then_inc(self.summed, 1)
                stage_end(pe)

            def dve(self, dve, own):
                dve.wait_ge(self.summed, 1)
                for i, v in enumerate(self.COLS):
                    own(dve.tensor_tensor(mod_cols[:, i], ps[:, 0, i * KC:(i + 1) * KC], col("ada_b_2", v * KC, KC), ALU.add))
                for i, name in ((1, "norm_mix_g_2"), (3, "norm_ffn_g_2")):
                    dve.scalar_tensor_tensor(out=mod_cols[:, i], in0=mod_cols[:, i], scalar=1.0, in1=col(name, 0, KC),
                                             op0=ALU.add, op1=ALU.mult)
                dve.wait_ge(self.b_landed, 32)
                for i in range(2):
                    dve.tensor_tensor(g_bc[:, i].rearrange("p (j n) -> p j n", j=2), ps[:, 1 + 2 * i:3 + 2 * i, :],
                                      g_bc[:, i].rearrange("p (j n) -> p j n", j=2), ALU.add)
                stage_end(dve)

        class ConformerStage:
            def __init__(self):
                self.first, self.out = FIRST["conv_in"], FIRST["conv_out"]
                self.made = sem("cf_made")
                self.cols = sem("cf_cols")
                self.tanh = sem("cf_tanh")
                self.u = sem("cf_u")
                self.conv = sem("cf_conv")
                self.mean = sem("cf_mean")
                self.centred = sem("cf_centred")
                self.squares = sem("cf_squares")
                self.var = sem("cf_var")
                self.normed = sem("cf_normed")
                self.tanh2 = sem("cf_tanh2")
                self.y = sem("cf_y")
                self.taps = sem("cf_taps")
                self.y_view = xn[:].rearrange("p t d -> p (t d)").rearrange("p (c s) -> p c s", c=KC)

            def pe(self, pe):
                for i in range(4):
                    wait_weights(pe, self.first + i)
                    w = slot(self.first + i)[:, 0:AT_DOWN].rearrange("p (k two n) -> p k two n", k=KC, two=2)
                    for j in range(2):
                        for g in range(2):
                            for k in range(KC):
                                last = pe.matmul(ps[:, 2 * i + j, g * S:(g + 1) * S], w[:, k, g, j * P:(j + 1) * P], hnT[:, k, :],
                                                 start=(k == 0), stop=(k == KC - 1))
                        last.then_inc(self.made if j == 0 else weights_used, 1)
                y = self.y_view
                pe.wait_ge(self.conv, KC)
                for c in range(KC):
                    last = pe.matmul(ps[:, 0, 0:S], mean_w[:], y[:, c], start=(c == 0), stop=(c == KC - 1))
                last.then_inc(self.mean, 1)
                pe.wait_ge(self.squares, 1)
                for c in range(KC):
                    last = pe.matmul(ps[:, 1, 0:S], mean_w[:], mixT[:, c], start=(c == 0), stop=(c == KC - 1))
                last.then_inc(self.var, 1)
                pe.wait_ge(self.y, KC)
                for i in range(2):
                    wait_weights(pe, self.out + i)
                    w = cols8(self.out + i)
                    for t in range(T):
                        for k in range(KC):
                            last = pe.matmul(ps[:, 2 + 2 * i + t, :], mixT[:, k, t * P:(t + 1) * P], w[:, k, :],
                                             start=(k == 0), stop=(k == KC - 1))
                    last.then_inc(weights_used, 1)
                stage_end(pe)

            def act(self, act):
                act.wait_ge(self.cols, 1)
                for c in range(KC):
                    if c % 2 == 0:
                        act.wait_ge(self.made, c // 2 + 1)
                    else:
                        act.wait_ge(weights_used, self.first + c // 2 + 1)
                    if c >= 2:
                        act.wait_ge(self.u, c - 1)
                    act.activation(cf_th[:, c % 2], ps[:, c, S:2 * S], ACT.Tanh, bias=half[:, c:c + 1],
                                   scale=0.5).then_inc(self.tanh, 1)
                act.wait_ge(self.centred, 1)
                act.activation(mixT[:], self.y_view, ACT.Square).then_inc(self.squares, 1)
                act.wait_ge(self.normed, 1)
                for c in range(KC):
                    act.activation(hnT[:, c], self.y_view[:, c], ACT.Tanh, bias=half[:, 2 * KC + c:2 * KC + c + 1],
                                   scale=half[:, KC + c:KC + c + 1]).then_inc(self.tanh2, 1)
                stage_end(act)

            def dve(self, dve, own):
                for i, (name, at) in enumerate((("conv_b_in_2", KC), ("conv_ln_g_2", 0), ("conv_ln_b_2", 0))):
                    last = dve.tensor_scalar(half[:, i * KC:(i + 1) * KC], col(name, at, KC), 0.5, None, ALU.mult)
                last.then_inc(self.cols, 1)
                own(dve.memset(u_pad[:, :, 0:TAPS - 1], 0.0))
                y = self.y_view
                for i in range(KC // 2):
                    for c in (2 * i, 2 * i + 1):
                        dve.wait_ge(self.tanh, c + 1)
                        own(dve.tensor_scalar(cf_a[:, c % 2], ps[:, c, 0:S], col("conv_b_in_2", c), 0.5, ALU.add, ALU.mult))
                        dve.scalar_tensor_tensor(out=u_pad[:, c, TAPS - 1:], in0=cf_th[:, c % 2], scalar=1.0, in1=cf_a[:, c % 2],
                                                 op0=ALU.add, op1=ALU.mult).then_inc(self.u, 1)
                    dve.wait_ge(self.u, 2 * i + 2)
                    for j in range(TAPS):
                        for c in (2 * i, 2 * i + 1):
                            w, src = w_dw[:, c, j:j + 1], u_pad[:, c, j:j + S]
                            if j == 0:
                                ins = dve.tensor_scalar(y[:, c], src, w, col("conv_b_dw_2", c), ALU.mult, ALU.add)
                            else:
                                dve.wait_ge(self.taps, 2 * (i * (TAPS - 1) + j - 1) + c % 2 + 1)
                                ins = dve.scalar_tensor_tensor(out=y[:, c], in0=src, scalar=w, in1=y[:, c], op0=ALU.mult,
                                                               op1=ALU.add)
                            if j < TAPS - 1:
                                ins.then_inc(self.taps, 1)
                            else:
                                ins.then_inc(self.conv, 1)
                dve.wait_ge(self.conv, KC)
                dve.wait_ge(self.mean, 1)
                dve.tensor_tensor(y, y, ps[:, 0, 0:S].unsqueeze(1).to_broadcast([P, KC, S]), ALU.subtract
                                  ).then_inc(self.centred, 1)
                dve.wait_ge(self.var, 1)
                own(dve.tensor_copy(cf_r[:, 0], ps[:, 1, 0:S]))
                rsqrt(dve, own, cf_r[:, 0], cf_r[:, 1], cf_r[:, 2], cf_r[:, 3])
                dve.wait_ge(self.centred, 1)
                dve.tensor_tensor(y, y, cf_r[:, 1].unsqueeze(1).to_broadcast([P, KC, S]), ALU.mult).then_inc(self.normed, 1)
                dve.wait_ge(self.normed, 1)
                for c in range(KC):
                    dve.wait_ge(self.tanh2, c + 1)
                    own(dve.tensor_scalar(y[:, c], y[:, c], half[:, KC + c:KC + c + 1], half[:, 2 * KC + c:2 * KC + c + 1],
                                          ALU.mult, ALU.add))
                    dve.scalar_tensor_tensor(out=mixT[:, c], in0=hnT[:, c], scalar=1.0, in1=y[:, c], op0=ALU.add,
                                             op1=ALU.mult).then_inc(self.y, 1)
                for i in range(2):
                    dve.wait_ge(weights_used, self.out + i + 1)
                    for t in range(T):
                        o, g = h[:, t, i * 512:(i + 1) * 512], g_bc[:, 0, i * 512:(i + 1) * 512]
                        tmp = xn[:, t, i * 512:(i + 1) * 512]
                        own(dve.tensor_tensor(tmp, ps[:, 2 + 2 * i + t, :], g, ALU.mult))
                        dve.tensor_tensor(o, o, tmp, ALU.add)
                stage_end(dve)

        class RouteStage:
            def __init__(self):
                self.made, self.gmax, self.gexp, self.diff, self.dexp = (sem("rt_" + n) for n in
                                                                        ("made", "gmax", "gexp", "diff", "dexp"))
                self.turned, self.chosen, self.counted = sem("rt_turned"), sem("rt_chosen"), sem("rt_counted")

            def pe(self, pe):
                for t in range(T):
                    for k in range(KC):
                        last = pe.matmul(ps[:, t, 0:GROUPS + EXPERTS], hnT[:, k, t * P:(t + 1) * P], w_route[:, k, :],
                                         start=(k == 0), stop=(k == KC - 1))
                last.then_inc(self.made, 1)
                for b in range(4):
                    for c in range(4):
                        k = (b % 2) * 4 + c
                        last = pe.transpose(ps[:, 4 + b, c * P:(c + 1) * P], hnT[:, k, (b // 2) * P:(b // 2 + 1) * P], ident[:])
                    last.then_inc(self.turned, 1)
                pe.wait_ge(self.chosen, 1)
                pe.matmul(ps[:, 2, 0:EXPERTS], upper[:], rt[:, 8, 0], start=True, stop=True)
                pe.matmul(ps[:, 2, EXPERTS:2 * EXPERTS], ones[:], rt[:, 8, 0], start=True, stop=False)
                pe.matmul(ps[:, 2, EXPERTS:2 * EXPERTS], upper[:], rt[:, 8, 1], start=False, stop=True)
                pe.matmul(ps[:, 3, 0:EXPERTS], ones[:], rt[:, 8, 0], start=True, stop=False)
                pe.matmul(ps[:, 3, 0:EXPERTS], ones[:], rt[:, 8, 1], start=False, stop=True).then_inc(self.counted, 1)
                stage_end(pe)

            def act(self, act):
                for b in range(4):
                    act.wait_ge(self.turned, b + 1)
                    act.copy(xn[:, b // 2, (b % 2) * 512:(b % 2 + 1) * 512], ps[:, 4 + b, :])
                act.wait_ge(self.gmax, 1)
                for t in range(T):
                    last = act.activation(rt[:, 1, t, 0:GROUPS], rt[:, 0, t, 0:GROUPS], ACT.Exp, bias=rts[:, 0, t:t + 1],
                                          accum_out=rts[:, 1, t:t + 1])
                last.then_inc(self.gexp, 1)
                act.wait_ge(self.diff, 1)
                act.activation(rts[:, 5], rts[:, 4], ACT.Exp).then_inc(self.dexp, 1)
                stage_end(act)

            def dve(self, dve, own):
                def wide(x, n=EXPERTS):
                    return x.unsqueeze(2).to_broadcast([P, T, n])

                def first_max(hot, x, top, key, key_top, n):
                    own(dve.tensor_tensor(key, x, wide(top, n), ALU.is_equal))
                    own(dve.tensor_tensor(key, key, rev[:, 0:n].unsqueeze(1).to_broadcast([P, T, n]), ALU.mult))
                    own(dve.tensor_reduce(key_top, key, AX.X, ALU.max))
                    own(dve.tensor_tensor(hot, key, wide(key_top, n), ALU.is_equal))

                grp, eg, key, hot1, hot2 = (rt[:, i] for i in (0, 2, 3, 4, 5))
                exp_l = rt[:, 6]
                g4 = grp[:, :, 0:GROUPS]
                dve.wait_ge(self.made, 1)
                own(dve.tensor_tensor(g4, ps[:, 0:T, 0:GROUPS], b_route[:, 0:GROUPS].unsqueeze(1).to_broadcast([P, T, GROUPS]),
                                      ALU.add))
                own(dve.tensor_tensor(exp_l, ps[:, 0:T, GROUPS:GROUPS + EXPERTS],
                                      b_route[:, GROUPS:].unsqueeze(1).to_broadcast([P, T, EXPERTS]), ALU.add))
                own(dve.tensor_reduce(rts[:, 2], g4, AX.X, ALU.max))
                dve.tensor_scalar(rts[:, 0], rts[:, 2], -1.0, None, ALU.mult).then_inc(self.gmax, 1)
                first_max(eg[:, :, 0:GROUPS], g4, rts[:, 2], key[:, :, 0:GROUPS], rts[:, 3], GROUPS)
                own(dve.tensor_scalar(eg[:, :, 0:GROUPS], eg[:, :, 0:GROUPS], -1.0, -NEG, ALU.add, ALU.mult))
                for t in range(T):
                    e3 = exp_l[:, t].rearrange("p (g e) -> p g e", g=GROUPS)
                    own(dve.tensor_tensor(e3, e3, eg[:, t, 0:GROUPS].unsqueeze(2).to_broadcast([P, GROUPS, PER_GROUP]), ALU.add))
                own(dve.tensor_reduce(rts[:, 6], exp_l, AX.X, ALU.max))
                first_max(hot1, exp_l, rts[:, 6], key, rts[:, 3], EXPERTS)
                own(dve.scalar_tensor_tensor(out=rt[:, 7], in0=hot1, scalar=3 * NEG, in1=exp_l, op0=ALU.mult, op1=ALU.add))
                own(dve.tensor_reduce(rts[:, 7], rt[:, 7], AX.X, ALU.max))
                first_max(hot2, rt[:, 7], rts[:, 7], key, rts[:, 3], EXPERTS)
                dve.tensor_tensor(rts[:, 4], rts[:, 7], rts[:, 6], ALU.subtract).then_inc(self.diff, 1)
                dve.tensor_tensor(rt[:, 8], hot1, hot2, ALU.add).then_inc(self.chosen, 1)
                dve.wait_ge(self.gexp, 1)
                own(dve.reciprocal(rts[:, 8], rts[:, 1]))
                dve.wait_ge(self.dexp, 1)
                own(dve.tensor_scalar(rts[:, 9], rts[:, 5], 1.0, None, ALU.add))
                own(dve.reciprocal(rts[:, 9], rts[:, 9]))
                own(dve.tensor_tensor(rts[:, 10], rts[:, 5], rts[:, 9], ALU.mult))
                for i in (9, 10):
                    own(dve.scalar_tensor_tensor(out=rts[:, i], in0=rts[:, i], scalar=0.5, in1=rts[:, 8], op0=ALU.mult,
                                                 op1=ALU.mult))
                own(dve.tensor_tensor(hot1, hot1, wide(rts[:, 9]), ALU.mult))
                own(dve.tensor_tensor(hot2, hot2, wide(rts[:, 10]), ALU.mult))
                own(dve.tensor_tensor(gate_half[:], hot1, hot2, ALU.add))
                dve.wait_ge(self.counted, 1)
                own(dve.tensor_tensor(place[:], ps[:, 2, 0:T * EXPERTS].rearrange("p (t e) -> p t e", t=T), rt[:, 8], ALU.mult))
                own(dve.tensor_scalar(place[:], place[:], -1.0, None, ALU.add))
                own(dve.tensor_reduce(rts[:, 0, 0:1], ps[:, 3, 0:EXPERTS], AX.X, ALU.max))
                own(dve.tensor_scalar(rts[:, 1, 0:1], rts[:, 0, 0:1], PLACES + 0.5, None, ALU.is_ge))
                own(dve.tensor_copy(crowded[:], rts[:, 1, 0:1]))
                stage_end(dve)

        class ExpertsStage:
            def __init__(self):
                self.first = FIRST["moe"]
                self.dense = GatedStage("moe", MOE_BLOCKS, True)
                self.sel = sem("ge_sel_ready")
                self.gathered = sem("ge_gathered")
                self.xT = sem("ge_xT_ready")
                self.gate_up = sem("ge_gate_up")
                self.tanh = sem("ge_tanh_ready")
                self.half = sem("ge_half")
                self.hid = sem("ge_hid_ready")
                self.turned = sem("ge_turned_made")
                self.copied = sem("ge_turned_copied")
                self.y = sem("ge_y_ready")
                self.summed = sem("ge_summed")

            def either(self, eng, gathered, dense):
                many = eng.value_load(crowded[0:1, 0:1], min_val=0, max_val=1)
                with eng.If(many == 0):
                    gathered()
                with eng.Else():
                    dense()

            def experts(self, step):
                def run(eng):
                    step(0, None)
                    step(1, None)
                    with eng.Fori(0, EXPERTS // 2 - 2) as it:
                        step(2, it)
                        step(3, it)
                    step(EXPERTS - 2, None)
                    step(EXPERTS - 1, None)
                return run

            @staticmethod
            def at(value, it, per_expert=1):
                return value if it is None else value + 2 * per_expert * it

            def pe(self, pe):
                at = self.at

                def gather(e, it):
                    pe.wait_ge(self.sel, at(e + 1, it))
                    for k in range(KC):
                        for t in range(T):
                            last = pe.matmul(ps[:, 0, k * PLACES:(k + 1) * PLACES], xn[:, t, k * P:(k + 1) * P], ge_sel[:, t],
                                             start=(t == 0), stop=(t == T - 1))
                    last.then_inc(self.gathered, 1)

                def gate_up(e, it):
                    item = self.first + HALVES * e
                    for f in range(HALVES):
                        wait_weights(pe, item + f, it)
                    pe.wait_ge(self.xT, at(e + 1, it))
                    for k in range(KC):
                        for f in range(HALVES):
                            last = pe.matmul(ps[f * PLACES:(f + 1) * PLACES, 1, :], ge_xT[:, k], cols8(item + f)[:, k, :],
                                             start=(k == 0), stop=(k == KC - 1))
                    last.then_inc(self.gate_up, 1)

                def turn(e, it):
                    for t in range(T):
                        pe.transpose(ps[:, 2, (2 + t) * P:(3 + t) * P], ge_share[:, e % 2, t], ident[:])
                    pe.wait_ge(self.hid, at(e + 1, it))
                    for c in range(2):
                        last = pe.transpose(ps[:, 2, c * P:(c + 1) * P], ge_hid[:, c * P:(c + 1) * P], ident[:])
                    last.then_inc(self.turned, 1)

                def down(e, it):
                    pe.wait_ge(self.copied, at(e + 1, it))
                    for f in range(HALVES):
                        w = slot(self.first + HALVES * e + f)[:, AT_DOWN:SLOT].rearrange("p (c d) -> p c d", c=2)
                        for c in range(2):
                            for n in range(2):
                                last = pe.matmul(ps[n * PLACES:(n + 1) * PLACES, 3, :], ge_turned[:, c, f * PLACES:(f + 1) * PLACES],
                                                 w[:, c, n * 512:(n + 1) * 512],
                                                 start=(f == 0 and c == 0), stop=(f == HALVES - 1 and c == 1))
                        last.then_inc(weights_used, 1)

                def give_back(e, it):
                    pe.wait_ge(self.y, at(e + 1, it))
                    for t in range(T):
                        for n in range(2):
                            cut = slice(n * PLACES, (n + 1) * PLACES)
                            last = pe.matmul(ps[:, 4 + 2 * t + n, :], ge_turned[cut, 2 + t], ge_y[cut, :],
                                             start=(e == 0), stop=(e == EXPERTS - 1))
                    return last

                def step(e, it):
                    gate_up(e, it)
                    if e > 0:
                        give_back(e - 1, it)
                    turn(e, it)
                    if e < EXPERTS - 1:
                        gather(e + 1, it)
                    down(e, it)

                def gathered():
                    gather(0, None)
                    self.experts(step)(pe)
                    give_back(EXPERTS - 1, None).then_inc(self.summed, 1)

                self.either(pe, gathered, lambda: self.dense.pe(pe))
                stage_end(pe)

            def act(self, act):
                at = self.at

                def copy_x(e, it):
                    act.wait_ge(self.gathered, at(e + 1, it))
                    act.copy(ge_xT[:], ps[:, 0, :].rearrange("p (k n) -> p k n", k=KC)).then_inc(self.xT, 1)

                def step(e, it):
                    act.wait_ge(self.gate_up, at(e + 1, it))
                    act.activation(ge_th[:], ps[:, 1, 0:BLK], ACT.Tanh, scale=0.5).then_inc(self.tanh, 1)
                    act.wait_ge(self.turned, at(e + 1, it))
                    act.copy(ge_turned[:], ps[:, 2, :].rearrange("p (c n) -> p c n", c=4)).then_inc(self.copied, 1)
                    if e < EXPERTS - 1:
                        copy_x(e + 1, it)

                def gathered():
                    copy_x(0, None)
                    self.experts(step)(act)

                self.either(act, gathered, lambda: self.dense.act(act))
                stage_end(act)

            def dve(self, dve, own):
                at = self.at

                def select(e, it):
                    column = e if it is None else e + 2 * it
                    for t in range(T):
                        where, share = place[:, t, bass.ds(column, 1)], gate_half[:, t, bass.ds(column, 1)]
                        dve.tensor_scalar(ge_sel[:, t], places[:, 0:PLACES], where, None, ALU.is_equal)
                        last = dve.tensor_scalar(ge_share[:, e % 2, t], places[:], where, share, ALU.is_equal, ALU.mult)
                    last.then_inc(self.sel, 1)

                def copy_y(e, it):
                    dve.wait_ge(weights_used, at(self.first + HALVES * (e + 1), it, HALVES))
                    dve.tensor_copy(ge_y[:], ps[:, 3, :]).then_inc(self.y, 1)

                def step(e, it):
                    if e > 0:
                        copy_y(e - 1, it)
                    else:
                        dve.wait_ge(self.gathered, 1)
                    if e < EXPERTS - 1:
                        select(e + 1, it)
                    dve.wait_ge(self.tanh, at(e + 1, it))
                    dve.scalar_tensor_tensor(out=ge_a[:], in0=ge_th[:], scalar=1.0, in1=ps[:, 1, 0:BLK], op0=ALU.add,
                                             op1=ALU.mult).then_inc(self.half, 1)
                    dve.wait_ge(self.half, at(e + 1, it))
                    dve.tensor_tensor(ge_hid[:], ge_a[:], ps[:, 1, BLK:2 * BLK], ALU.mult).then_inc(self.hid, 1)

                def gathered():
                    select(0, None)
                    self.experts(step)(dve)
                    copy_y(EXPERTS - 1, None)
                    dve.wait_ge(self.summed, 1)

                self.either(dve, gathered, lambda: self.dense.dve(dve, own))
                for t in range(T):
                    for half in range(2):
                        cut = slice(half * 512, (half + 1) * 512)
                        own(dve.tensor_tensor(xn[:, t, cut], ps[:, 4 + 2 * t + half, :], g_bc[:, 1, cut], ALU.mult))
                        dve.tensor_tensor(h[:, t, cut], h[:, t, cut], xn[:, t, cut], ALU.add)
                stage_end(dve)

        class FinalStage:
            def __init__(self):
                self.squares, self.rstd, self.made = sem("fin_squares"), sem("fin_rstd"), sem("fin_made")
                self.f_landed = sem("fin_gain_landed")

            def load(self, act):
                act.dma_start(f_bc[:], a["final_g_2"].partition_broadcast(P)).then_inc(self.f_landed, 16)

            def act(self, act):
                for t in range(T):
                    act.activation(xn[:, t], h[:, t], ACT.Square, scale=float(D) ** -0.5,
                                   accum_out=ms[:, t:t + 1]).then_inc(self.squares, 1)

            def dve(self, dve, own):
                dve.wait_ge(self.squares, T)
                rsqrt_ms(dve, own, T, self.rstd)
                dve.wait_ge(self.rstd, 1)
                dve.wait_ge(self.f_landed, 16)
                for t in range(T):
                    dve.scalar_tensor_tensor(out=xn[:, t], in0=h[:, t], scalar=rs[:, t:t + 1], in1=f_bc[:], op0=ALU.mult,
                                             op1=ALU.mult).then_inc(self.made, 1)

            def store(self, sp):
                o = out[0].rearrange("(t p) d -> p t d", p=P)
                for t in range(T):
                    sp.wait_ge(self.made, t + 1)
                    sp.dma_start(o[:, t], xn[:, t]).then_inc(out_landed, 16)
                sp.wait_ge(out_landed, 16 * T)

        def idle(eng):
            stage_end(eng)

        setup = SetupStage()
        norms = [NormStage(i, gain, shift) for i, (gain, shift) in enumerate([
            (lambda c: col("g_mix", c), None), (lambda c: col("g_ffn", c), None), (lambda c: col("g_ple", c), None),
            (lambda c: col("g_mix", KC + c), None), (lambda c: col("g_ffn", KC + c), None),
            (lambda c: col("g_ple", KC + c), None),
            (lambda c: mod_cols[:, 1, c:c + 1], lambda c: mod_cols[:, 0, c:c + 1]),
            (lambda c: mod_cols[:, 3, c:c + 1], lambda c: mod_cols[:, 2, c:c + 1])])]
        even = EvenStage()
        ffn = [GatedStage("ffn0", FF_BLOCKS, False), GatedStage("ffn1", FF_BLOCKS, False, ada_products)]
        ple = [PleStage(0), PleStage(1)]
        odd_in, odd_up, odd_heads, odd_attend, odd_out = OddIn(), OddUp(), OddHeads(), OddAttend(), OddOut()
        mod, conformer, route, final = ModStage(), ConformerStage(), RouteStage(), FinalStage()
        moe = ExpertsStage()

        block = ctx.enter_context(nc.Block())

        @block.scalar
        def _(act):
            setup.act(act)
            norms[0].act(act)
            even.act(act)
            norms[1].act(act)
            ffn[0].act(act)
            norms[2].act(act)
            ple[0].act(act)
            norms[3].act(act)
            odd_in.act(act)
            odd_up.act(act)
            odd_heads.act(act)
            odd_attend.act(act)
            odd_out.act(act)
            norms[4].act(act)
            mod.load(act)
            ffn[1].act(act)
            norms[5].act(act)
            ple[1].act(act)
            idle(act)
            final.load(act)
            norms[6].act(act)
            conformer.act(act)
            norms[7].act(act)
            route.act(act)
            moe.act(act)
            final.act(act)

        @block.gpsimd
        def _(pool):
            setup.pool(pool)
            for _ in range(7):
                idle(pool)
            odd_in.pool(pool)
            for _ in range(5):
                idle(pool)
            ada_loads(pool)
            for _ in range(8):
                idle(pool)

        @block.tensor
        def _(pe):
            setup.pe(pe)
            norms[0].pe(pe)
            even.pe(pe)
            norms[1].pe(pe)
            ffn[0].pe(pe)
            norms[2].pe(pe)
            ple[0].pe(pe)
            norms[3].pe(pe)
            odd_in.pe(pe)
            odd_up.pe(pe)
            odd_heads.pe(pe)
            odd_attend.pe(pe)
            odd_out.pe(pe)
            norms[4].pe(pe)
            ffn[1].pe(pe)
            norms[5].pe(pe)
            ple[1].pe(pe)
            mod.pe(pe)
            norms[6].pe(pe)
            conformer.pe(pe)
            norms[7].pe(pe)
            route.pe(pe)
            moe.pe(pe)

        @block.vector
        def _(dve):
            own = Own(dve, dve_own)
            setup.dve(dve, own)
            norms[0].dve(dve, own)
            even.dve(dve, own)
            norms[1].dve(dve, own)
            ffn[0].dve(dve, own)
            norms[2].dve(dve, own)
            ple[0].dve(dve, own)
            norms[3].dve(dve, own)
            odd_in.dve(dve, own)
            odd_up.dve(dve, own)
            odd_heads.dve(dve, own)
            odd_attend.dve(dve, own)
            odd_out.dve(dve, own)
            norms[4].dve(dve, own)
            ffn[1].dve(dve, own)
            norms[5].dve(dve, own)
            ple[1].dve(dve, own)
            mod.dve(dve, own)
            norms[6].dve(dve, own)
            conformer.dve(dve, own)
            norms[7].dve(dve, own)
            route.dve(dve, own)
            moe.dve(dve, own)
            final.dve(dve, own)

        @block.sync
        def _(sp):
            weight_stream(sp)
            final.store(sp)


_INS = ["x", "p", "positions", "g_mix", "g_ffn", "g_ple", "ev_w_in", "ev_w_conv", "ev_g_v", "ev_w_s", "ev_b_s", "ev_w_out",
        "od_w_in", "od_b_gate", "od_g_qa", "od_g_kva", "od_w_q_up", "od_w_kv_up", "od_g_q", "od_g_k", "od_g_mh", "od_w_out",
        "w_gate", "w_up", "w_down", "w_ple_proj", "w_ple_gate", "c_2", "ada_w_2", "ada_b_2", "norm_mix_g_2",
        "norm_ffn_g_2", "final_g_2", "conv_w_in_2", "conv_b_in_2", "conv_w_dw_2", "conv_b_dw_2", "conv_ln_g_2",
        "conv_ln_b_2", "conv_w_out_2", "moe_w_rg_2", "moe_b_rg_2", "moe_w_re_2", "moe_b_re_2", "moe_w_gate_2",
        "moe_w_up_2", "moe_w_down_2"]


def kernel(**inputs):
    import numpy as _np
    import concourse.bacc as _bacc
    from concourse import mybir as _mybir
    from concourse.bass_utils import run_bass_kernel_spmd as _run

    nc = _bacc.Bacc("TRN2", target_bir_lowering=False, num_devices=1)
    arrays, args = {}, {}
    for name in _INS:
        v = _np.ascontiguousarray(inputs[name])
        arrays[f"in_{name}"] = v
        args[name] = nc.dram_tensor(f"in_{name}", v.shape, _mybir.dt.from_np(v.dtype), kind="ExternalInput").ap()
    out = nc.dram_tensor("out", (1, S, D), F32, kind="ExternalOutput").ap()
    build(nc, args, out)
    r = _run(nc, [arrays], core_ids=[0])
    return r.results[0]["out"]
```

```python
from contextlib import ExitStack, contextmanager

import numpy as np

import concourse.bass as bass
from concourse import mybir

F32 = mybir.dt.float32
I32 = mybir.dt.int32
F32R = mybir.dt.float32r
ALU = mybir.AluOpType
ACT = mybir.ActivationFunctionType
AX = mybir.AxisListType

P = 128
D = 1024
S = 256
T = S // P
KC = D // P
EPS = 1e-6
NEG = -1e30

CONV_DIM = 512
GM_HEADS, GM_HD = 8, 64
Q_LORA, KV_LORA = 384, 256
HEADS, NOPE, ROPE, VD = 8, 64, 32, 64
QK = NOPE + ROPE
MH, MQK, MV = 4, 64, 128
ROPE_THETA = 10000.0
ODD_IN = Q_LORA + KV_LORA + ROPE + 2 * MH * MQK + 2 * MH * MV + 2 * MH
AT_KPE = Q_LORA + KV_LORA
AT_MQ = AT_KPE + ROPE
AT_MK = AT_MQ + MH * MQK
AT_MV = AT_MK + MH * MQK
AT_MO = AT_MV + MH * MV
AT_MI = AT_MO + MH * MV
D_FF = 2816
TAPS = 31
CONV_PE = (5, 6, 7)
DIAGS = 48
GROUPS, PER_GROUP = 4, 8
EXPERTS = GROUPS * PER_GROUP
EXPERT_HID = 512

BLK = 256
FF_BLOCKS = D_FF // BLK
HALVES = EXPERT_HID // BLK
MOE_BLOCKS = EXPERTS * HALVES
PLACES = 64
SLOT = 3 * KC * BLK
AT_DOWN = 2 * KC * BLK
SLOTS = 2

ITEMS = [("ev_in", 5, 1, 0), ("ev_out", 2, 1, 0), ("ffn0", FF_BLOCKS, 2, 1), ("ple0", 2, 1, 1), ("od_in", 5, 1, 0),
         ("od_up", 1, 1, 1), ("od_out", 2, 1, 0), ("ffn1", FF_BLOCKS, 2, 1), ("ple1", 2, 1, 1), ("conv_in", 4, 2, 0),
         ("conv_out", 2, 1, 0)]


class Part:

    def __init__(self, column):
        self.first, self.landed, counts = {}, [], [0] * SLOTS
        for row in ITEMS:
            self.first[row[0]] = len(self.landed)
            for _ in range(row[1] if row[column] else 0):
                s = len(self.landed) % SLOTS
                counts[s] += 16 * row[column]
                self.landed.append(counts[s])


A, B = Part(2), Part(3)

PIECE = 4 * BLK
PIECES = []
for _name, _n, _, _ in ITEMS:
    if _name == "od_up":
        continue
    for _i in range(_n):
        PIECES += [(_name, _i, _j) for _j in range(4)]
        if _name.startswith("ffn") and _i > 0:
            PIECES += [(_name, _i - 1, _j) for _j in (4, 5)]
    if _name.startswith("ffn"):
        PIECES += [(_name, _n - 1, _j) for _j in (4, 5)]
PIECE_AT = {_piece: _at for _at, _piece in enumerate(PIECES)}
BUFFERS = 4
FF_PIECES = 6
ADA_BUFFERS = 4
FF_ROUND = 4

ROWS_A, ROWS_B = {}, {}
for _rows, _names in ((ROWS_A, [("g_mix", 16), ("g_ffn", 16), ("g_ple", 16), ("norm_mix_g_2", 8), ("norm_ffn_g_2", 8),
                                ("conv_b_dw_2", 8), ("conv_ln_g_2", 8), ("conv_ln_b_2", 8), ("conv_b_in_2", 16),
                                ("od_g_qa", 3), ("od_g_kva", 2), ("ev_w_conv", 12)]),
                      (ROWS_B, [("ada_b_2", 48), ("ev_b_s", 8), ("c_2", 8)])):
    _at = 0
    for _n, _c in _names:
        _rows[_n] = (_at, _c)
        _at += _c
N_ROWS_A = sum(c for _, c in ROWS_A.values())
N_ROWS_B = sum(c for _, c in ROWS_B.values())
SMALL_LANDED = 16 * (14 + len(ROWS_B))


class Own:

    def __init__(self, eng, sem):
        self.eng, self.sem, self.n = eng, sem, 0

    def __call__(self, ins):
        self.n += 1
        ins.then_inc(self.sem, 1)
        self.eng.wait_ge(self.sem, self.n)


def build(nc, a, out, stop_after=None):
    ctx = ExitStack()
    with ctx:
        def sb(name, shape, dt=F32):
            return ctx.enter_context(nc.sbuf_tensor(name, shape, dt))

        def sem(name):
            return ctx.enter_context(nc.semaphore(name))

        dense_weights = sb("dense_weights", [P, SLOTS, SLOT])
        ring = [dense_weights[:, s] for s in range(SLOTS)]
        h = sb("h", [P, T, D])
        hnT = sb("hnT", [P, KC, S])
        xT_hi = sb("xT_hi", [P, KC, S], F32R)
        xT_lo = sb("xT_lo", [P, KC, S], F32R)
        g_bc = sb("g_bc", [P, 2, D])
        rstd = sb("rstd", [P, 4, T])
        xn = sb("xn", [P, T, D])
        mixT = sb("mixT", [P, KC, S])
        ident = sb("ident", [P, P])
        ones = sb("ones", [P, P])
        mean_w = sb("mean_w", [P, P])
        upper = sb("upper", [P, P])
        cmask = sb("cmask", [P, 3 * P])
        wsT = sb("wsT", [P, GM_HEADS, P])
        pT = sb("pT", [P, 2, 2, S])
        cols_a = sb("cols_a", [P, P])
        cols_b = sb("cols_b", [P, P])
        w_dw = sb("w_dw", [P, KC, TAPS])
        g_v = sb("g_v", [P, GM_HEADS * GM_HD])
        g_q = sb("g_q", [P, QK])
        g_k = sb("g_k", [P, QK])
        g_mh = sb("g_mh", [P, MH * MV])
        b_gate = sb("b_gate", [P, 2 * MH])
        b_route = sb("b_route", [P, GROUPS + EXPERTS])
        w_route = sb("w_route", [P, KC, GROUPS + EXPERTS])
        rev = sb("rev", [P, EXPERTS])
        pos_i = sb("pos_i", [P, T], I32)
        ms = sb("ms", [P, 64])
        rs = sb("rs", [P, 64])
        rtmp = sb("rtmp", [P, 2, 64])
        c_act = sb("c_act", [P, KC])
        mod_cols = sb("mod_cols", [P, 4, KC])
        gate_half = sb("gate_half", [P, T, EXPERTS])
        places = sb("places", [P, PLACES])
        ps = ctx.enter_context(nc.psum_tensor("ps", [P, 8, 512], F32))

        def col(name, c, n=1):
            rows, tile = (ROWS_A, cols_a) if name in ROWS_A else (ROWS_B, cols_b)
            at = rows[name][0] + c
            return tile[:, at:at + n]

        @contextmanager
        def scope():
            with ExitStack() as inner:
                yield lambda name, shape, dt=F32: inner.enter_context(nc.sbuf_tensor(name, shape, dt))

        with scope() as dense:
            w_hi = dense("w_hi", [P, BUFFERS, PIECE], F32R)
            w_lo = dense("w_lo", [P, BUFFERS, PIECE], F32R)
            with scope() as st:
                ws_rows = st("ws_rows", [P, GM_HEADS, P])
                p_rows = st("p_rows", [P, 2, T, 256])
                rows_a = st("rows_a", [P, P])
                rows_b = st("rows_b", [P, P])
                dw_rows = st("dw_rows", [TAPS, D])
                rev_i = st("rev_i", [P, EXPERTS], I32)
                places_i = st("places_i", [P, PLACES], I32)
            with scope() as st:
                ev_x = st("ev_x", [P, 4, S])
                ev_z = st("ev_z", [P, 4, S + 2])
                ev_y = st("ev_y", [P, 4, S])
                gm_v = st("gm_v", [P, T, 512])
                gm_u = st("gm_u", [P, T, 512])
                gm_t = st("gm_t", [P, T, 512])
                gm_s = st("gm_s", [P, T, 512])
            with scope() as st:
                od_z = st("od_z", [P, T, ODD_IN])
                od_q = st("od_q", [P, T, HEADS, QK])
                od_kv = st("od_kv", [P, T, HEADS, NOPE + VD])
                od_k = st("od_k", [P, T, HEADS, QK])
                cs = st("cs", [P, 2, T, ROPE // 2])
                ang = st("ang", [P, T, ROPE // 2])
                inv_freq = st("inv_freq", [P, ROPE // 2])
                posf = st("posf", [P, T])
                turns = st("turns", [P, T, ROPE // 2])
                sm = st("sm", [P, 2, 3 * P])
                prob = st("prob", [P, 2, 3 * P])
                probT = st("probT", [P, 2, 3 * P])
                nmax = st("nmax", [P, HEADS + MH, T])
                rsum = st("rsum", [P, T, HEADS])
                gts = st("gts", [P, T, 2 * MH])
                lf = st("lf", [P, 3, T, MH])
                acum = st("acum", [P, T, MH])
                bcol = st("bcol", [P, T, MH])
                emt = st("emt", [P, T, MH])
                den = st("den", [P, 2, T])
            with scope() as st:
                ff_th = st("ff_th", [P, T, BLK])
                ff_a = st("ff_a", [P, T, BLK])
                ff_hid = st("ff_hid", [P, T, BLK])
                ff_hidT_hi = st("ff_hidT_hi", [P, 2, S], F32R)
                ff_hidT_lo = st("ff_hidT_lo", [P, 2, S], F32R)
                ada_acc = st("ada_acc", [P, 6 * D])
                with scope() as st2:
                    ada_w = st2("ada_w", [P, ADA_BUFFERS, KC // 2, BLK])
                with scope() as st2:
                    ple_th = st2("ple_th", [P, T, 512])
                    ple_a = st2("ple_a", [P, T, 512])
            with scope() as st:
                u_pad = st("u_pad", [P, KC, S + TAPS - 1])
                cf_th = st("cf_th", [P, 2, S])
                cf_a = st("cf_a", [P, 2, S])
                cf_r = st("cf_r", [P, 4, S])
                diag = st("diag", [P, DIAGS, P])
                half = st("half", [P, 4 * KC])
        with scope() as experts:
            odd_expert = experts("odd_expert", [P, SLOTS * SLOT])
            f_bc = experts("f_bc", [P, D])
            place = experts("place", [P, T, EXPERTS])
            crowded = experts("crowded", [P, 1], I32)
            with scope() as st:
                rt = st("rt", [P, 9, T, EXPERTS])
                rts = st("rts", [P, 11, T])
            with scope() as st:
                ge_sel = st("ge_sel", [P, T, P])
                ge_share = st("ge_share", [P, T, P])
                ge_xT = st("ge_xT", [P, KC, P])
                ge_th = st("ge_th", [P, 2, BLK])
                ge_a = st("ge_a", [P, BLK])
                ge_hid = st("ge_hid", [P, 2, BLK])
                ge_hidT = st("ge_hidT", [P, 2, 2, P])
                ge_shareT = st("ge_shareT", [P, T, P])
                ge_y = st("ge_y", [P, 2, 512])
            with scope() as st:
                all_th = st("all_th", [P, T, BLK])
                all_a = st("all_a", [P, T, BLK])
                all_hid = st("all_hid", [P, 2, T, BLK])
                all_hidT = st("all_hidT", [P, 2, S])
        mqkT = wsT[:].rearrange("p h n -> p (h n)").rearrange("p (c s) -> p c s", c=4)
        lat = xn[:, :, 0:Q_LORA + KV_LORA]
        latT = mixT[:, 0:5, :]
        qT, kT = hnT, mixT
        v_aug = od_q[:].rearrange("p t h d -> p (t h d)")[:, 0:T * MH * (MV + 1)].rearrange(
            "p (t h d) -> p t h d", t=T, h=MH)
        b_masked = od_k[:].rearrange("p t h d -> p (t h d)").rearrange("p (h n) -> p h n", h=MH)
        diag_b = xn[:].rearrange("p t d -> p (t d)")[:, 0:T * MH * P].rearrange("p (t h n) -> p t h n", t=T, h=MH)
        mix = xn
        y_d = mix[:, :, HEADS * VD:].rearrange("p t (h d) -> p t h d", h=MH)
        a_landed = [sem(f"weights_a_landed{s}") for s in range(SLOTS)]
        b_landed = [sem(f"weights_b_landed{s}") for s in range(SLOTS)]
        hi_ready = sem("pieces_hi_ready")
        piece_ready = sem("pieces_ready")
        pieces_used = sem("pieces_used")
        ple_used = sem("ple_proj_used")
        up_used = sem("od_up_used")
        gu_landed = [sem(f"experts_gate_up_landed{s}") for s in range(2)]
        down_landed = [sem(f"experts_down_landed{s}") for s in range(2)]
        gu_used, down_used = sem("experts_gate_up_used"), sem("experts_down_used")
        stage_over = sem("stage_over")
        small_landed = sem("small_landed")
        out_landed = sem("out_landed")
        dve_own = sem("dve_own")
        h_ready = sem("h_ready")
        ada_landed = [sem(f"ada_landed{s}") for s in range(ADA_BUFFERS)]
        ada_used = sem("ada_used")
        ends = {}

        def stage_end(eng):
            ends[id(eng)] = ends.get(id(eng), 0) + 1
            eng.drain().then_inc(stage_over, 1)
            eng.wait_ge(stage_over, 4 * ends[id(eng)])

        def per_round(value, it, count):
            return value if it is None else value + count * it

        def part_a(name, i, n=AT_DOWN):
            return ring[(A.first[name] + i) % SLOTS][:, 0:n]

        def part_b(name, i):
            return ring[(B.first[name] + i) % SLOTS][:, AT_DOWN:SLOT]

        def wait_a(eng, name, i, it=None):
            at = A.first[name] + i
            eng.wait_ge(a_landed[at % SLOTS], per_round(A.landed[at], it, 32 * FF_ROUND // SLOTS))

        def wait_b(eng, name, i, it=None):
            at = B.first[name] + i
            eng.wait_ge(b_landed[at % SLOTS], per_round(B.landed[at], it, 16 * FF_ROUND // SLOTS))

        def width(name, i):
            return min(512, ODD_IN - 512 * i) if name == "od_in" else 512

        def piece(name, i, j):
            if j >= 4:
                return part_b(name, i)[:, (j - 4) * PIECE:(j - 3) * PIECE]
            n = width(name, i)
            if name == "ev_in" and i >= 2:
                return part_a(name, i).rearrange("p (k n) -> p k n", k=KC)[:, :, j * P:(j + 1) * P]
            if name == "conv_in":
                ag = part_a(name, i).rearrange("p (k two n) -> p k two n", k=KC, two=2)
                return ag[:, :, j % 2, (j // 2) * P:(j // 2 + 1) * P]
            return part_a(name, i)[:, 2 * n * j:2 * n * (j + 1)]

        def split_view(parts, name, i, j):
            v = parts[:, PIECE_AT[name, i, j] % BUFFERS]
            if (name == "ev_in" and i >= 2) or name == "conv_in":
                return v.rearrange("p (k n) -> p k n", k=KC)
            return v if j >= 4 else v[:, 0:2 * width(name, i)]

        def split_hi(act, name, i, j, it=None):
            at = PIECE_AT[name, i, j]
            if j == 0:
                wait_a(act, name, i, it)
            elif j == 4:
                wait_b(act, name, i, it)
            if at >= BUFFERS:
                act.wait_ge(pieces_used, per_round(at - BUFFERS + 1, it, FF_ROUND * FF_PIECES))
            act.copy(split_view(w_hi, name, i, j), piece(name, i, j)).then_inc(hi_ready, 1)

        def split_lo(dve, name, i, j, it=None):
            dve.wait_ge(hi_ready, per_round(PIECE_AT[name, i, j] + 1, it, FF_ROUND * FF_PIECES))
            dve.tensor_tensor(split_view(w_lo, name, i, j), piece(name, i, j), split_view(w_hi, name, i, j).bitcast(F32),
                              ALU.subtract).then_inc(piece_ready, 1)

        split_done = {}

        def split_upto(eng, split, name, i, j, ahead=BUFFERS - 1):
            for at in range(split_done.get(id(eng), 0), min(PIECE_AT[name, i, j] + ahead + 1, len(PIECES))):
                split(eng, *PIECES[at])
                split_done[id(eng)] = at + 1

        def split_counted(eng, name, i, j):
            split_done[id(eng)] = PIECE_AT[name, i, j] + 1

        def halves(pe, name, i, j, it=None):
            pe.wait_ge(piece_ready, per_round(PIECE_AT[name, i, j] + 1, it, FF_ROUND * FF_PIECES))
            return split_view(w_hi, name, i, j), split_view(w_lo, name, i, j)

        def wait_used(eng, name, i, j, it=None):
            eng.wait_ge(pieces_used, per_round(PIECE_AT[name, i, j] + 1, it, FF_ROUND * FF_PIECES))

        def three_passes(pe, out, left, right, start, stop):
            pe.matmul(out, left[1], right[0], start=start, stop=False)
            pe.matmul(out, left[0], right[1], start=False, stop=False)
            return pe.matmul(out, left[0], right[0], start=False, stop=stop)

        def tokens_by_columns(pe, name, i, banks, n=512, norm=None):
            for j in range(4):
                w = [v.rearrange("p (k n) -> p k n", k=2) for v in halves(pe, name, i, j)]
                if j == 2 and norm is not None:
                    norm.wait_rest(pe)
                for kk in range(2):
                    for t in range(T):
                        x = [v[:, 2 * j + kk, t * P:(t + 1) * P] for v in (xT_hi, xT_lo)]
                        last = three_passes(pe, ps[:, banks[t], 0:n], x, [v[:, kk, :] for v in w],
                                            start=(j == 0 and kk == 0), stop=(j == 3 and kk == 1))
                last.then_inc(pieces_used, 1)

        def columns_by_tokens(pe, out, w):
            for k in range(KC):
                last = three_passes(pe, out, [v[:, k, :] for v in w], (xT_hi[:, k], xT_lo[:, k]),
                                    start=(k == 0), stop=(k == KC - 1))
            return last

        expert_tiles = [dense_weights[:].rearrange("p s f -> p (s f)"), odd_expert[:]]

        def gate_up_of(e):
            return expert_tiles[e % 2][:, 0:KC * 2 * EXPERT_HID].rearrange("p (k two f) -> p k two f", k=KC, two=2)

        def down_of(e):
            return expert_tiles[e % 2][:, KC * 2 * EXPERT_HID:].rearrange("p (c d) -> p c d", d=D)

        def wait_gate_up(eng, e, it=None):
            eng.wait_ge(gu_landed[e % 2], per_round(32 * (e // 2 + 1), it, 32))

        def wait_down(eng, e, it=None):
            eng.wait_ge(down_landed[e % 2], per_round(16 * (e // 2 + 1), it, 16))

        def cols8(tile, n=512):
            return tile[:, 0:KC * n].rearrange("p (k n) -> p k n", k=KC)

        def weight_stream(sp):
            def wait_split(name, i, j, it):
                sp.wait_ge(piece_ready, per_round(PIECE_AT[name, i, j] + 1, it, FF_ROUND * FF_PIECES))

            def before(part, name, i):
                at = part.first[name] + i - SLOTS
                if at < 0:
                    return None, None
                stage = [row[0] for row in ITEMS if row[2 if part is A else 3] and part.first[row[0]] <= at][-1]
                return stage, at - part.first[stage]

            def load_a(name, i, dst, srcs, it=None):
                stage, k = before(A, name, i)
                if stage == "od_up":
                    sp.wait_ge(up_used, 1)
                elif stage is not None:
                    wait_split(stage, k, 3, it)
                for d, src in zip(dst, srcs):
                    sp.dma_start(d, src).then_inc(a_landed[(A.first[name] + i) % SLOTS], 16)

            def load_b(name, i, dst, src, it=None):
                stage, k = before(B, name, i)
                if stage == "od_up":
                    sp.wait_ge(up_used, 1)
                elif stage is not None and stage.startswith("ple"):
                    sp.wait_ge(ple_used, 2 * int(stage[-1]) + k + 1)
                elif stage is not None:
                    wait_split(stage, k, 5, it)
                sp.dma_start(dst, src).then_inc(b_landed[(B.first[name] + i) % SLOTS], 16)

            def columns(name, w, starts):
                wv = w.rearrange("(k p) n -> p k n", p=P)
                for i, c in enumerate(starts):
                    if name == "ev_in" and i == 1:
                        sp.wait_ge(small_landed, SMALL_LANDED)
                    n = width(name, i)
                    load_a(name, i, [cols8(part_a(name, i, KC * n), n)], [wv[:, :, c:c + n]])

            def two_sided(name, i):
                ag = part_a(name, i).rearrange("p (k two n) -> p k two n", k=KC, two=2)
                return [ag[:, :, side, :] for side in range(2)]

            def ffn(layer):
                name = f"ffn{layer}"
                g = a["w_gate"][layer].rearrange("(k p) f -> p k f", p=P)
                u = a["w_up"][layer].rearrange("(k p) f -> p k f", p=P)
                d = a["w_down"][layer].rearrange("(n c p) d -> p n c d", p=P, c=2)

                def block(n, it):
                    m = n if it is None else n + FF_ROUND * it
                    cut = bass.ds(m * BLK, BLK)
                    load_a(name, n, two_sided(name, n), [g[:, :, cut], u[:, :, cut]], it)
                    load_b(name, n, part_b(name, n).rearrange("p (c d) -> p c d", c=2), d[:, m], it)
                for n in range(3):
                    block(n, None)
                with sp.Fori(0, (FF_BLOCKS - 3) // FF_ROUND) as it:
                    for n in range(3, 3 + FF_ROUND):
                        block(n, it)

            def ple(layer):
                name = f"ple{layer}"
                w = a["w_ple_gate"][layer].rearrange("(k p) n -> p k n", p=P)
                q = a["w_ple_proj"][layer].rearrange("(k p) n -> p k n", p=P)
                for i in range(2):
                    load_a(name, i, [cols8(part_a(name, i))], [w[:, :, i * 512:(i + 1) * 512]])
                    load_b(name, i, part_b(name, i)[:, 0:2 * 512].rearrange("p (k n) -> p k n", k=2),
                           q[:, :, i * 512:(i + 1) * 512])

            columns("ev_in", a["ev_w_in"][0], [2048, 1536, 512, 1024, 0])
            columns("ev_out", a["ev_w_out"][0], [0, 512])
            ffn(0)
            ple(0)
            columns("od_in", a["od_w_in"][0], range(0, ODD_IN, 512))
            load_a("od_up", 0, [part_a("od_up", 0, 3 * 768).rearrange("p (k n) -> p k n", k=3)],
                   [a["od_w_q_up"][0].rearrange("(k p) n -> p k n", p=P)])
            load_b("od_up", 0, part_b("od_up", 0).rearrange("p (k n) -> p k n", k=2),
                   a["od_w_kv_up"][0].rearrange("(k p) n -> p k n", p=P))
            columns("od_out", a["od_w_out"][0], [0, 512])
            ffn(1)
            ple(1)
            w = a["conv_w_in_2"][0].rearrange("(k p) n -> p k n", p=P)
            for i in range(4):
                load_a("conv_in", i, two_sided("conv_in", i), [w[:, :, j * D + i * BLK:j * D + (i + 1) * BLK] for j in range(2)])
            columns("conv_out", a["conv_w_out_2"][0], [0, 512])

            g = a["moe_w_gate_2"][0].rearrange("e (k p) f -> p e k f", p=P)
            u = a["moe_w_up_2"][0].rearrange("e (k p) f -> p e k f", p=P)
            d = a["moe_w_down_2"][0].rearrange("e (c p) d -> p e c d", p=P)

            def gate_up(e, it):
                for side, w in enumerate((g, u)):
                    sp.dma_start(gate_up_of(e)[:, :, side, :], w[:, per_round(e, it, 2)]).then_inc(gu_landed[e % 2], 16)

            def down(e, it):
                sp.dma_start(down_of(e), d[:, per_round(e, it, 2)]).then_inc(down_landed[e % 2], 16)

            wait_split("conv_out", 1, 3, None)
            sp.wait_ge(ple_used, 4)
            gate_up(0, None)
            sp.wait_ge(h_ready, 14)
            gate_up(1, None)
            for e in range(2):
                down(e, None)
            with sp.Fori(0, EXPERTS // 2 - 1) as it:
                for e in range(2):
                    sp.wait_ge(gu_used, per_round(e + 1, it, 2))
                    gate_up(2 + e, it)
                sp.wait_ge(down_used, it + 1)
                for e in range(2):
                    down(2 + e, it)

        def rsqrt(dve, own, x, y, t0, t1, done=None):
            own(dve.tensor_scalar(x, x, EPS, None, ALU.add))
            own(dve.tensor_scalar(t0.bitcast(I32), x.bitcast(I32), 1, None, ALU.logical_shift_right))
            own(dve.tensor_scalar(y.bitcast(I32), t0.bitcast(I32), -1.0, float(0x5F3759DF), ALU.mult, ALU.add))
            for i in range(3):
                own(dve.tensor_tensor(t0, y, y, ALU.mult))
                own(dve.scalar_tensor_tensor(out=t1, in0=t0, scalar=-0.5, in1=x, op0=ALU.mult, op1=ALU.mult))
                last = dve.scalar_tensor_tensor(out=y, in0=t1, scalar=1.5, in1=y, op0=ALU.add, op1=ALU.mult)
                if i < 2 or done is None:
                    own(last)
            if done is not None:
                last.then_inc(done, 1)

        def rsqrt_ms(dve, own, n, done=None):
            rsqrt(dve, own, ms[:, 0:n], rs[:, 0:n], rtmp[:, 0, 0:n], rtmp[:, 1, 0:n], done)

        class NormStage:
            squares, made, scaled, turned, hi, ready = (sem("norm_" + n) for n in ("squares", "made", "scaled", "turned", "hi",
                                                                                   "ready"))

            def __init__(self, index, gain, shift=None, folded=False, split=True):
                self.index, self.gain, self.shift, self.folded, self.split = index, gain, shift, folded, split
                self.scaled_before = T * sum(1 for i in (0, 6, 7) if i < index)
                self.split_before = KC * index

            def source(self, c):
                return ps[:, c // 2, (c % 2) * S:(c % 2 + 1) * S]

            def act(self, act, split_ahead=None):
                if split_ahead is not None:
                    split_upto(act, split_hi, *split_ahead, ahead=0)
                if not self.folded:
                    self.sum_squares(act)
                    act.wait_ge(self.made, self.index + 1)
                    act.activation(xn[:, 0], h[:, 0], ACT.Copy, scale=rstd[:, 0, 0:1]).then_inc(self.scaled, 1)
                if self.split:
                    for c in range(KC):
                        if c % 2 == 0:
                            act.wait_ge(self.turned, 4 * self.index + c // 2 + 1)
                        bias = 0.0 if self.shift is None else self.shift(c)
                        act.activation(xT_hi[:, c], self.source(c), ACT.Identity, scale=self.gain(c), bias=bias).then_inc(self.hi, 1)
                if self.folded:
                    self.sum_squares(act)

            def sum_squares(self, act):
                if self.index:
                    act.wait_ge(h_ready, 2 * self.index)
                for t in range(T):
                    act.activation(xn[:, t], h[:, t], ACT.Square, scale=float(D) ** -0.5,
                                   accum_out=ms[:, t:t + 1]).then_inc(self.squares, 1)

            def dve(self, dve, own, split_ahead=None):
                if split_ahead is not None:
                    split_upto(dve, split_lo, *split_ahead, ahead=0)
                if not self.folded:
                    self.factors(dve, own)
                    dve.wait_ge(self.made, self.index + 1)
                    dve.tensor_scalar(xn[:, 1], h[:, 1], rstd[:, 0, 1:2], None, ALU.mult).then_inc(self.scaled, 1)
                for c in range(KC):
                    if c % 2 == 0:
                        dve.wait_ge(self.turned, 4 * self.index + c // 2 + 1)
                        if self.split:
                            dve.wait_ge(self.hi, KC * self.index + c + 2)
                    if self.shift is not None:
                        own(dve.tensor_scalar(hnT[:, c], self.source(c), self.gain(c), self.shift(c), ALU.mult, ALU.add))
                    if self.split:
                        hi = xT_hi[:, c].bitcast(F32)
                        if self.shift is None:
                            ins = dve.scalar_tensor_tensor(out=xT_lo[:, c], in0=self.source(c), scalar=self.gain(c), in1=hi,
                                                           op0=ALU.mult, op1=ALU.subtract)
                        else:
                            ins = dve.tensor_tensor(xT_lo[:, c], hnT[:, c], hi, ALU.subtract)
                        ins.then_inc(self.ready, 1)
                if self.folded:
                    self.factors(dve, own)

            def factors(self, dve, own):
                dve.wait_ge(self.squares, T * (self.index + 1))
                rsqrt(dve, own, ms[:, 0:T], rstd[:, 0], rtmp[:, 0, 0:T], rtmp[:, 1, 0:T])
                own(dve.tensor_scalar(rstd[:, 1], rstd[:, 0], 0.5, None, ALU.mult))
                dve.tensor_tensor(rstd[:, 2], rstd[:, 0], rstd[:, 1], ALU.mult).then_inc(self.made, 1)

            def pe(self, pe):
                if not self.folded:
                    pe.wait_ge(self.scaled, self.scaled_before + T)
                src = h if self.folded else xn
                for b in range(4):
                    if self.folded and b % 2 == 0:
                        pe.wait_ge(h_ready, 2 * self.index - 1 + b // 2)
                    for c in (2 * b, 2 * b + 1):
                        for t in range(T):
                            last = pe.transpose(self.source(c)[:, t * P:(t + 1) * P], src[:, t, c * P:(c + 1) * P], ident[:])
                    last.then_inc(self.turned, 1)
                if self.folded:
                    pe.wait_ge(self.ready, KC * self.index + KC // 2)
                elif self.split:
                    self.wait_rest(pe)

            def wait_rest(self, pe):
                pe.wait_ge(self.ready, KC * (self.index + 1))

            def wait_factors(self, eng):
                eng.wait_ge(self.made, self.index + 1)

        class FfnStage:
            gate_half_made, hid, turned, hidT_hi, hidT = (sem("ff_" + n) for n in ("half_made", "hid_ready", "turned", "hidT_hi_ready",
                                                                                  "hidT_ready"))
            tanh = sem("ff_tanh")

            def __init__(self, layer, norm, side=None):
                self.name, self.norm = f"ffn{layer}", norm
                self.before = layer * FF_BLOCKS
                self.side = side

            def count(self, blocks, it, per_block=1):
                return per_round(per_block * (self.before + blocks), it, per_block * FF_ROUND)

            def run(self, eng, step):
                step(0, None)
                step(1, None)
                split_counted_at = 2 + FF_ROUND
                with eng.Fori(0, (FF_BLOCKS - 3) // FF_ROUND) as it:
                    for n in range(2, split_counted_at):
                        step(n, it)
                step(FF_BLOCKS - 1, None)

            def pe(self, pe):
                name, last_block = self.name, FF_BLOCKS - 1

                def gate_up(n, it, pieces):
                    for j in pieces:
                        w = [v.rearrange("p (k n) -> p k n", k=2) for v in halves(pe, name, n, j, it)]
                        if n == 0 and j == 2:
                            self.norm.wait_rest(pe)
                        if j == 0 and n >= 1:
                            pe.wait_ge(self.hid, self.count(n, it, T))
                        for kk in range(2):
                            for t in range(T):
                                x = [v[:, 2 * j + kk, t * P:(t + 1) * P] for v in (xT_hi, xT_lo)]
                                last = three_passes(pe, ps[:, t, :], x, [v[:, kk, :] for v in w],
                                                    start=(j == 0 and kk == 0), stop=(j == 3 and kk == 1))
                        last.then_inc(pieces_used, 1)

                def turn(n, it):
                    pe.wait_ge(self.hid, self.count(n + 1, it, T))
                    for c in range(2):
                        for t in range(T):
                            last = pe.transpose(ps[:, 2, c * S + t * P:c * S + (t + 1) * P],
                                                ff_hid[:, t, c * P:(c + 1) * P], ident[:])
                    last.then_inc(self.turned, 1)

                def down(n, it):
                    pe.wait_ge(self.hidT, self.count(n + 1, it))
                    for c in range(2):
                        w = halves(pe, name, n, 4 + c, it)
                        for t in range(T):
                            x = [v[:, c, t * P:(t + 1) * P] for v in (ff_hidT_hi, ff_hidT_lo)]
                            for half in range(2):
                                last = three_passes(pe, ps[:, 4 + 2 * t + half, :], x, [v[:, half * 512:(half + 1) * 512] for v in w],
                                                    start=(n == 0 and c == 0), stop=(n == last_block and c == 1))
                        last.then_inc(pieces_used, 1)

                def step(n, it):
                    gate_up(n, it, (0, 1))
                    if n >= 1:
                        turn(n - 1, it)
                    gate_up(n, it, (2, 3))
                    if n >= 1:
                        down(n - 1, it)

                self.run(pe, step)
                turn(last_block, None)
                down(last_block, None)

            def splits(self, eng, split, n, it, which):
                ahead = [(n, 3), (n - 1, 4), (n - 1, 5), (n + 1, 0), (n + 1, 1), (n + 1, 2)]
                if n == FF_BLOCKS - 1:
                    at = PIECE_AT[self.name, n - 1, 5]
                    ahead[3:] = [PIECES[at + 1], PIECES[at + 2], PIECES[at + 3]]
                for q in which:
                    stage, block, j = ahead[q] if len(ahead[q]) == 3 else (self.name,) + ahead[q]
                    if block >= 0:
                        split(eng, stage, block, j, it)

            def act(self, act):
                split_upto(act, split_hi, self.name, 0, 2, ahead=0)
                self.norm.wait_factors(act)

                def step(n, it):
                    self.splits(act, split_hi, n, it, (0, 1, 2))
                    if n >= 1:
                        copy(n - 1, it)
                    self.splits(act, split_hi, n, it, (3,))
                    wait_used(act, self.name, n, 3, it)
                    for t in range(T):
                        act.activation(ff_th[:, t], ps[:, t, 0:BLK], ACT.Tanh, scale=rstd[:, 1, t:t + 1]).then_inc(self.tanh, 1)
                    self.splits(act, split_hi, n, it, (4, 5))

                def copy(n, it):
                    act.wait_ge(self.turned, self.count(n + 1, it))
                    act.copy(ff_hidT_hi[:], ps[:, 2, :].rearrange("p (c s) -> p c s", c=2)).then_inc(self.hidT_hi, 1)

                self.run(act, step)
                self.rest(act, split_hi, copy)

            def rest(self, eng, split, copy):
                copy(FF_BLOCKS - 1, None)
                at = PIECE_AT[self.name, FF_BLOCKS - 1, 5]
                split_counted(eng, *PIECES[at + 1])
                split_upto(eng, split, *PIECES[at + 3], ahead=0)

            def dve(self, dve, own):
                split_upto(dve, split_lo, self.name, 0, 2, ahead=0)

                def step(n, it):
                    self.splits(dve, split_lo, n, it, (0, 1, 2))
                    if n >= 1:
                        copy(n - 1, it)
                    self.splits(dve, split_lo, n, it, (3,))
                    for t in range(T):
                        dve.wait_ge(self.tanh, self.count(n, it, T) + t + 1)
                        dve.scalar_tensor_tensor(out=ff_a[:, t], in0=ff_th[:, t], scalar=1.0, in1=ps[:, t, 0:BLK],
                                                 op0=ALU.add, op1=ALU.mult).then_inc(self.gate_half_made, 1)
                    for t in range(T):
                        dve.wait_ge(self.gate_half_made, self.count(n, it, T) + t + 1)
                        dve.scalar_tensor_tensor(out=ff_hid[:, t], in0=ff_a[:, t], scalar=rstd[:, 2, t:t + 1],
                                                 in1=ps[:, t, BLK:2 * BLK], op0=ALU.mult, op1=ALU.mult).then_inc(self.hid, 1)
                    self.splits(dve, split_lo, n, it, (4, 5))
                    if self.side is not None:
                        self.side(dve, n, it)

                def copy(n, it):
                    dve.wait_ge(self.hidT_hi, self.count(n + 1, it))
                    dve.tensor_tensor(ff_hidT_lo[:], ps[:, 2, :].rearrange("p (c s) -> p c s", c=2), ff_hidT_hi[:].bitcast(F32),
                                      ALU.subtract).then_inc(self.hidT, 1)

                self.run(dve, step)
                self.rest(dve, split_lo, copy)
                wait_used(dve, self.name, FF_BLOCKS - 1, 5)
                for half in range(2):
                    for t in range(T):
                        o = h[:, t, half * 512:(half + 1) * 512]
                        ins = dve.tensor_tensor(o, o, ps[:, 4 + 2 * t + half, :], ALU.add)
                    ins.then_inc(h_ready, 1)

        class PleStage:
            tanh = sem("ple_tanh")

            def __init__(self, layer, norm):
                self.layer, self.name, self.norm = layer, f"ple{layer}", norm

            def pe(self, pe):
                for i in range(2):
                    tokens_by_columns(pe, self.name, i, (4 * i, 4 * i + 1), norm=self.norm if i == 0 else None)
                    wait_b(pe, self.name, i)
                    q = part_b(self.name, i)[:, 0:2 * 512].rearrange("p (k n) -> p k n", k=2)
                    for t in range(T):
                        for k in range(2):
                            last = pe.matmul(ps[:, 4 * i + 2 + t, :], pT[:, self.layer, k, t * P:(t + 1) * P],
                                             q[:, k, :], start=(k == 0), stop=(k == 1))
                    last.then_inc(ple_used, 1)

            def act(self, act):
                split_upto(act, split_hi, self.name, 0, 2, ahead=0)
                self.norm.wait_factors(act)
                for i in range(2):
                    split_upto(act, split_hi, self.name, i, 3)
                    wait_used(act, self.name, i, 3)
                    for t in range(T):
                        if i > 0:
                            act.wait_ge(self.used, 2 * (2 * self.layer + i - 1) + t + 1)
                        act.activation(ple_th[:, t], ps[:, 4 * i + t, :], ACT.Tanh,
                                       scale=rstd[:, 1, t:t + 1]).then_inc(self.tanh, 1)

            used = sem("ple_tanh_used")

            def dve(self, dve, own):
                for i in range(2):
                    split_upto(dve, split_lo, self.name, i, 3)
                    dve.wait_ge(ple_used, 2 * self.layer + i + 1)
                    for t in range(T):
                        n = 2 * (2 * self.layer + i) + t + 1
                        dve.wait_ge(self.tanh, n)
                        dve.scalar_tensor_tensor(out=ple_a[:, t], in0=ple_th[:, t], scalar=1.0, in1=ps[:, 4 * i + 2 + t, :],
                                                 op0=ALU.add, op1=ALU.mult).then_inc(self.used, 1)
                        dve.wait_ge(self.used, n)
                        o = h[:, t, i * 512:(i + 1) * 512]
                        ins = dve.scalar_tensor_tensor(out=o, in0=ple_a[:, t], scalar=0.5, in1=o, op0=ALU.mult, op1=ALU.add)
                    ins.then_inc(h_ready, 1)

        class SetupStage:
            def __init__(self):
                self.rows_landed = sem("rows_landed")
                self.consts = sem("consts_made")
                self.own_consts = sem("consts_under_way")
                self.turned = sem("setup_turned")
                self.h_landed = sem("h_landed")
                self.cols = sem("setup_cols")

            def loads(self):
                for name, dst in (("ev_g_v", g_v), ("od_g_mh", g_mh)):
                    yield dst[:], a[name][0].rearrange("h d -> (h d)").partition_broadcast(P)
                yield g_q[:], a["od_g_q"][0].partition_broadcast(P)
                yield g_k[:], a["od_g_k"][0].partition_broadcast(P)
                yield b_gate[:], a["od_b_gate"][0].partition_broadcast(P)
                yield b_route[:, 0:GROUPS], a["moe_b_rg_2"][0].partition_broadcast(P)
                yield b_route[:, GROUPS:], a["moe_b_re_2"][0].partition_broadcast(P)
                yield w_route[:, :, 0:GROUPS], a["moe_w_rg_2"][0].rearrange("(k p) n -> p k n", p=P)
                yield w_route[:, :, GROUPS:], a["moe_w_re_2"][0].rearrange("(k p) n -> p k n", p=P)
                yield pos_i[:], a["positions"].rearrange("b (t p) -> p (b t)", p=P)
                yield ws_rows[:], a["ev_w_s"][0].rearrange("h t s -> t h s")
                for layer in range(2):
                    yield p_rows[:, layer], a["p"][layer, 0].rearrange("(t p) d -> p t d", p=P)
                yield dw_rows[:], a["conv_w_dw_2"][0]
                yield from self.rows(ROWS_B, rows_b)

            def rows(self, rows, tile):
                for name, (at, n) in rows.items():
                    v = a[name]
                    flat = v.rearrange(" ".join("abcd"[:len(v.shape)]) + " -> (" + " ".join("abcd"[:len(v.shape)]) + ")")
                    yield tile[at:at + n, :], flat.rearrange("(c p) -> c p", p=P)

            def act(self, act):
                act.dma_start(h[:], a["x"][0].rearrange("(t p) d -> p t d", p=P)).then_inc(self.h_landed, 16)
                for dst, src in self.rows(ROWS_A, rows_a):
                    act.dma_start(dst, src).then_inc(self.rows_landed, 16)
                for dst, src in self.loads():
                    act.dma_start(dst, src, allow_slow_non_contiguous=dst.dtype == I32).then_inc(small_landed, 16)
                act.wait_ge(self.h_landed, 16)
                act.wait_ge(self.turned, 1)
                act.copy(cols_a[:, 0:N_ROWS_A], ps[:, 4, 0:N_ROWS_A])
                stage_end(act)

            def act_rest(self, act):
                act.wait_ge(self.turned, 3)
                act.copy(wsT[:, 0:4], ps[:, 0, :].rearrange("p (h n) -> p h n", h=4))
                act.copy(wsT[:, 4:8], ps[:, 1, :].rearrange("p (h n) -> p h n", h=4))
                act.wait_ge(self.turned, 5)
                for layer in range(2):
                    act.copy(pT[:, layer], ps[:, 2 + layer, :].rearrange("p (c s) -> p c s", c=2))
                act.wait_ge(self.turned, 6)
                act.copy(cols_b[:, 0:N_ROWS_B], ps[:, 5, 0:N_ROWS_B]).then_inc(self.cols, 1)
                act.wait_ge(self.cols, 1)
                act.activation(c_act[:], col("c_2", 0, KC), ACT.Tanh, scale=0.5)
                act.wait_ge(self.turned, 7)
                act.copy(w_dw[:], ps[:, 6, 0:KC * TAPS].rearrange("p (c j) -> p c j", c=KC))
                stage_end(act)

            def pool(self, pool):
                own = Own(pool, self.own_consts)
                pool.memset(ones[:], 1.0)
                pool.memset(mean_w[:], 1.0 / D)
                pool.memset(cmask[:], 0.0)
                pool.iota(rev_i[:], pattern=[[-1, EXPERTS]], base=EXPERTS, channel_multiplier=0)
                pool.iota(places_i[:], pattern=[[1, PLACES]], base=0, channel_multiplier=0)
                pool.memset(ms[:], 0.0)
                own(pool.memset(ident[:], 0.0))
                own(pool.affine_select(out=ident[:], in_=ident[:], compare_op=ALU.not_equal, fill=1.0, base=0,
                                       pattern=[[-1, P]], channel_multiplier=1))
                own(pool.affine_select(out=upper[:], in_=ones[:], compare_op=ALU.is_ge, fill=0.0, base=0,
                                       pattern=[[1, P]], channel_multiplier=-1))
                for at in (0, 2 * P):
                    own(pool.affine_select(out=cmask[:, at:at + P], in_=cmask[:, at:at + P], compare_op=ALU.is_ge,
                                           fill=NEG, base=0, pattern=[[-1, P]], channel_multiplier=1))
                pool.tensor_copy(places[:], places_i[:])
                pool.tensor_copy(rev[:], rev_i[:]).then_inc(self.consts, 1)
                stage_end(pool)

            def pe(self, pe):
                pe.wait_ge(self.consts, 1)
                pe.wait_ge(self.rows_landed, 16 * len(ROWS_A))
                pe.transpose(ps[:, 4, 0:N_ROWS_A], rows_a[0:N_ROWS_A, :], ident[0:N_ROWS_A, 0:N_ROWS_A]).then_inc(self.turned, 1)
                stage_end(pe)

            def pe_rest(self, pe):
                pe.wait_ge(small_landed, SMALL_LANDED)
                for hd in range(GM_HEADS):
                    last = pe.transpose(ps[:, hd // 4, (hd % 4) * P:(hd % 4 + 1) * P], ws_rows[:, hd], ident[:])
                    if hd % 4 == 3:
                        last.then_inc(self.turned, 1)
                for layer in range(2):
                    for c in range(2):
                        for t in range(T):
                            last = pe.transpose(ps[:, 2 + layer, c * S + t * P:c * S + (t + 1) * P],
                                                p_rows[:, layer, t, c * P:(c + 1) * P], ident[:])
                    last.then_inc(self.turned, 1)
                pe.transpose(ps[:, 5, 0:N_ROWS_B], rows_b[0:N_ROWS_B, :], ident[0:N_ROWS_B, 0:N_ROWS_B]).then_inc(self.turned, 1)
                for c in range(KC):
                    last = pe.transpose(ps[:, 6, c * TAPS:(c + 1) * TAPS], dw_rows[:, c * P:(c + 1) * P],
                                        ident[0:TAPS, 0:TAPS])
                last.then_inc(self.turned, 1)
                stage_end(pe)

            def dve_rest(self, dve, own):
                stage_end(dve)
                own(dve.tensor_tensor(wsT[:], wsT[:], upper[:].unsqueeze(1).to_broadcast([P, GM_HEADS, P]), ALU.mult))
                own(dve.scalar_tensor_tensor(out=c_act[:], in0=c_act[:], scalar=1.0, in1=col("c_2", 0, KC), op0=ALU.add,
                                             op1=ALU.mult))
                own(dve.tensor_scalar(c_act[:], c_act[:], 0.5, None, ALU.mult))

        class EvenStage:
            def __init__(self):
                self.v_copied = sem("ev_v_copied")
                self.u_copied = sem("ev_u_copied")
                self.x_copied = sem("ev_x_copied")
                self.v_tanh_in = sem("ev_v_tanh_in")
                self.v_tanh = sem("ev_v_tanh")
                self.u_tanh_in = sem("ev_u_tanh_in")
                self.u_tanh = sem("ev_u_tanh")
                self.vn = sem("ev_vn")
                self.mixed = sem("ev_mixed")
                self.y_b = sem("ev_y_b")
                self.y_turned = sem("ev_y_turned")
                self.mixT_ready = sem("ev_mixT_ready")
                self.mix_hi = sem("ev_mix_hi")
                self.mix_split = sem("ev_mix_split")

            def pe(self, pe):
                for i in range(2):
                    tokens_by_columns(pe, "ev_in", i, (2 * i, 2 * i + 1))
                for i in range(3):
                    if i == 2:
                        pe.wait_ge(self.v_copied, 1)
                    for f in range(4):
                        at = ps[:, (4, 6, 0)[i] + f // 2, (f % 2) * S:(f % 2 + 1) * S]
                        columns_by_tokens(pe, at, halves(pe, "ev_in", 2 + i, f)).then_inc(pieces_used, 1)
                pe.wait_ge(self.vn, 1)
                pe.wait_ge(self.u_copied, 1)
                for t in range(T):
                    for hd in range(GM_HEADS):
                        last = pe.matmul(ps[:, 2 + t, hd * GM_HD:(hd + 1) * GM_HD], wsT[:, hd, :],
                                         gm_v[:, t, hd * GM_HD:(hd + 1) * GM_HD], start=True, stop=True)
                last.then_inc(self.mixed, 1)
                pe.wait_ge(self.y_b, 1)
                for c in range(4):
                    for t in range(T):
                        at = (c % 2) * S + t * P
                        last = pe.transpose(ps[:, 4 + c // 2, at:at + P], gm_s[:, t, c * P:(c + 1) * P], ident[:])
                last.then_inc(self.y_turned, 1)
                pe.wait_ge(self.mix_split, 2)
                for i in range(2):
                    tokens_by_columns(pe, "ev_out", i, (6 - 2 * i, 7 - 2 * i))

            def act(self, act):
                split_upto(act, split_hi, "ev_in", 0, 3)
                wait_used(act, "ev_in", 0, 3)
                act.copy(gm_v[:], ps[:, 0:2, :]).then_inc(self.v_copied, 1)
                split_upto(act, split_hi, "ev_in", 1, 3)
                wait_used(act, "ev_in", 1, 3)
                act.copy(gm_u[:], ps[:, 2:4, :]).then_inc(self.u_copied, 1)
                split_upto(act, split_hi, "ev_in", 2, 3)
                act.wait_ge(self.v_tanh_in, 1)
                act.activation(gm_t[:], gm_t[:], ACT.Tanh, scale=0.7978845608028654).then_inc(self.v_tanh, 1)
                split_upto(act, split_hi, "ev_in", 3, 3)
                wait_used(act, "ev_in", 3, 3)
                act.copy(ev_x[:], ps[:, 6:8, :].rearrange("p b (c s) -> p (b c) s", c=2)).then_inc(self.x_copied, 1)
                act.wait_ge(self.u_tanh_in, 1)
                act.activation(gm_s[:], gm_s[:], ACT.Tanh, scale=0.7978845608028654).then_inc(self.u_tanh, 1)
                split_upto(act, split_hi, "ev_out", 0, 2, ahead=0)
                act.wait_ge(self.mixT_ready, 1)
                act.copy(xT_hi[:, 0:4, :], mixT[:, 0:4, :]).then_inc(self.mix_hi, 1)
                act.wait_ge(self.y_turned, 1)
                act.copy(xT_hi[:, 4:8, :], ps[:, 4:6, :].rearrange("p b (c s) -> p (b c) s", c=2)).then_inc(self.mix_hi, 1)
                split_upto(act, split_hi, "ev_out", 1, 3)

            def dve(self, dve, own):
                def gelu_in(x, t, done):
                    own(dve.tensor_tensor(t, x, x, ALU.mult))
                    own(dve.tensor_scalar(t, t, 0.044715, 1.0, ALU.mult, ALU.add))
                    dve.tensor_tensor(t, t, x, ALU.mult).then_inc(done, 1)

                own(dve.memset(ev_z[:, :, 0:2], 0.0))
                split_upto(dve, split_lo, "ev_in", 0, 3)
                dve.wait_ge(self.v_copied, 1)
                gelu_in(gm_v[:], gm_t[:], self.v_tanh_in)
                split_upto(dve, split_lo, "ev_in", 1, 3)
                dve.wait_ge(self.u_copied, 1)
                gelu_in(gm_u[:], gm_s[:], self.u_tanh_in)
                split_upto(dve, split_lo, "ev_in", 2, 1)
                dve.wait_ge(self.v_tanh, 1)
                own(dve.scalar_tensor_tensor(out=gm_v[:], in0=gm_t[:], scalar=1.0, in1=gm_v[:], op0=ALU.add, op1=ALU.mult))
                own(dve.tensor_tensor(gm_t[:], gm_v[:], gm_v[:], ALU.mult))
                n = T * GM_HEADS
                split_upto(dve, split_lo, "ev_in", 2, 3)
                own(dve.tensor_reduce(ms[:, 0:n], gm_t[:].rearrange("p t (h d) -> p (t h) d", d=GM_HD), AX.X, ALU.add))
                own(dve.tensor_scalar(ms[:, 0:n], ms[:, 0:n], 0.25 / GM_HD, None, ALU.mult))
                rsqrt_ms(dve, own, n)
                own(dve.tensor_scalar(rs[:, 0:n], rs[:, 0:n], 0.5, None, ALU.mult))
                split_upto(dve, split_lo, "ev_in", 3, 1)
                v3 = gm_v[:].rearrange("p t (h d) -> p (t h) d", d=GM_HD)
                own(dve.tensor_tensor(v3, v3, rs[:, 0:n].unsqueeze(2).to_broadcast([P, n, GM_HD]), ALU.mult))
                dve.tensor_tensor(gm_v[:], gm_v[:], g_v[:].unsqueeze(1).to_broadcast([P, T, 512]),
                                  ALU.mult).then_inc(self.vn, 1)
                split_upto(dve, split_lo, "ev_in", 3, 3)
                dve.wait_ge(self.u_tanh, 1)
                own(dve.scalar_tensor_tensor(out=gm_u[:], in0=gm_s[:], scalar=1.0, in1=gm_u[:], op0=ALU.add, op1=ALU.mult))
                dve.wait_ge(self.x_copied, 1)
                own(dve.tensor_tensor(ev_z[:, :, 2:], ps[:, 4:6, :].rearrange("p b (c s) -> p (b c) s", c=2), ev_x[:],
                                      ALU.mult))
                for j in range(3):
                    for c in range(4):
                        w = col("ev_w_conv", 4 * j + c)
                        if j == 0:
                            own(dve.tensor_scalar(ev_y[:, c], ev_z[:, c, 0:S], w, None, ALU.mult))
                        else:
                            own(dve.scalar_tensor_tensor(out=ev_y[:, c], in0=ev_z[:, c, j:j + S], scalar=w,
                                                         in1=ev_y[:, c], op0=ALU.mult, op1=ALU.add))
                split_upto(dve, split_lo, "ev_out", 0, 2, ahead=0)
                wait_used(dve, "ev_in", 4, 3)
                dve.tensor_tensor(mixT[:, 0:4, :], ps[:, 0:2, :].rearrange("p b (c s) -> p (b c) s", c=2), ev_y[:],
                                  ALU.mult).then_inc(self.mixT_ready, 1)
                dve.wait_ge(self.mixed, 1)
                bias = col("ev_b_s", 0, GM_HEADS).unsqueeze(2).to_broadcast([P, GM_HEADS, GM_HD])
                for t in range(T):
                    own(dve.tensor_tensor(gm_t[:, t].rearrange("p (h d) -> p h d", d=GM_HD),
                                          ps[:, 2 + t, :].rearrange("p (h d) -> p h d", d=GM_HD), bias, ALU.add))
                dve.scalar_tensor_tensor(out=gm_s[:], in0=gm_t[:], scalar=0.5, in1=gm_u[:], op0=ALU.mult,
                                         op1=ALU.mult).then_inc(self.y_b, 1)
                dve.wait_ge(self.mix_hi, 1)
                dve.tensor_tensor(xT_lo[:, 0:4], mixT[:, 0:4], xT_hi[:, 0:4].bitcast(F32), ALU.subtract).then_inc(self.mix_split, 1)
                dve.wait_ge(self.mix_hi, 2)
                dve.tensor_tensor(xT_lo[:, 4:8], ps[:, 4:6, :].rearrange("p b (c s) -> p (b c) s", c=2),
                                  xT_hi[:, 4:8].bitcast(F32), ALU.subtract).then_inc(self.mix_split, 1)
                for i in range(2):
                    split_upto(dve, split_lo, "ev_out", i, 3)
                    wait_used(dve, "ev_out", i, 3)
                    for t in range(T):
                        o = h[:, t, i * 512:(i + 1) * 512]
                        ins = dve.tensor_tensor(o, o, ps[:, 6 - 2 * i + t, :], ALU.add)
                    ins.then_inc(h_ready, 1)

        class OddIn:
            def __init__(self, norm):
                self.norm = norm
                self.copied = [sem(f"od_z_copied{t}") for t in range(T)]

            def pe(self, pe):
                for i in range(5):
                    if i == 4:
                        for t in range(T):
                            pe.wait_ge(self.copied[t], 1)
                    tokens_by_columns(pe, "od_in", i, [(2 * i + t) % 8 for t in range(T)], width("od_in", i),
                                      self.norm if i == 0 else None)
                stage_end(pe)

            def act(self, act):
                split_upto(act, split_hi, "od_in", 0, 2, ahead=0)
                self.norm.wait_factors(act)
                for i in range(5):
                    n = width("od_in", i)
                    split_upto(act, split_hi, "od_in", i, 3)
                    wait_used(act, "od_in", i, 3)
                    act.activation(od_z[:, 0, 512 * i:512 * i + n], ps[:, (2 * i) % 8, 0:n], ACT.Copy, scale=rstd[:, 0, 0:1]
                                   ).then_inc(self.copied[0], 1)
                stage_end(act)

            def dve(self, dve, own):
                for i in range(5):
                    n = width("od_in", i)
                    split_upto(dve, split_lo, "od_in", i, 3)
                    wait_used(dve, "od_in", i, 3)
                    dve.tensor_scalar(od_z[:, 1, 512 * i:512 * i + n], ps[:, (2 * i + 1) % 8, 0:n], rstd[:, 0, 1:2], None,
                                      ALU.mult).then_inc(self.copied[1], 1)
                stage_end(dve)

            def pool(self, pool):
                pool.wait_ge(h_ready, 6)
                freq = (np.float32(ROPE_THETA) ** (-np.arange(0, ROPE, 2, dtype=np.float32) / np.float32(ROPE))
                        ).astype(np.float32)
                for i in range(ROPE // 2):
                    pool.memset(inv_freq[:, i:i + 1], float(freq[i]))
                stage_end(pool)

        class OddUp:
            def __init__(self):
                self.squares = sem("od_squares")
                self.rstd = sem("od_rstd")
                self.lat = sem("od_lat")
                self.lat_turned = sem("od_lat_turned")
                self.latT = sem("od_latT")
                self.mqk_turned = sem("od_mqk_turned")
                self.mqk_freed = sem("od_mqk_freed")
                self.angles = sem("od_angles")
                self.trig = sem("od_trig")

            def act(self, act):
                for kind, (at, n) in enumerate(((0, Q_LORA), (Q_LORA, KV_LORA), (AT_KPE, ROPE))):
                    for t in range(T):
                        last = act.activation(xn[:, t, at:at + n], od_z[:, t, at:at + n], ACT.Square, scale=float(n) ** -0.5,
                                              accum_out=ms[:, kind * T + t:kind * T + t + 1])
                last.then_inc(self.squares, 1)
                act.wait_ge(self.rstd, 1)
                for t in range(T):
                    act.activation(lat[:, t, 0:Q_LORA], od_z[:, t, 0:Q_LORA], ACT.Copy,
                                   scale=rs[:, t:t + 1]).then_inc(self.lat, 1)
                act.wait_ge(self.lat_turned, 1)
                for c in range(5):
                    gain = col("od_g_qa", c) if c < 3 else col("od_g_kva", c - 3)
                    last = act.activation(latT[:, c, :], ps[:, c // 2, (c % 2) * S:(c % 2 + 1) * S], ACT.Copy, scale=gain)
                last.then_inc(self.latT, 1)
                act.wait_ge(self.mqk_turned, 1)
                act.copy(mqkT[:], ps[:, 3:5, :].rearrange("p b (c s) -> p (b c) s", c=2)).then_inc(self.mqk_freed, 1)
                act.wait_ge(self.angles, 1)
                act.activation(cs[:], cs[:], ACT.Sin).then_inc(self.trig, 1)
                act.wait_ge(up_used, 1)
                act.copy(od_q[:].rearrange("p t h d -> p t (h d)").rearrange("p t (a b) -> p (t a) b", a=2),
                         ps[:, 0:4, 0:384])
                act.copy(od_kv[:].rearrange("p t h d -> p t (h d)").rearrange("p t (a b) -> p (t a) b", a=2),
                         ps[:, 4:8, :])
                stage_end(act)

            def dve(self, dve, own):
                own(dve.tensor_copy(posf[:], pos_i[:]))
                for t in range(T):
                    own(dve.tensor_scalar(ang[:, t], inv_freq[:], posf[:, t:t + 1], None, ALU.mult))
                first_part = 6.25
                second_part = np.floor((2 * np.pi - first_part) * 2.0 ** 19) / 2.0 ** 19
                parts = [first_part, second_part, 2 * np.pi - first_part - second_part]
                big = 1.5 * 2.0 ** 23
                for k, quarter in ((0, 0.25), (1, 0.0)):
                    own(dve.tensor_scalar(turns[:], ang[:], float(1 / (2 * np.pi)), quarter, ALU.mult, ALU.add))
                    own(dve.tensor_scalar(turns[:], turns[:], big, None, ALU.add))
                    own(dve.tensor_scalar(turns[:], turns[:], big, None, ALU.subtract))
                    own(dve.scalar_tensor_tensor(out=cs[:, k], in0=turns[:], scalar=-float(parts[0]), in1=ang[:],
                                                 op0=ALU.mult, op1=ALU.add))
                    for part in parts[1:]:
                        own(dve.scalar_tensor_tensor(out=cs[:, k], in0=turns[:], scalar=-float(part), in1=cs[:, k],
                                                     op0=ALU.mult, op1=ALU.add))
                    if quarter:
                        own(dve.tensor_scalar(cs[:, k], cs[:, k], float(np.pi / 2), None, ALU.add))
                    last = dve.tensor_scalar(cs[:, k], cs[:, k], 3.1415925, -3.1415925, ALU.min, ALU.max)
                    if k == 0:
                        own(last)
                last.then_inc(self.angles, 1)
                dve.wait_ge(self.squares, 1)
                rsqrt_ms(dve, own, 3 * T, self.rstd)
                dve.wait_ge(self.rstd, 1)
                for t in range(T):
                    dve.tensor_scalar(lat[:, t, Q_LORA:], od_z[:, t, Q_LORA:AT_KPE], rs[:, T + t:T + t + 1], None,
                                      ALU.mult).then_inc(self.lat, 1)
                for t in range(T):
                    kp = od_z[:, t, AT_KPE:AT_KPE + ROPE]
                    own(dve.scalar_tensor_tensor(out=kp, in0=kp, scalar=rs[:, 2 * T + t:2 * T + t + 1], in1=g_k[:, NOPE:],
                                                 op0=ALU.mult, op1=ALU.mult))
                stage_end(dve)

            def pe(self, pe):
                for c in range(4):
                    for t in range(T):
                        at = (c % 2) * S + t * P
                        last = pe.transpose(ps[:, 3 + c // 2, at:at + P], od_z[:, t, AT_MQ + c * P:AT_MQ + (c + 1) * P],
                                            ident[:])
                last.then_inc(self.mqk_turned, 1)
                pe.wait_ge(self.lat, 2 * T)
                for c in range(5):
                    for t in range(T):
                        at = (c % 2) * S + t * P
                        last = pe.transpose(ps[:, c // 2, at:at + P], lat[:, t, c * P:(c + 1) * P], ident[:])
                last.then_inc(self.lat_turned, 1)
                pe.wait_ge(self.latT, 1)
                pe.wait_ge(self.mqk_freed, 1)
                wait_a(pe, "od_up", 0)
                wait_b(pe, "od_up", 0)
                wq = part_a("od_up", 0, 3 * 768).rearrange("p (k n) -> p k n", k=3)
                wkv = part_b("od_up", 0).rearrange("p (k n) -> p k n", k=2)
                for t in range(T):
                    for half_ in range(2):
                        for k in range(3):
                            pe.matmul(ps[:, 2 * t + half_, 0:384], latT[:, k, t * P:(t + 1) * P],
                                      wq[:, k, half_ * 384:(half_ + 1) * 384], start=(k == 0), stop=(k == 2))
                for t in range(T):
                    for half_ in range(2):
                        for k in range(2):
                            last = pe.matmul(ps[:, 4 + 2 * t + half_, :], latT[:, 3 + k, t * P:(t + 1) * P],
                                             wkv[:, k, half_ * 512:(half_ + 1) * 512], start=(k == 0), stop=(k == 1))
                last.then_inc(up_used, 1)
                stage_end(pe)

        class OddHeads:

            def __init__(self):
                self.sq_k = sem("od_sq_k")
                self.q_ready, self.k_ready = sem("od_q_ready"), sem("od_k_ready")
                self.turned, self.exps, self.logs = sem("od_heads_turned"), sem("od_gate_exp"), sem("od_gate_log")
                self.gate_abs = sem("od_gate_abs")

            def dve(self, dve, own):
                n = T * HEADS
                q3 = od_q[:].rearrange("p t h d -> p (t h) d")
                kv3 = od_kv[:].rearrange("p t h d -> p (t h) d")
                k3 = od_k[:].rearrange("p t h d -> p (t h) d")
                sq = xn[:].rearrange("p t d -> p (t d)")[:, 0:n * QK].rearrange("p (n d) -> p n d", d=QK)
                own(dve.tensor_tensor(sq, q3, q3, ALU.mult))
                own(dve.tensor_reduce(ms[:, 0:n], sq[:, :, 0:NOPE], AX.X, ALU.add))
                own(dve.tensor_reduce(ms[:, n:2 * n], sq[:, :, NOPE:], AX.X, ALU.add))
                own(dve.tensor_tensor(sq[:, :, 0:NOPE], kv3[:, :, 0:NOPE], kv3[:, :, 0:NOPE], ALU.mult))
                own(dve.tensor_reduce(ms[:, 2 * n:3 * n], sq[:, :, 0:NOPE], AX.X, ALU.add))
                own(dve.tensor_scalar(ms[:, 0:n], ms[:, 0:n], 1.0 / NOPE, None, ALU.mult))
                own(dve.tensor_scalar(ms[:, n:2 * n], ms[:, n:2 * n], 1.0 / ROPE, None, ALU.mult))
                own(dve.tensor_scalar(ms[:, 2 * n:3 * n], ms[:, 2 * n:3 * n], 1.0 / NOPE, None, ALU.mult))
                rsqrt_ms(dve, own, 3 * n)

                def per_head(x, at, width):
                    return rs[:, at:at + n].unsqueeze(2).to_broadcast([P, n, width])

                own(dve.tensor_tensor(q3[:, :, 0:NOPE], q3[:, :, 0:NOPE], per_head(rs, 0, NOPE), ALU.mult))
                own(dve.tensor_tensor(q3[:, :, NOPE:], q3[:, :, NOPE:], per_head(rs, n, ROPE), ALU.mult))
                own(dve.tensor_tensor(q3, q3, g_q[:].unsqueeze(1).to_broadcast([P, n, QK]), ALU.mult))
                own(dve.tensor_tensor(k3[:, :, 0:NOPE], kv3[:, :, 0:NOPE], per_head(rs, 2 * n, NOPE), ALU.mult))
                own(dve.tensor_tensor(k3[:, :, 0:NOPE], k3[:, :, 0:NOPE],
                                      g_k[:, 0:NOPE].unsqueeze(1).to_broadcast([P, n, NOPE]), ALU.mult))
                hr = ROPE // 2
                for t in range(T):
                    r1 = sq[:, 0:HEADS, 0:hr]
                    r2 = sq[:, 0:HEADS, hr:2 * hr]
                    cos = cs[:, 0, t].unsqueeze(1).to_broadcast([P, HEADS, hr])
                    sin = cs[:, 1, t].unsqueeze(1).to_broadcast([P, HEADS, hr])
                    x1, x2 = od_q[:, t, :, NOPE:NOPE + hr], od_q[:, t, :, NOPE + hr:]
                    own(dve.tensor_tensor(r1, x2, sin, ALU.mult))
                    own(dve.tensor_tensor(r2, x1, sin, ALU.mult))
                    own(dve.tensor_tensor(x1, x1, cos, ALU.mult))
                    own(dve.tensor_tensor(x2, x2, cos, ALU.mult))
                    own(dve.tensor_tensor(x1, x1, r1, ALU.subtract))
                    last = dve.tensor_tensor(x2, x2, r2, ALU.add)
                    last.then_inc(self.q_ready, 1)
                for t in range(T):
                    k1, k2 = od_z[:, t, AT_KPE:AT_KPE + hr], od_z[:, t, AT_KPE + hr:AT_KPE + ROPE]
                    r1, r2 = sq[:, HEADS, 0:hr], sq[:, HEADS, hr:2 * hr]
                    cos, sin = cs[:, 0, t], cs[:, 1, t]
                    own(dve.tensor_tensor(r1, k2, sin, ALU.mult))
                    own(dve.tensor_tensor(r2, k1, sin, ALU.mult))
                    own(dve.tensor_tensor(k1, k1, cos, ALU.mult))
                    own(dve.tensor_tensor(k2, k2, cos, ALU.mult))
                    own(dve.tensor_tensor(k1, k1, r1, ALU.subtract))
                    own(dve.tensor_tensor(k2, k2, r2, ALU.add))
                    dve.tensor_copy(od_k[:, t, :, NOPE:],
                                    od_z[:, t, AT_KPE:AT_KPE + ROPE].unsqueeze(1).to_broadcast([P, HEADS, ROPE])
                                    ).then_inc(self.k_ready, 1)
                own(dve.tensor_tensor(gts[:], od_z[:, :, AT_MI:], b_gate[:].unsqueeze(1).to_broadcast([P, T, 2 * MH]),
                                      ALU.add))
                f = gts[:, :, MH:]
                own(dve.tensor_scalar(lf[:, 2], f, -1.0, None, ALU.mult))
                dve.tensor_tensor(lf[:, 0], f, lf[:, 2], ALU.max).then_inc(self.gate_abs, 1)
                dve.wait_ge(self.logs, 1)
                own(dve.tensor_scalar(lf[:, 2], f, 0.0, None, ALU.min))
                own(dve.tensor_tensor(lf[:, 2], lf[:, 2], lf[:, 1], ALU.subtract))
                for b in range(0, 8, 2):
                    dve.wait_ge(self.turned, b + 1)
                    dst = (qT if b < 4 else kT)[0:QK, 2 * (b % 4):2 * (b % 4) + 2, :]
                    dve.tensor_copy(dst, ps[0:QK, b, :].rearrange("p (h s) -> p h s", h=2))
                stage_end(dve)

            def act(self, act):
                act.wait_ge(self.gate_abs, 1)
                act.activation(lf[:, 0], lf[:, 0], ACT.Exp, scale=-1.0).then_inc(self.exps, 1)
                act.wait_ge(self.exps, 1)
                act.activation(lf[:, 1], lf[:, 0], ACT.Ln, bias=1.0).then_inc(self.logs, 1)
                for b in range(1, 8, 2):
                    act.wait_ge(self.turned, b + 1)
                    dst = (qT if b < 4 else kT)[0:QK, 2 * (b % 4):2 * (b % 4) + 2, :]
                    act.copy(dst, ps[0:QK, b, :].rearrange("p (h s) -> p h s", h=2))
                stage_end(act)

            def pe(self, pe):
                for b in range(8):
                    ready, src = (self.q_ready, od_q) if b < 4 else (self.k_ready, od_k)
                    if b % 4 == 0:
                        pe.wait_ge(ready, T)
                    for hd in range(2):
                        for t in range(T):
                            at = hd * S + t * P
                            last = pe.transpose(ps[0:QK, b, at:at + P], src[:, t, 2 * (b % 4) + hd, :], ident[:])
                    last.then_inc(self.turned, 1)
                stage_end(pe)

        class OddAttend:

            def __init__(self):
                self.cum = sem("oa_cum")
                self.diag = sem("oa_diag")
                self.rows = sem("oa_rows")
                self.rows_freed = sem("oa_rows_freed")
                self.scores = sem("oa_scores")
                self.masked = sem("oa_masked")
                self.prob = sem("oa_prob")
                self.turned = sem("oa_turned")
                self.probT = sem("oa_probT")
                self.valued = sem("oa_valued")
                self.nm = sem("oa_nm")
                self.w_mem = sem("oa_w_mem")
                self.mx = sem("oa_mx")
                self.v_aug_ready = sem("oa_v_aug_ready")
                self.y_freed = sem("oa_y_freed")

            N = HEADS + MH

            def pe(self, pe):
                for t in range(T):
                    o = ps[:, 5, t * MH:(t + 1) * MH]
                    if t:
                        pe.matmul(o, ones[:], lf[:, 2, 0], start=True, stop=False)
                    last = pe.matmul(o, upper[:], lf[:, 2, t], start=(t == 0), stop=True)
                last.then_inc(self.cum, 1)
                pe.wait_ge(self.diag, T)
                for t in range(T):
                    last = pe.matmul(ps[:, 3 + t, :], ones[:], diag_b[:, t], start=True, stop=True)
                last.then_inc(self.rows, 1)

                def scores(hd):
                    if hd >= 3:
                        pe.wait_ge(self.masked, hd - 2)
                    if hd < HEADS:
                        q, k = qT[0:QK, hd, :], kT[0:QK, hd, :]
                    else:
                        m = hd - HEADS
                        rows = slice((m % 2) * MQK, (m % 2 + 1) * MQK)
                        q, k = mqkT[rows, m // 2, :], mqkT[rows, 2 + m // 2, :]
                    pe.matmul(ps[:, hd % 3, 0:P], q[:, 0:P], k[:, 0:P], start=True, stop=True)
                    pe.matmul(ps[:, hd % 3, P:3 * P], q[:, P:S], k, start=True, stop=True).then_inc(self.scores, 1)

                def turn(hd):
                    if hd == 0:
                        pe.wait_ge(self.rows_freed, 1)
                    if hd < HEADS:
                        pe.wait_ge(self.prob, hd + 1)
                    else:
                        pe.wait_ge(self.masked, hd + 1)
                    if hd >= 2:
                        pe.wait_ge(self.probT, hd - 1)
                    for j in range(3):
                        last = pe.transpose(ps[:, 3 + hd % 2, j * P:(j + 1) * P], prob[:, hd % 2, j * P:(j + 1) * P], ident[:])
                    last.then_inc(self.turned, 1)

                def values(hd):
                    pe.wait_ge(self.probT, hd + 1)
                    if hd == HEADS:
                        pe.wait_ge(self.v_aug_ready, 1)
                        pe.wait_ge(self.y_freed, T)
                    elif hd > HEADS + 1:
                        pe.wait_ge(self.y_freed, T + hd - HEADS - 1)
                    for t in range(T):
                        for j in range(t + 1):
                            w = probT[:, hd % 2, (t + j) * P:(t + j + 1) * P]
                            if hd < HEADS:
                                o, v = ps[:, 6 + t, hd * VD:(hd + 1) * VD], od_kv[:, j, hd, NOPE:]
                            else:
                                m = hd - HEADS
                                o = ps[:, 6 + m % 2, t * (MV + 1):(t + 1) * (MV + 1)]
                                v = v_aug[:, j, m, :]
                            last = pe.matmul(o, w, v, start=(j == 0), stop=(j == t))
                    last.then_inc(self.valued, 1)

                for step in range(self.N + 2):
                    if step < self.N:
                        scores(step)
                    if 1 <= step <= self.N:
                        turn(step - 1)
                    if step >= 2:
                        values(step - 2)
                stage_end(pe)

            def act(self, act):
                def copy(hd):
                    act.wait_ge(self.turned, hd + 1)
                    if hd >= 2:
                        act.wait_ge(self.valued, hd - 1)
                    act.copy(probT[:, hd % 2], ps[:, 3 + hd % 2, 0:3 * P]).then_inc(self.probT, 1)

                act.wait_ge(self.mx, 1)
                for m in range(MH):
                    for t in range(T):
                        b = b_masked[:, m, 0:P] if t == 0 else b_masked[:, m, P:3 * P]
                        act.activation(b, b, ACT.Exp, bias=nmax[:, HEADS + m, t:t + 1])
                act.activation(emt[:], emt[:], ACT.Exp, scale=-1.0).then_inc(self.w_mem, 1)
                for hd in range(HEADS):
                    act.wait_ge(self.nm, hd + 1)
                    if hd >= 2:
                        act.wait_ge(self.turned, hd - 1)
                    for t in range(T):
                        cut = slice(0, P) if t == 0 else slice(P, 3 * P)
                        last = act.activation(prob[:, hd % 2, cut], sm[:, hd % 2, cut], ACT.Exp,
                                              bias=nmax[:, hd, t:t + 1], accum_out=rsum[:, t, hd:hd + 1])
                    last.then_inc(self.prob, 1)
                    copy(hd)
                for hd in range(HEADS, self.N):
                    copy(hd)
                stage_end(act)

            def dve(self, dve, own):
                dve.wait_ge(self.cum, 1)
                own(dve.tensor_copy(acum[:], ps[:, 5, 0:T * MH].rearrange("p (t h) -> p t h", t=T)))
                own(dve.tensor_tensor(bcol[:], gts[:, :, 0:MH], acum[:], ALU.subtract))

                def masked(hd):
                    dve.wait_ge(self.scores, hd + 1)
                    if hd < HEADS:
                        if hd >= 2:
                            dve.wait_ge(self.prob, hd - 1)
                        ins = dve.scalar_tensor_tensor(out=sm[:, hd % 2], in0=ps[:, hd % 3, 0:3 * P], scalar=float(QK) ** -0.5,
                                                       in1=cmask[:], op0=ALU.mult, op1=ALU.add)
                        ins.then_inc(self.masked, 1)
                        dve.wait_ge(self.masked, hd + 1)
                        dve.tensor_reduce(nmax[:, hd, 0:1], sm[:, hd % 2, 0:P], AX.X, ALU.max, negate=True)
                        dve.tensor_reduce(nmax[:, hd, 1:2], sm[:, hd % 2, P:3 * P], AX.X, ALU.max,
                                          negate=True).then_inc(self.nm, 1)
                    else:
                        m = hd - HEADS
                        if m == 0:
                            dve.wait_ge(self.w_mem, 1)
                        dve.wait_ge(self.turned, hd - 1)
                        ins = dve.scalar_tensor_tensor(out=prob[:, hd % 2], in0=ps[:, hd % 3, 0:3 * P],
                                                       scalar=float(MQK) ** -0.5, in1=b_masked[:, m, :],
                                                       op0=ALU.mult, op1=ALU.mult)
                        ins.then_inc(self.masked, 1)

                for t in range(T):
                    dve.tensor_tensor(diag_b[:, t], ident[:].unsqueeze(1).to_broadcast([P, MH, P]),
                                      bcol[:, t].unsqueeze(2).to_broadcast([P, MH, P]), ALU.mult).then_inc(self.diag, 1)
                dve.wait_ge(self.rows, 1)
                tri = cmask[:, 0:P].unsqueeze(1).to_broadcast([P, MH, P])
                row = [ps[:, 3 + t, :].rearrange("p (h n) -> p h n", h=MH) for t in range(T)]
                own(dve.tensor_tensor(b_masked[:, :, 0:P], row[0], tri, ALU.add))
                own(dve.tensor_copy(b_masked[:, :, P:2 * P], row[0]))
                dve.tensor_tensor(b_masked[:, :, 2 * P:3 * P], row[1], tri, ALU.add).then_inc(self.rows_freed, 1)
                dve.wait_ge(self.rows_freed, 1)
                top = nmax[:, HEADS:, :].rearrange("p h t -> p t h")
                own(dve.tensor_reduce(nmax[:, HEADS:, 0:1], b_masked[:, :, 0:P], AX.X, ALU.max))
                own(dve.tensor_reduce(nmax[:, HEADS:, 1:2], b_masked[:, :, P:3 * P], AX.X, ALU.max))
                own(dve.tensor_scalar(nmax[:, HEADS:, :], nmax[:, HEADS:, :], 0.0, None, ALU.max))
                own(dve.tensor_tensor(emt[:], acum[:], top, ALU.add))
                dve.tensor_scalar(nmax[:, HEADS:, :], nmax[:, HEADS:, :], -1.0, None, ALU.mult).then_inc(self.mx, 1)
                own(dve.memset(v_aug[:, :, :, MV:], 1.0))
                dve.tensor_copy(v_aug[:, :, :, 0:MV], od_z[:, :, AT_MV:AT_MO].rearrange("p t (h d) -> p t h d", h=MH)
                                ).then_inc(self.v_aug_ready, 1)
                for hd in range(self.N):
                    masked(hd)
                    if hd == HEADS + 1:
                        dve.wait_ge(self.valued, HEADS)
                        own(dve.reciprocal(rsum[:], rsum[:]))
                        for t in range(T):
                            dve.tensor_tensor(mix[:, t, 0:HEADS * VD].rearrange("p (h d) -> p h d", h=HEADS),
                                              ps[:, 6 + t, :].rearrange("p (h d) -> p h d", h=HEADS),
                                              rsum[:, t].unsqueeze(2).to_broadcast([P, HEADS, VD]),
                                              ALU.mult).then_inc(self.y_freed, 1)
                for m in range(MH):
                    dve.wait_ge(self.valued, HEADS + m + 1)
                    dve.wait_ge(self.y_freed, T + m)
                    num = ps[:, 6 + m % 2, 0:T * (MV + 1)].rearrange("p (t d) -> p t d", t=T)
                    own(dve.tensor_copy(den[:, 0], num[:, :, MV]))
                    own(dve.tensor_scalar(den[:, 1], den[:, 0], -1.0, None, ALU.mult))
                    own(dve.tensor_tensor(den[:, 0], den[:, 0], den[:, 1], ALU.max))
                    own(dve.tensor_tensor(den[:, 0], den[:, 0], emt[:, :, m], ALU.max))
                    own(dve.reciprocal(den[:, 0], den[:, 0]))
                    dve.tensor_tensor(y_d[:, :, m, :], num[:, :, 0:MV], den[:, 0].unsqueeze(2).to_broadcast([P, T, MV]),
                                      ALU.mult).then_inc(self.y_freed, 1)
                stage_end(dve)

        class OddOut:
            def __init__(self):
                self.tanh, self.y, self.turned, self.hi, self.lo = (sem("oo_" + n) for n in ("tanh", "y", "turned", "hi", "lo"))

            def act(self, act):
                mo = od_z[:, :, AT_MO:AT_MI]
                act.activation(od_z[:, :, AT_MV:AT_MO], mo, ACT.Tanh, scale=0.5).then_inc(self.tanh, 1)
                split_upto(act, split_hi, "od_out", 0, 3, ahead=0)
                for b in range(4):
                    act.wait_ge(self.turned, b + 1)
                    act.copy(xT_hi[:, 2 * b:2 * b + 2, :], ps[:, b, :].rearrange("p (c s) -> p c s", c=2)).then_inc(self.hi, 1)
                split_upto(act, split_hi, "od_out", 1, 3)

            def dve(self, dve, own):
                n = T * MH
                sq = od_kv[:].rearrange("p t h d -> p t (h d)")[:, :, 0:MH * MV].rearrange("p t (h d) -> p t h d", h=MH)
                own(dve.tensor_tensor(sq, y_d, y_d, ALU.mult))
                own(dve.tensor_reduce(ms[:, 0:n].rearrange("p (t h) -> p t h", t=T), sq, AX.X, ALU.add))
                own(dve.tensor_scalar(ms[:, 0:n], ms[:, 0:n], 1.0 / MV, None, ALU.mult))
                rsqrt_ms(dve, own, n)
                own(dve.tensor_scalar(rs[:, 0:n], rs[:, 0:n], 0.5, None, ALU.mult))
                for t in range(T):
                    own(dve.tensor_tensor(y_d[:, t], y_d[:, t],
                                          rs[:, t * MH:(t + 1) * MH].unsqueeze(2).to_broadcast([P, MH, MV]), ALU.mult))
                flat = mix[:, :, HEADS * VD:]
                own(dve.tensor_tensor(flat, flat, g_mh[:].unsqueeze(1).to_broadcast([P, T, MH * MV]), ALU.mult))
                dve.wait_ge(self.tanh, 1)
                dve.scalar_tensor_tensor(out=flat, in0=od_z[:, :, AT_MV:AT_MO], scalar=1.0, in1=flat, op0=ALU.add,
                                         op1=ALU.mult).then_inc(self.y, 1)
                split_upto(dve, split_lo, "od_out", 0, 3, ahead=0)
                for b in range(4):
                    dve.wait_ge(self.hi, b + 1)
                    dve.tensor_tensor(xT_lo[:, 2 * b:2 * b + 2, :], ps[:, b, :].rearrange("p (c s) -> p c s", c=2),
                                      xT_hi[:, 2 * b:2 * b + 2, :].bitcast(F32), ALU.subtract).then_inc(self.lo, 1)
                for i in range(2):
                    split_upto(dve, split_lo, "od_out", i, 3)
                    wait_used(dve, "od_out", i, 3)
                    for t in range(T):
                        o = h[:, t, i * 512:(i + 1) * 512]
                        ins = dve.tensor_tensor(o, o, ps[:, 4 + 2 * i + t, :], ALU.add)
                    ins.then_inc(h_ready, 1)

            def pe(self, pe):
                for b in range(4):
                    if b == 2:
                        pe.wait_ge(self.y, 1)
                    for c in (2 * b, 2 * b + 1):
                        for t in range(T):
                            at = (c % 2) * S + t * P
                            last = pe.transpose(ps[:, b, at:at + P], mix[:, t, c * P:(c + 1) * P], ident[:])
                    last.then_inc(self.turned, 1)
                pe.wait_ge(self.lo, 4)
                for i in range(2):
                    tokens_by_columns(pe, "od_out", i, (4 + 2 * i, 5 + 2 * i))

        ADA_ITEMS = 2 * 6 * D // BLK
        HALF_ROWS = KC // 2
        ada_steps = sem("ada_steps")

        def ada_loads(pool):
            w = a["ada_w_2"][0].rearrange("(s k p) n -> p s k n", p=P, s=2)

            def load(q, it):
                cut = bass.ds(per_round(q % 2 * BLK, it, 2 * BLK), BLK)
                pool.dma_start(ada_w[:, q], w[:, q // 2, :, cut]).then_inc(ada_landed[q], 16)

            pool.wait_ge(h_ready, 8)
            for q in range(ADA_BUFFERS):
                load(q, None)
            with pool.Fori(1, ADA_ITEMS // ADA_BUFFERS) as it:
                for q in range(ADA_BUFFERS):
                    pool.wait_ge(ada_used, ADA_BUFFERS * it + q // 2 * 2 - 2)
                    load(q, it)

        def ada_products(dve, block, it):
            groups = (block + 1,) if block >= 2 else (0,) if block == 0 else (1, 2)
            for j in groups:
                for second in range(2):
                    for q in range(2):
                        buffer = 2 * second + q
                        dve.wait_ge(ada_landed[buffer], per_round(16 * (j + 1), it, 16 * FF_ROUND))
                    if second:
                        dve.wait_ge(ada_used, per_round(4 * j + 2, it, 4 * FF_ROUND))
                    steps = 4 * (HALF_ROWS - 1) * j + 2 * (HALF_ROWS - 1) * second
                    for k in range(HALF_ROWS):
                        for q in range(2):
                            acc = ada_acc[:, bass.ds(per_round((2 * j + q) * BLK, it, 2 * FF_ROUND * BLK), BLK)]
                            c = second * HALF_ROWS + k
                            w, c_col = ada_w[:, 2 * second + q, k], c_act[:, c:c + 1]
                            if c == 0:
                                ins = dve.tensor_scalar(acc, w, c_col, None, ALU.mult)
                            else:
                                if k > 0:
                                    dve.wait_ge(ada_steps, per_round(steps + 2 * (k - 1) + q + 1, it,
                                                                     4 * (HALF_ROWS - 1) * FF_ROUND))
                                ins = dve.scalar_tensor_tensor(out=acc, in0=w, scalar=c_col, in1=acc, op0=ALU.mult, op1=ALU.add)
                            ins.then_inc(ada_steps if k < HALF_ROWS - 1 else ada_used, 1)

        class ModStage:
            COLS, ROWS = (0, 1, 3, 4), (2, 5)

            def __init__(self):
                self.summed = sem("mod_summed")
                self.b_landed = sem("mod_b_landed")

            def load(self, act):
                for i, v in enumerate(self.ROWS):
                    act.dma_start(g_bc[:, i], a["ada_b_2"][0, v * D:(v + 1) * D].partition_broadcast(P)
                                  ).then_inc(self.b_landed, 16)

            def pe(self, pe):
                pe.wait_ge(h_ready, 12)
                pe.wait_ge(ada_used, ADA_ITEMS)
                for i, v in enumerate(self.COLS):
                    for c in range(KC):
                        pe.matmul(ps[:, 0, i * KC + c:i * KC + c + 1], ada_acc[:, v * D + c * P:v * D + (c + 1) * P],
                                  ones[:, 0:1], start=True, stop=True)
                for i, v in enumerate(self.ROWS):
                    for j in range(2):
                        last = pe.matmul(ps[:, 1 + 2 * i + j, :], ones[:], ada_acc[:, v * D + j * 512:v * D + (j + 1) * 512],
                                         start=True, stop=True)
                last.then_inc(self.summed, 1)
                stage_end(pe)

            def dve(self, dve, own):
                dve.wait_ge(self.summed, 1)
                for i, v in enumerate(self.COLS):
                    own(dve.tensor_tensor(mod_cols[:, i], ps[:, 0, i * KC:(i + 1) * KC], col("ada_b_2", v * KC, KC), ALU.add))
                for i, name in ((1, "norm_mix_g_2"), (3, "norm_ffn_g_2")):
                    dve.scalar_tensor_tensor(out=mod_cols[:, i], in0=mod_cols[:, i], scalar=1.0, in1=col(name, 0, KC),
                                             op0=ALU.add, op1=ALU.mult)
                dve.wait_ge(self.b_landed, 32)
                for i in range(2):
                    dve.tensor_tensor(g_bc[:, i].rearrange("p (j n) -> p j n", j=2), ps[:, 1 + 2 * i:3 + 2 * i, :],
                                      g_bc[:, i].rearrange("p (j n) -> p j n", j=2), ALU.add)
                stage_end(dve)

        class ConformerStage:
            def __init__(self):
                self.hi = sem("cf_hi")
                self.lo = sem("cf_lo")
                self.cols = sem("cf_cols")
                self.tanh = sem("cf_tanh")
                self.u = sem("cf_u")
                self.conv = sem("cf_conv")
                self.mean = sem("cf_mean")
                self.centred = sem("cf_centred")
                self.squares = sem("cf_squares")
                self.var = sem("cf_var")
                self.normed = sem("cf_normed")
                self.tanh2 = sem("cf_tanh2")
                self.y = sem("cf_y")
                self.taps = sem("cf_taps")
                self.diag_ready, self.diag_used, self.conv_pe = sem("cf_diag_ready"), sem("cf_diag_used"), sem("cf_conv_pe")
                self.y_view = xn[:].rearrange("p t d -> p (t d)").rearrange("p (c s) -> p c s", c=KC)

            def pe(self, pe):
                for c in range(KC):
                    for g in range(2):
                        w = halves(pe, "conv_in", c // 2, 2 * (c % 2) + g)
                        columns_by_tokens(pe, ps[:, c, g * S:(g + 1) * S], w).then_inc(pieces_used, 1)
                for i, c in enumerate(CONV_PE):
                    pe.wait_ge(self.u, c + 1)
                    for j in range(TAPS):
                        pe.wait_ge(self.diag_ready, i * TAPS + j + 1)
                        pe.matmul(ps[:, i, 0:S], diag[:, (i * TAPS + j) % DIAGS], u_pad[:, c, j:j + S],
                                  start=(j == 0), stop=(j == TAPS - 1)).then_inc(self.diag_used, 1)
                y = self.y_view
                pe.wait_ge(self.conv, KC - len(CONV_PE))
                pe.wait_ge(self.conv_pe, len(CONV_PE))
                for c in range(KC):
                    last = pe.matmul(ps[:, 6, 0:S], mean_w[:], y[:, c], start=(c == 0), stop=(c == KC - 1))
                last.then_inc(self.mean, 1)
                pe.wait_ge(self.squares, 1)
                for c in range(KC):
                    last = pe.matmul(ps[:, 7, 0:S], mean_w[:], mixT[:, c], start=(c == 0), stop=(c == KC - 1))
                last.then_inc(self.var, 1)
                pe.wait_ge(self.lo, KC)
                for i in range(2):
                    tokens_by_columns(pe, "conv_out", i, (2 + 2 * i, 3 + 2 * i))

            def act(self, act):
                made = [0]

                def diagonals(act, upto):
                    for n in range(made[0], min(upto, len(CONV_PE) * TAPS)):
                        c, j = CONV_PE[n // TAPS], n % TAPS
                        if n >= DIAGS:
                            act.wait_ge(self.diag_used, n - DIAGS + 1)
                        act.activation(diag[:, n % DIAGS], ident[:], ACT.Copy, scale=w_dw[:, c, j:j + 1]).then_inc(self.diag_ready, 1)
                        made[0] = n + 1

                act.wait_ge(self.cols, 1)
                for c in range(KC):
                    split_upto(act, split_hi, "conv_in", c // 2, 2 * (c % 2) + 1)
                    wait_used(act, "conv_in", c // 2, 2 * (c % 2) + 1)
                    if c >= 2:
                        act.wait_ge(self.u, c - 1)
                    act.activation(cf_th[:, c % 2], ps[:, c, S:2 * S], ACT.Tanh, bias=half[:, c:c + 1],
                                   scale=0.5).then_inc(self.tanh, 1)
                    diagonals(act, DIAGS // KC * (c + 1))
                for i, c in enumerate(CONV_PE):
                    diagonals(act, (i + 1) * TAPS + DIAGS - TAPS)
                    act.wait_ge(self.diag_used, (i + 1) * TAPS)
                    act.activation(self.y_view[:, c], ps[:, i, 0:S], ACT.Identity, bias=col("conv_b_dw_2", c)).then_inc(self.conv_pe, 1)
                act.wait_ge(self.centred, 1)
                act.activation(mixT[:], self.y_view, ACT.Square).then_inc(self.squares, 1)
                act.wait_ge(self.normed, 1)
                for c in range(KC):
                    act.activation(hnT[:, c], self.y_view[:, c], ACT.Tanh, bias=half[:, 2 * KC + c:2 * KC + c + 1],
                                   scale=half[:, KC + c:KC + c + 1]).then_inc(self.tanh2, 1)
                for c in range(KC):
                    act.wait_ge(self.y, c + 1)
                    act.copy(xT_hi[:, c], mixT[:, c]).then_inc(self.hi, 1)
                split_upto(act, split_hi, "conv_out", 1, 3)

            def dve(self, dve, own):
                for i, (name, at) in enumerate((("conv_b_in_2", KC), ("conv_ln_g_2", 0), ("conv_ln_b_2", 0))):
                    last = dve.tensor_scalar(half[:, i * KC:(i + 1) * KC], col(name, at, KC), 0.5, None, ALU.mult)
                last.then_inc(self.cols, 1)
                own(dve.memset(u_pad[:, :, 0:TAPS - 1], 0.0))
                y = self.y_view
                def gated(c):
                    dve.wait_ge(self.tanh, c + 1)
                    own(dve.tensor_scalar(cf_a[:, c % 2], ps[:, c, 0:S], col("conv_b_in_2", c), 0.5, ALU.add, ALU.mult))
                    dve.scalar_tensor_tensor(out=u_pad[:, c, TAPS - 1:], in0=cf_th[:, c % 2], scalar=1.0, in1=cf_a[:, c % 2],
                                             op0=ALU.add, op1=ALU.mult).then_inc(self.u, 1)

                def convolve(chunks, before, first, last):
                    for j in range(first, last):
                        for at, c in enumerate(chunks):
                            w, src = w_dw[:, c, j:j + 1], u_pad[:, c, j:j + S]
                            if j == 0:
                                dve.wait_ge(self.u, c + 1)
                                ins = dve.tensor_scalar(y[:, c], src, w, col("conv_b_dw_2", c), ALU.mult, ALU.add)
                            else:
                                dve.wait_ge(self.taps, before + len(chunks) * (j - 1) + at + 1)
                                ins = dve.scalar_tensor_tensor(out=y[:, c], in0=src, scalar=w, in1=y[:, c], op0=ALU.mult,
                                                               op1=ALU.add)
                            ins.then_inc(self.taps if j < TAPS - 1 else self.conv, 1)

                early, late = (0, 1), tuple(range(2, CONV_PE[0]))
                beside = 6
                for c in range(KC):
                    split_upto(dve, split_lo, "conv_in", c // 2, 2 * (c % 2) + 1)
                    gated(c)
                    if c >= 2:
                        convolve(early, 0, min(beside * (c - 2), TAPS), min(beside * (c - 1), TAPS))
                convolve(late, len(early) * (TAPS - 1), 0, TAPS)
                dve.wait_ge(self.conv, KC - len(CONV_PE))
                dve.wait_ge(self.conv_pe, len(CONV_PE))
                dve.wait_ge(self.mean, 1)
                dve.tensor_tensor(y, y, ps[:, 6, 0:S].unsqueeze(1).to_broadcast([P, KC, S]), ALU.subtract
                                  ).then_inc(self.centred, 1)
                dve.wait_ge(self.var, 1)
                own(dve.tensor_copy(cf_r[:, 0], ps[:, 7, 0:S]))
                rsqrt(dve, own, cf_r[:, 0], cf_r[:, 1], cf_r[:, 2], cf_r[:, 3])
                dve.wait_ge(self.centred, 1)
                dve.tensor_tensor(y, y, cf_r[:, 1].unsqueeze(1).to_broadcast([P, KC, S]), ALU.mult).then_inc(self.normed, 1)
                dve.wait_ge(self.normed, 1)
                for c in range(KC):
                    dve.wait_ge(self.tanh2, c + 1)
                    own(dve.tensor_scalar(y[:, c], y[:, c], half[:, KC + c:KC + c + 1], half[:, 2 * KC + c:2 * KC + c + 1],
                                          ALU.mult, ALU.add))
                    dve.scalar_tensor_tensor(out=mixT[:, c], in0=hnT[:, c], scalar=1.0, in1=y[:, c], op0=ALU.add,
                                             op1=ALU.mult).then_inc(self.y, 1)
                for c in range(KC):
                    dve.wait_ge(self.hi, c + 1)
                    dve.tensor_tensor(xT_lo[:, c], mixT[:, c], xT_hi[:, c].bitcast(F32), ALU.subtract).then_inc(self.lo, 1)
                for i in range(2):
                    split_upto(dve, split_lo, "conv_out", i, 3)
                    wait_used(dve, "conv_out", i, 3)
                    for t in range(T):
                        o, g = h[:, t, i * 512:(i + 1) * 512], g_bc[:, 0, i * 512:(i + 1) * 512]
                        tmp = xn[:, t, i * 512:(i + 1) * 512]
                        own(dve.tensor_tensor(tmp, ps[:, 2 + 2 * i + t, :], g, ALU.mult))
                        ins = dve.tensor_tensor(o, o, tmp, ALU.add)
                    ins.then_inc(h_ready, 1)

        class RouteStage:
            def __init__(self):
                self.made, self.gmax, self.gexp, self.diff, self.dexp = (sem("rt_" + n) for n in
                                                                        ("made", "gmax", "gexp", "diff", "dexp"))
                self.turned, self.chosen, self.counted = sem("rt_turned"), sem("rt_chosen"), sem("rt_counted")

            def pe(self, pe):
                for t in range(T):
                    for k in range(KC):
                        last = pe.matmul(ps[:, t, 0:GROUPS + EXPERTS], hnT[:, k, t * P:(t + 1) * P], w_route[:, k, :],
                                         start=(k == 0), stop=(k == KC - 1))
                last.then_inc(self.made, 1)
                for b in range(4):
                    for c in range(4):
                        k = (b % 2) * 4 + c
                        last = pe.transpose(ps[:, 4 + b, c * P:(c + 1) * P], hnT[:, k, (b // 2) * P:(b // 2 + 1) * P], ident[:])
                    last.then_inc(self.turned, 1)
                pe.wait_ge(self.chosen, 1)
                pe.matmul(ps[:, 2, 0:EXPERTS], upper[:], rt[:, 8, 0], start=True, stop=True)
                pe.matmul(ps[:, 2, EXPERTS:2 * EXPERTS], ones[:], rt[:, 8, 0], start=True, stop=False)
                pe.matmul(ps[:, 2, EXPERTS:2 * EXPERTS], upper[:], rt[:, 8, 1], start=False, stop=True)
                pe.matmul(ps[:, 3, 0:EXPERTS], ones[:], rt[:, 8, 0], start=True, stop=False)
                pe.matmul(ps[:, 3, 0:EXPERTS], ones[:], rt[:, 8, 1], start=False, stop=True).then_inc(self.counted, 1)
                stage_end(pe)

            def act(self, act):
                for b in range(4):
                    act.wait_ge(self.turned, b + 1)
                    act.copy(xn[:, b // 2, (b % 2) * 512:(b % 2 + 1) * 512], ps[:, 4 + b, :])
                act.wait_ge(self.gmax, 1)
                for t in range(T):
                    last = act.activation(rt[:, 1, t, 0:GROUPS], rt[:, 0, t, 0:GROUPS], ACT.Exp, bias=rts[:, 0, t:t + 1],
                                          accum_out=rts[:, 1, t:t + 1])
                last.then_inc(self.gexp, 1)
                act.wait_ge(self.diff, 1)
                act.activation(rts[:, 5], rts[:, 4], ACT.Exp).then_inc(self.dexp, 1)
                stage_end(act)

            def dve(self, dve, own):
                def wide(x, n=EXPERTS):
                    return x.unsqueeze(2).to_broadcast([P, T, n])

                def first_max(hot, x, top, key, key_top, n):
                    own(dve.tensor_tensor(key, x, wide(top, n), ALU.is_equal))
                    own(dve.tensor_tensor(key, key, rev[:, 0:n].unsqueeze(1).to_broadcast([P, T, n]), ALU.mult))
                    own(dve.tensor_reduce(key_top, key, AX.X, ALU.max))
                    own(dve.tensor_tensor(hot, key, wide(key_top, n), ALU.is_equal))

                grp, eg, key, hot1, hot2 = (rt[:, i] for i in (0, 2, 3, 4, 5))
                exp_l = rt[:, 6]
                g4 = grp[:, :, 0:GROUPS]
                dve.wait_ge(self.made, 1)
                own(dve.tensor_tensor(g4, ps[:, 0:T, 0:GROUPS], b_route[:, 0:GROUPS].unsqueeze(1).to_broadcast([P, T, GROUPS]),
                                      ALU.add))
                own(dve.tensor_tensor(exp_l, ps[:, 0:T, GROUPS:GROUPS + EXPERTS],
                                      b_route[:, GROUPS:].unsqueeze(1).to_broadcast([P, T, EXPERTS]), ALU.add))
                own(dve.tensor_reduce(rts[:, 2], g4, AX.X, ALU.max))
                dve.tensor_scalar(rts[:, 0], rts[:, 2], -1.0, None, ALU.mult).then_inc(self.gmax, 1)
                first_max(eg[:, :, 0:GROUPS], g4, rts[:, 2], key[:, :, 0:GROUPS], rts[:, 3], GROUPS)
                own(dve.tensor_scalar(eg[:, :, 0:GROUPS], eg[:, :, 0:GROUPS], -1.0, -NEG, ALU.add, ALU.mult))
                for t in range(T):
                    e3 = exp_l[:, t].rearrange("p (g e) -> p g e", g=GROUPS)
                    own(dve.tensor_tensor(e3, e3, eg[:, t, 0:GROUPS].unsqueeze(2).to_broadcast([P, GROUPS, PER_GROUP]), ALU.add))
                own(dve.tensor_reduce(rts[:, 6], exp_l, AX.X, ALU.max))
                first_max(hot1, exp_l, rts[:, 6], key, rts[:, 3], EXPERTS)
                own(dve.scalar_tensor_tensor(out=rt[:, 7], in0=hot1, scalar=3 * NEG, in1=exp_l, op0=ALU.mult, op1=ALU.add))
                own(dve.tensor_reduce(rts[:, 7], rt[:, 7], AX.X, ALU.max))
                first_max(hot2, rt[:, 7], rts[:, 7], key, rts[:, 3], EXPERTS)
                dve.tensor_tensor(rts[:, 4], rts[:, 7], rts[:, 6], ALU.subtract).then_inc(self.diff, 1)
                dve.tensor_tensor(rt[:, 8], hot1, hot2, ALU.add).then_inc(self.chosen, 1)
                dve.wait_ge(self.gexp, 1)
                own(dve.reciprocal(rts[:, 8], rts[:, 1]))
                dve.wait_ge(self.dexp, 1)
                own(dve.tensor_scalar(rts[:, 9], rts[:, 5], 1.0, None, ALU.add))
                own(dve.reciprocal(rts[:, 9], rts[:, 9]))
                own(dve.tensor_tensor(rts[:, 10], rts[:, 5], rts[:, 9], ALU.mult))
                for i in (9, 10):
                    own(dve.scalar_tensor_tensor(out=rts[:, i], in0=rts[:, i], scalar=0.5, in1=rts[:, 8], op0=ALU.mult,
                                                 op1=ALU.mult))
                own(dve.tensor_tensor(hot1, hot1, wide(rts[:, 9]), ALU.mult))
                own(dve.tensor_tensor(hot2, hot2, wide(rts[:, 10]), ALU.mult))
                own(dve.tensor_tensor(gate_half[:], hot1, hot2, ALU.add))
                dve.wait_ge(self.counted, 1)
                own(dve.tensor_tensor(place[:], ps[:, 2, 0:T * EXPERTS].rearrange("p (t e) -> p t e", t=T), rt[:, 8], ALU.mult))
                own(dve.tensor_scalar(place[:], place[:], -1.0, None, ALU.add))
                own(dve.tensor_reduce(rts[:, 0, 0:1], ps[:, 3, 0:EXPERTS], AX.X, ALU.max))
                own(dve.tensor_scalar(rts[:, 1, 0:1], rts[:, 0, 0:1], PLACES + 0.5, None, ALU.is_ge))
                own(dve.tensor_copy(crowded[:], rts[:, 1, 0:1]))
                stage_end(dve)

        class AllTokens:
            def __init__(self):
                self.blocks = MOE_BLOCKS
                self.gate_up = sem("all_gate_up")
                self.tanh = sem("all_tanh")
                self.half = sem("all_half")
                self.hid = sem("all_hid_ready")
                self.turned = sem("all_turned")
                self.hidT = sem("all_hidT_ready")
                self.loops = (self.blocks - 2) // 4

            def blocks_in_loop(self, eng, step):
                with eng.Fori(0, self.loops) as it:
                    for j in range(4):
                        step(2 + j, it)
                for n in range(2 + 4 * self.loops, self.blocks):
                    step(n, None)

            @staticmethod
            def at(value, per_block, it):
                return value if it is None else value + 4 * per_block * it

            def pe(self, pe):
                at = self.at

                def gate_up(n, it, t):
                    if t == 0:
                        wait_gate_up(pe, n // HALVES, it)
                    if n >= 1:
                        pe.wait_ge(self.hid, at(2 * (n - 1) + t + 1, 2, it))
                    w = gate_up_of(n // HALVES)[:, :, :, n % HALVES * BLK:(n % HALVES + 1) * BLK]
                    for k in range(KC):
                        last = pe.matmul(ps[:, t, :].rearrange("p (two f) -> p two f", two=2), hnT[:, k, t * P:(t + 1) * P], w[:, k],
                                         start=(k == 0), stop=(k == KC - 1))
                    last.then_inc(self.gate_up, 1)
                    if n % HALVES == 1 and t == 1:
                        pe.drain().then_inc(gu_used, 1)

                def turn(n, it):
                    pe.wait_ge(self.hid, at(2 * n + 2, 2, it))
                    if n >= 1:
                        pe.wait_ge(self.hidT, at(n, 1, it))
                    for c in range(2):
                        for t in range(T):
                            last = pe.transpose(ps[:, 2, c * S + t * P:c * S + (t + 1) * P],
                                                all_hid[:, n % 2, t, c * P:(c + 1) * P], ident[:])
                    last.then_inc(self.turned, 1)

                def down(n, it):
                    pe.wait_ge(self.hidT, at(n + 1, 1, it))
                    wait_down(pe, n // HALVES, it)
                    w = down_of(n // HALVES)[:, n % HALVES * 2:n % HALVES * 2 + 2]
                    for t in range(T):
                        for half in range(2):
                            for c in range(2):
                                last = pe.matmul(ps[:, 4 + 2 * t + half, :], all_hidT[:, c, t * P:(t + 1) * P],
                                                 w[:, c, half * 512:(half + 1) * 512],
                                                 start=(n == 0 and c == 0), stop=(n == self.blocks - 1 and c == 1))
                    if n % (2 * HALVES) == 2 * HALVES - 1:
                        last.then_inc(down_used, 1)

                def step(n, it):
                    gate_up(n, it, 0)
                    turn(n - 1, it)
                    gate_up(n, it, 1)
                    down(n - 1, it)

                gate_up(0, None, 0)
                gate_up(0, None, 1)
                step(1, None)
                self.blocks_in_loop(pe, step)
                turn(self.blocks - 1, None)
                down(self.blocks - 1, None)

            def act(self, act):
                at = self.at

                def tanh(n, it, t):
                    act.wait_ge(self.gate_up, at(2 * n + t + 1, 2, it))
                    act.activation(all_th[:, t], ps[:, t, 0:BLK], ACT.Tanh, scale=0.5).then_inc(self.tanh, 1)

                def copy(n, it):
                    act.wait_ge(self.turned, at(n + 1, 1, it))
                    act.copy(all_hidT[:], ps[:, 2, :].rearrange("p (c s) -> p c s", c=2)).then_inc(self.hidT, 1)

                def step(n, it):
                    tanh(n, it, 0)
                    copy(n - 1, it)
                    tanh(n, it, 1)

                tanh(0, None, 0)
                tanh(0, None, 1)
                step(1, None)
                self.blocks_in_loop(act, step)
                copy(self.blocks - 1, None)

            def dve(self, dve):
                at = self.at

                def step(n, it):
                    for t in range(T):
                        dve.wait_ge(self.tanh, at(2 * n + t + 1, 2, it))
                        dve.scalar_tensor_tensor(out=all_a[:, t], in0=all_th[:, t], scalar=1.0, in1=ps[:, t, 0:BLK],
                                                 op0=ALU.add, op1=ALU.mult).then_inc(self.half, 1)
                        if n >= 2:
                            dve.wait_ge(self.turned, at(n - 1, 1, it))
                        dve.wait_ge(self.half, at(2 * n + t + 1, 2, it))
                        e = n // HALVES if it is None else n // HALVES + it * (4 // HALVES)
                        share = gate_half[:, t, bass.ds(e, 1)]
                        dve.scalar_tensor_tensor(out=all_hid[:, n % 2, t], in0=all_a[:, t], scalar=share,
                                                 in1=ps[:, t, BLK:2 * BLK], op0=ALU.mult,
                                                 op1=ALU.mult).then_inc(self.hid, 1)

                step(0, None)
                step(1, None)
                self.blocks_in_loop(dve, step)
                dve.wait_ge(down_used, EXPERTS // 2)

        class ExpertsStage:
            PAIRS = EXPERTS // 2

            def __init__(self):
                self.all_tokens = AllTokens()
                self.sel = sem("ge_sel_ready")
                self.share = sem("ge_share_ready")
                self.gathered = sem("ge_gathered")
                self.xT = sem("ge_xT_ready")
                self.tanh = sem("ge_tanh_ready")
                self.half = sem("ge_half")
                self.hid = sem("ge_hid_ready")
                self.share_turned = sem("ge_share_turned")
                self.turned = sem("ge_hid_turned")
                self.copied = sem("ge_turned_copied")
                self.y = sem("ge_y_ready")
                self.given = sem("ge_given_back")

            def either(self, eng, gathered, dense):
                many = eng.value_load(crowded[0:1, 0:1], min_val=0, max_val=1)
                with eng.If(many == 0):
                    gathered()
                with eng.Else():
                    dense()

            def pairs(self, eng, step):
                step(0, None)
                step(1, None)
                with eng.Fori(0, self.PAIRS - 3) as it:
                    step(2, it)
                step(self.PAIRS - 1, None)

            def pe(self, pe):
                at = per_round

                def gather(p, it):
                    pe.wait_ge(self.sel, at(p + 1, it, 1))
                    for k in range(KC):
                        for t in range(T):
                            last = pe.matmul(ps[:, 2 + k // 4, (k % 4) * P:(k % 4 + 1) * P], xn[:, t, k * P:(k + 1) * P], ge_sel[:, t],
                                             start=(t == 0), stop=(t == T - 1))
                    last.then_inc(self.gathered, 1)

                def gate_up(p, it, e):
                    wait_gate_up(pe, 2 * p + e, it)
                    if e == 0:
                        pe.wait_ge(self.xT, at(p + 1, it, 1))
                    for k in range(KC):
                        for f in range(HALVES):
                            out = ps[f * PLACES:(f + 1) * PLACES, 2 + e, :].rearrange("p (two f) -> p two f", two=2)
                            last = pe.matmul(out, ge_xT[:, k, e * PLACES:(e + 1) * PLACES],
                                             gate_up_of(e)[:, k, :, f * BLK:(f + 1) * BLK], start=(k == 0), stop=(k == KC - 1))
                    last.then_inc(gu_used, 1)

                def turn_shares(p, it):
                    pe.wait_ge(self.share, at(p + 1, it, 1))
                    if p >= 1:
                        pe.wait_ge(self.y, at(p, it, 1))
                    for t in range(T):
                        last = pe.transpose(ps[:, 1, t * P:(t + 1) * P], ge_share[:, t], ident[:])
                    last.then_inc(self.share_turned, 1)

                def turn(p, it):
                    pe.wait_ge(self.hid, at(2 * p + 2, it, 2))
                    for e in range(2):
                        for c in range(2):
                            n = (2 * e + c) * P
                            last = pe.transpose(ps[:, 0, n:n + P], ge_hid[:, e, c * P:(c + 1) * P], ident[:])
                    last.then_inc(self.turned, 1)

                def down(p, it):
                    for e in range(2):
                        wait_down(pe, 2 * p + e, it)
                    pe.wait_ge(self.copied, at(2 * p + 2, it, 2))
                    for f in range(HALVES):
                        for c in range(2):
                            for n in range(2):
                                for e in range(2):
                                    last = pe.matmul(ps[e * PLACES:(e + 1) * PLACES, n, :], ge_hidT[:, e, c, f * PLACES:(f + 1) * PLACES],
                                                     down_of(e)[:, 2 * f + c, n * 512:(n + 1) * 512],
                                                     start=(f == 0 and c == 0), stop=(f == HALVES - 1 and c == 1))
                    last.then_inc(down_used, 1)

                def give_back(p, it):
                    pe.wait_ge(self.y, at(p + 1, it, 1))
                    for t in range(T):
                        for n in range(2):
                            last = pe.matmul(ps[:, 4 + 2 * t + n, :], ge_shareT[:, t], ge_y[:, n],
                                             start=(p == 0), stop=(p == self.PAIRS - 1))
                    last.then_inc(self.given, 1)

                def step(p, it):
                    gate_up(p, it, 0)
                    turn_shares(p, it)
                    gate_up(p, it, 1)
                    if p > 0:
                        give_back(p - 1, it)
                    turn(p, it)
                    if p < self.PAIRS - 1:
                        gather(p + 1, it)
                    down(p, it)

                def gathered():
                    gather(0, None)
                    self.pairs(pe, step)
                    give_back(self.PAIRS - 1, None)

                self.either(pe, gathered, lambda: self.all_tokens.pe(pe))
                stage_end(pe)

            def act(self, act):
                at = per_round

                def copy_x(p, it):
                    act.wait_ge(self.gathered, at(p + 1, it, 1))
                    act.copy(ge_xT[:], ps[:, 2:4, :].rearrange("p b (k n) -> p (b k) n", k=4)).then_inc(self.xT, 1)

                def step(p, it):
                    for e in range(2):
                        act.wait_ge(gu_used, at(2 * p + e + 1, it, 2))
                        act.activation(ge_th[:, e], ps[:, 2 + e, 0:BLK], ACT.Tanh, scale=0.5).then_inc(self.tanh, 1)
                    act.wait_ge(self.share_turned, at(p + 1, it, 1))
                    if p > 0:
                        act.wait_ge(self.given, at(p, it, 1))
                    act.copy(ge_shareT[:], ps[:, 1, 0:T * P].rearrange("p (t n) -> p t n", t=T)).then_inc(self.copied, 1)
                    act.wait_ge(self.turned, at(p + 1, it, 1))
                    act.copy(ge_hidT[:], ps[:, 0, :].rearrange("p (e c n) -> p e c n", e=2, c=2)).then_inc(self.copied, 1)
                    if p < self.PAIRS - 1:
                        copy_x(p + 1, it)

                def gathered():
                    copy_x(0, None)
                    self.pairs(act, step)

                self.either(act, gathered, lambda: self.all_tokens.act(act))
                stage_end(act)

            def dve(self, dve, own):
                at = per_round

                def columns(p, it):
                    for e in range(2):
                        for t in range(T):
                            c = bass.ds(at(2 * p + e, it, 2), 1)
                            yield t, slice(e * PLACES, (e + 1) * PLACES), place[:, t, c], gate_half[:, t, c]

                def select(p, it):
                    for t, cut, where, _ in columns(p, it):
                        last = dve.tensor_scalar(ge_sel[:, t, cut], places[:], where, None, ALU.is_equal)
                    last.then_inc(self.sel, 1)

                def shares(p, it):
                    if p >= 1:
                        dve.wait_ge(self.share_turned, at(p, it, 1))
                    for t, cut, where, share in columns(p, it):
                        last = dve.tensor_scalar(ge_share[:, t, cut], places[:], where, share, ALU.is_equal, ALU.mult)
                    last.then_inc(self.share, 1)

                def copy_y(p, it):
                    dve.wait_ge(down_used, at(p + 1, it, 1))
                    dve.tensor_copy(ge_y[:], ps[:, 0:2, :]).then_inc(self.y, 1)

                def hidden(p, it, e):
                    n = at(2 * p + e + 1, it, 2)
                    dve.wait_ge(self.tanh, n)
                    dve.scalar_tensor_tensor(out=ge_a[:], in0=ge_th[:, e], scalar=1.0, in1=ps[:, 2 + e, 0:BLK], op0=ALU.add,
                                             op1=ALU.mult).then_inc(self.half, 1)
                    dve.wait_ge(self.half, n)
                    dve.tensor_tensor(ge_hid[:, e], ge_a[:], ps[:, 2 + e, BLK:2 * BLK], ALU.mult).then_inc(self.hid, 1)
                    dve.wait_ge(self.hid, n)

                def step(p, it):
                    if p > 0:
                        copy_y(p - 1, it)
                    else:
                        dve.wait_ge(self.gathered, 1)
                    if p < self.PAIRS - 1:
                        select(p + 1, it)
                    hidden(p, it, 0)
                    if p < self.PAIRS - 1:
                        shares(p + 1, it)
                    hidden(p, it, 1)

                def gathered():
                    select(0, None)
                    shares(0, None)
                    self.pairs(dve, step)
                    copy_y(self.PAIRS - 1, None)
                    dve.wait_ge(self.given, self.PAIRS)

                self.either(dve, gathered, lambda: self.all_tokens.dve(dve))
                for t in range(T):
                    for half in range(2):
                        cut = slice(half * 512, (half + 1) * 512)
                        own(dve.tensor_tensor(xn[:, t, cut], ps[:, 4 + 2 * t + half, :], g_bc[:, 1, cut], ALU.mult))
                        dve.tensor_tensor(h[:, t, cut], h[:, t, cut], xn[:, t, cut], ALU.add)
                stage_end(dve)

        class FinalStage:
            def __init__(self):
                self.squares, self.rstd, self.made = sem("fin_squares"), sem("fin_rstd"), sem("fin_made")
                self.f_landed = sem("fin_gain_landed")

            def load(self, act):
                act.dma_start(f_bc[:], a["final_g_2"].partition_broadcast(P)).then_inc(self.f_landed, 16)

            def act(self, act):
                for t in range(T):
                    act.activation(xn[:, t], h[:, t], ACT.Square, scale=float(D) ** -0.5,
                                   accum_out=ms[:, t:t + 1]).then_inc(self.squares, 1)

            def dve(self, dve, own):
                dve.wait_ge(self.squares, T)
                rsqrt_ms(dve, own, T, self.rstd)
                dve.wait_ge(self.rstd, 1)
                dve.wait_ge(self.f_landed, 16)
                for t in range(T):
                    dve.scalar_tensor_tensor(out=xn[:, t], in0=h[:, t], scalar=rs[:, t:t + 1], in1=f_bc[:], op0=ALU.mult,
                                             op1=ALU.mult).then_inc(self.made, 1)

            def store(self, sp):
                o = out[0].rearrange("(t p) d -> p t d", p=P)
                for t in range(T):
                    sp.wait_ge(self.made, t + 1)
                    sp.dma_start(o[:, t], xn[:, t]).then_inc(out_landed, 16)
                sp.wait_ge(out_landed, 16 * T)

        def idle(eng):
            stage_end(eng)

        setup = SetupStage()
        norms = [NormStage(0, lambda c: col("g_mix", c)),
                 NormStage(1, lambda c: col("g_ffn", c), folded=True),
                 NormStage(2, lambda c: col("g_ple", c), folded=True),
                 NormStage(3, lambda c: col("g_mix", KC + c), folded=True),
                 NormStage(4, lambda c: col("g_ffn", KC + c), folded=True),
                 NormStage(5, lambda c: col("g_ple", KC + c), folded=True),
                 NormStage(6, lambda c: mod_cols[:, 1, c:c + 1], lambda c: mod_cols[:, 0, c:c + 1]),
                 NormStage(7, lambda c: mod_cols[:, 3, c:c + 1], lambda c: mod_cols[:, 2, c:c + 1], split=False)]
        even = EvenStage()
        ffn = [FfnStage(0, norms[1]), FfnStage(1, norms[4], ada_products)]
        ple = [PleStage(0, norms[2]), PleStage(1, norms[5])]
        odd_in, odd_up, odd_heads, odd_attend, odd_out = OddIn(norms[3]), OddUp(), OddHeads(), OddAttend(), OddOut()
        mod, conformer, route, final = ModStage(), ConformerStage(), RouteStage(), FinalStage()
        moe = ExpertsStage()

        block = ctx.enter_context(nc.Block())

        @block.scalar
        def _(act):
            setup.act(act)
            norms[0].act(act, ("ev_in", 0, 3))
            setup.act_rest(act)
            even.act(act)
            norms[1].act(act, ("ffn0", 0, 2))
            ffn[0].act(act)
            norms[2].act(act)
            ple[0].act(act)
            norms[3].act(act, ("od_in", 0, 2))
            odd_in.act(act)
            odd_up.act(act)
            odd_heads.act(act)
            odd_attend.act(act)
            odd_out.act(act)
            norms[4].act(act, ("ffn1", 0, 2))
            mod.load(act)
            ffn[1].act(act)
            norms[5].act(act)
            ple[1].act(act)
            stage_end(act)
            norms[6].act(act, ("conv_in", 0, 3))
            conformer.act(act)
            norms[7].act(act)
            final.load(act)
            stage_end(act)
            route.act(act)
            moe.act(act)
            final.act(act)

        @block.gpsimd
        def _(pool):
            setup.pool(pool)
            stage_end(pool)
            odd_in.pool(pool)
            for _ in range(3):
                stage_end(pool)
            ada_loads(pool)
            for _ in range(4):
                stage_end(pool)

        @block.tensor
        def _(pe):
            setup.pe(pe)
            norms[0].pe(pe)
            setup.pe_rest(pe)
            even.pe(pe)
            norms[1].pe(pe)
            ffn[0].pe(pe)
            norms[2].pe(pe)
            ple[0].pe(pe)
            norms[3].pe(pe)
            odd_in.pe(pe)
            odd_up.pe(pe)
            odd_heads.pe(pe)
            odd_attend.pe(pe)
            odd_out.pe(pe)
            norms[4].pe(pe)
            ffn[1].pe(pe)
            norms[5].pe(pe)
            ple[1].pe(pe)
            mod.pe(pe)
            norms[6].pe(pe)
            conformer.pe(pe)
            norms[7].pe(pe)
            stage_end(pe)
            route.pe(pe)
            moe.pe(pe)

        @block.vector
        def _(dve):
            own = Own(dve, dve_own)
            stage_end(dve)
            norms[0].dve(dve, own, ("ev_in", 0, 3))
            setup.dve_rest(dve, own)
            even.dve(dve, own)
            norms[1].dve(dve, own, ("ffn0", 0, 2))
            ffn[0].dve(dve, own)
            norms[2].dve(dve, own)
            ple[0].dve(dve, own)
            norms[3].dve(dve, own, ("od_in", 0, 2))
            odd_in.dve(dve, own)
            odd_up.dve(dve, own)
            odd_heads.dve(dve, own)
            odd_attend.dve(dve, own)
            odd_out.dve(dve, own)
            norms[4].dve(dve, own, ("ffn1", 0, 2))
            ffn[1].dve(dve, own)
            norms[5].dve(dve, own)
            ple[1].dve(dve, own)
            mod.dve(dve, own)
            norms[6].dve(dve, own, ("conv_in", 0, 3))
            conformer.dve(dve, own)
            norms[7].dve(dve, own)
            stage_end(dve)
            route.dve(dve, own)
            moe.dve(dve, own)
            final.dve(dve, own)

        @block.sync
        def _(sp):
            weight_stream(sp)
            final.store(sp)


_INS = ["x", "p", "positions", "g_mix", "g_ffn", "g_ple", "ev_w_in", "ev_w_conv", "ev_g_v", "ev_w_s", "ev_b_s", "ev_w_out",
        "od_w_in", "od_b_gate", "od_g_qa", "od_g_kva", "od_w_q_up", "od_w_kv_up", "od_g_q", "od_g_k", "od_g_mh", "od_w_out",
        "w_gate", "w_up", "w_down", "w_ple_proj", "w_ple_gate", "c_2", "ada_w_2", "ada_b_2", "norm_mix_g_2",
        "norm_ffn_g_2", "final_g_2", "conv_w_in_2", "conv_b_in_2", "conv_w_dw_2", "conv_b_dw_2", "conv_ln_g_2",
        "conv_ln_b_2", "conv_w_out_2", "moe_w_rg_2", "moe_b_rg_2", "moe_w_re_2", "moe_b_re_2", "moe_w_gate_2",
        "moe_w_up_2", "moe_w_down_2"]


def kernel(**inputs):
    import numpy as _np
    import concourse.bacc as _bacc
    from concourse import mybir as _mybir
    from concourse.bass_utils import run_bass_kernel_spmd as _run

    nc = _bacc.Bacc("TRN2", target_bir_lowering=False, num_devices=1)
    arrays, args = {}, {}
    for name in _INS:
        v = _np.ascontiguousarray(inputs[name])
        arrays[f"in_{name}"] = v
        args[name] = nc.dram_tensor(f"in_{name}", v.shape, _mybir.dt.from_np(v.dtype), kind="ExternalInput").ap()
    out = nc.dram_tensor("out", (1, S, D), F32, kind="ExternalOutput").ap()
    build(nc, args, out)
    r = _run(nc, [arrays], core_ids=[0])
    return r.results[0]["out"]
```

```python
from contextlib import ExitStack, contextmanager

import numpy as np

import concourse.bass as bass
from concourse import mybir

F32 = mybir.dt.float32
I32 = mybir.dt.int32
F32R = mybir.dt.float32r
ALU = mybir.AluOpType
ACT = mybir.ActivationFunctionType
AX = mybir.AxisListType

P = 128
D = 1024
S = 256
T = S // P
KC = D // P
EPS = 1e-6
NEG = -1e30

GM_HEADS, GM_HD = 8, 64
Q_LORA, KV_LORA = 384, 256
HEADS, NOPE, ROPE, VD = 8, 64, 32, 64
QK = NOPE + ROPE
MH, MQK, MV = 4, 64, 128
ROPE_THETA = 10000.0
ODD_IN = Q_LORA + KV_LORA + ROPE + 2 * MH * MQK + 2 * MH * MV + 2 * MH
AT_KPE = Q_LORA + KV_LORA
AT_MQ = AT_KPE + ROPE
AT_MK = AT_MQ + MH * MQK
AT_MV = AT_MK + MH * MQK
AT_MO = AT_MV + MH * MV
AT_MI = AT_MO + MH * MV
D_FF = 2816
TAPS = 31
CONV_PE = (5, 6, 7)
DIAGS = 48
GROUPS, PER_GROUP = 4, 8
EXPERTS = GROUPS * PER_GROUP
EXPERT_HID = 512

BLK = 256
FF_BLOCKS = D_FF // BLK
HALVES = EXPERT_HID // BLK
MOE_BLOCKS = EXPERTS * HALVES
PLACES = 64
SLOT = 3 * KC * BLK
AT_DOWN = 2 * KC * BLK
SLOTS = 2

ITEMS = [("ev_in", 5, 1, 0), ("ev_out", 2, 1, 0), ("ffn0", FF_BLOCKS, 2, 1), ("ple0", 2, 1, 1), ("od_in", 5, 1, 0),
         ("od_up", 1, 1, 1), ("od_out", 2, 1, 0), ("ffn1", FF_BLOCKS, 2, 1), ("ple1", 2, 1, 1), ("conv_in", 4, 2, 0),
         ("conv_out", 2, 1, 0)]
EARLY = 3
EARLY_DOWN_ROWS = EXPERT_HID // P - 1
EARLY_DMAS = 2 * 4 + 2


class Part:

    def __init__(self, column):
        self.first, self.landed, counts = {}, [], [0] * SLOTS
        for row in ITEMS:
            self.first[row[0]] = len(self.landed)
            for _ in range(row[1] if row[column] else 0):
                s = len(self.landed) % SLOTS
                counts[s] += 16 * row[column]
                self.landed.append(counts[s])


A, B = Part(2), Part(3)

PIECE = 4 * BLK
PIECES = []
for _name, _n, _, _ in ITEMS:
    if _name == "od_up":
        continue
    for _i in range(_n):
        PIECES += [(_name, _i, _j) for _j in range(4)]
        if _name.startswith("ffn") and _i > 0:
            PIECES += [(_name, _i - 1, _j) for _j in (4, 5)]
    if _name.startswith("ffn"):
        PIECES += [(_name, _n - 1, _j) for _j in (4, 5)]
PIECE_AT = {_piece: _at for _at, _piece in enumerate(PIECES)}
BUFFERS = 4
FF_PIECES = 6
ADA_BUFFERS = 4
FF_ROUND = 4

ROWS_A, ROWS_B = {}, {}
for _rows, _names in ((ROWS_A, [("g_mix", 16), ("g_ffn", 16), ("g_ple", 16), ("norm_mix_g_2", 8), ("norm_ffn_g_2", 8),
                                ("conv_b_dw_2", 8), ("conv_ln_g_2", 8), ("conv_ln_b_2", 8), ("conv_b_in_2", 16),
                                ("od_g_qa", 3), ("od_g_kva", 2), ("ev_w_conv", 12)]),
                      (ROWS_B, [("ada_b_2", 48), ("ev_b_s", 8), ("c_2", 8)])):
    _at = 0
    for _n, _c in _names:
        _rows[_n] = (_at, _c)
        _at += _c
N_ROWS_A = sum(c for _, c in ROWS_A.values())
N_ROWS_B = sum(c for _, c in ROWS_B.values())
SMALL_LANDED = 16 * (14 + len(ROWS_B))


class Own:

    def __init__(self, eng, sem):
        self.eng, self.sem, self.n = eng, sem, 0

    def __call__(self, ins):
        self.n += 1
        ins.then_inc(self.sem, 1)
        self.eng.wait_ge(self.sem, self.n)


def build(nc, a, out):
    ctx = ExitStack()
    with ctx:
        def sb(name, shape, dt=F32):
            return ctx.enter_context(nc.sbuf_tensor(name, shape, dt))

        def sem(name):
            return ctx.enter_context(nc.semaphore(name))

        dense_weights = sb("dense_weights", [P, SLOTS, SLOT])
        ring = [dense_weights[:, s] for s in range(SLOTS)]
        h = sb("h", [P, T, D])
        hnT = sb("hnT", [P, KC, S])
        g_bc = sb("g_bc", [P, 2, D])
        rstd = sb("rstd", [P, 4, T])
        xn = sb("xn", [P, T, D])
        mixT = sb("mixT", [P, KC, S])
        ident = sb("ident", [P, P])
        ones = sb("ones", [P, P])
        mean_w = sb("mean_w", [P, P])
        upper = sb("upper", [P, P])
        cmask = sb("cmask", [P, 3 * P])
        wsT = sb("wsT", [P, GM_HEADS, P])
        pT = sb("pT", [P, 2, 2, S])
        cols_a = sb("cols_a", [P, P])
        cols_b = sb("cols_b", [P, P])
        w_dw = sb("w_dw", [P, KC, TAPS])
        g_v = sb("g_v", [P, GM_HEADS * GM_HD])
        g_q = sb("g_q", [P, QK])
        g_k = sb("g_k", [P, QK])
        g_mh = sb("g_mh", [P, MH * MV])
        b_gate = sb("b_gate", [P, 2 * MH])
        b_route = sb("b_route", [P, GROUPS + EXPERTS])
        w_route = sb("w_route", [P, KC, GROUPS + EXPERTS])
        rev = sb("rev", [P, EXPERTS])
        pos_i = sb("pos_i", [P, T], I32)
        ms = sb("ms", [P, 64])
        rs = sb("rs", [P, 64])
        rtmp = sb("rtmp", [P, 2, 64])
        c_act = sb("c_act", [P, KC])
        mod_cols = sb("mod_cols", [P, 4, KC])
        gate_half = sb("gate_half", [P, T, EXPERTS])
        places = sb("places", [P, PLACES])
        ps = ctx.enter_context(nc.psum_tensor("ps", [P, 8, 512], F32))

        def col(name, c, n=1):
            rows, tile = (ROWS_A, cols_a) if name in ROWS_A else (ROWS_B, cols_b)
            at = rows[name][0] + c
            return tile[:, at:at + n]

        @contextmanager
        def scope():
            with ExitStack() as inner:
                yield lambda name, shape, dt=F32: inner.enter_context(nc.sbuf_tensor(name, shape, dt))

        with scope() as dense:
            xT_hi = dense("xT_hi", [P, KC, S], F32R)
            xT_lo = dense("xT_lo", [P, KC, S], F32R)
            w_hi = dense("w_hi", [P, BUFFERS, PIECE], F32R)
            w_lo = dense("w_lo", [P, BUFFERS, PIECE], F32R)
            with scope() as st:
                ws_rows = st("ws_rows", [P, GM_HEADS, P])
                p_rows = st("p_rows", [P, 2, T, 256])
                rows_a = st("rows_a", [P, P])
                rows_b = st("rows_b", [P, P])
                dw_rows = st("dw_rows", [TAPS, D])
                rev_i = st("rev_i", [P, EXPERTS], I32)
                places_i = st("places_i", [P, PLACES], I32)
                with scope() as st:
                    ev_x = st("ev_x", [P, 4, S])
                    ev_z = st("ev_z", [P, 4, S + 2])
                    ev_y = st("ev_y", [P, 4, S])
                    gm_v = st("gm_v", [P, T, 512])
                    gm_u = st("gm_u", [P, T, 512])
                    gm_t = st("gm_t", [P, T, 512])
                    gm_s = st("gm_s", [P, T, 512])
            with scope() as st:
                od_z = st("od_z", [P, T, ODD_IN])
                od_q = st("od_q", [P, T, HEADS, QK])
                od_kv = st("od_kv", [P, T, HEADS, NOPE + VD])
                od_k = st("od_k", [P, T, HEADS, QK])
                cs = st("cs", [P, 2, T, ROPE // 2])
                ang = st("ang", [P, T, ROPE // 2])
                inv_freq = st("inv_freq", [P, ROPE // 2])
                posf = st("posf", [P, T])
                turns = st("turns", [P, T, ROPE // 2])
                sm = st("sm", [P, 2, 3 * P])
                prob = st("prob", [P, 2, 3 * P])
                probT = st("probT", [P, 2, 3 * P])
                nmax = st("nmax", [P, HEADS + MH, T])
                rsum = st("rsum", [P, T, HEADS])
                gts = st("gts", [P, T, 2 * MH])
                lf = st("lf", [P, 3, T, MH])
                acum = st("acum", [P, T, MH])
                bcol = st("bcol", [P, T, MH])
                emt = st("emt", [P, T, MH])
                den = st("den", [P, 2, T])
            with scope() as st:
                ff_th = st("ff_th", [P, T, BLK])
                ff_a = st("ff_a", [P, T, BLK])
                ff_hid = st("ff_hid", [P, T, BLK])
                ff_hidT_hi = st("ff_hidT_hi", [P, 2, S], F32R)
                ff_hidT_lo = st("ff_hidT_lo", [P, 2, S], F32R)
                ada_acc = st("ada_acc", [P, 6 * D])
                ada_w = st("ada_w", [P, ADA_BUFFERS, KC // 2, BLK])
            with scope() as st:
                u_pad = st("u_pad", [P, KC, S + TAPS - 1])
                cf_th = st("cf_th", [P, 2, S])
                cf_a = st("cf_a", [P, 2, S])
                cf_r = st("cf_r", [P, 4, S])
                diag = st("diag", [P, DIAGS, P])
                half = st("half", [P, 4 * KC])
        with scope() as experts:
            early_rows = experts("early_rows", [P, KC // 2, 2, EXPERT_HID])
            odd_expert = experts("odd_expert", [P, SLOTS * SLOT])
            f_bc = experts("f_bc", [P, D])
            place = experts("place", [P, T, EXPERTS])
            crowded = experts("crowded", [P, 1], I32)
            early_down_rows = experts("early_down_rows", [P, EARLY_DOWN_ROWS, D])
            with scope() as st:
                rt = st("rt", [P, 9, T, EXPERTS])
                rts = st("rts", [P, 11, T])
            with scope() as st:
                ge_sel = st("ge_sel", [P, T, P])
                ge_share = st("ge_share", [P, T, P])
                ge_xT = st("ge_xT", [P, KC, P])
                ge_th = st("ge_th", [P, 2, BLK])
                ge_a = st("ge_a", [P, BLK])
                ge_hid = st("ge_hid", [P, 2, BLK])
                ge_hidT = st("ge_hidT", [P, 2, 2, P])
                ge_shareT = st("ge_shareT", [P, T, P])
                ge_y = st("ge_y", [P, 2, 512])
            with scope() as st:
                all_th = st("all_th", [P, T, BLK])
                all_a = st("all_a", [P, T, BLK])
                all_hid = st("all_hid", [P, 2, T, BLK])
                all_hidT = st("all_hidT", [P, 2, S])
        ple_th, ple_a = (mixT[:, i * KC // 2:(i + 1) * KC // 2, :].rearrange("p k s -> p (k s)").rearrange("p (t n) -> p t n", t=T)
                         for i in range(2))
        mqkT = wsT[:].rearrange("p h n -> p (h n)").rearrange("p (c s) -> p c s", c=4)
        lat = xn[:, :, 0:Q_LORA + KV_LORA]
        latT = mixT[:, 0:5, :]
        qT, kT = hnT, mixT
        v_aug = od_q[:].rearrange("p t h d -> p (t h d)")[:, 0:T * MH * (MV + 1)].rearrange(
            "p (t h d) -> p t h d", t=T, h=MH)
        b_masked = od_k[:].rearrange("p t h d -> p (t h d)").rearrange("p (h n) -> p h n", h=MH)
        diag_b = xn[:].rearrange("p t d -> p (t d)")[:, 0:T * MH * P].rearrange("p (t h n) -> p t h n", t=T, h=MH)
        mix = xn
        y_d = mix[:, :, HEADS * VD:].rearrange("p t (h d) -> p t h d", h=MH)
        a_landed = [sem(f"weights_a_landed{s}") for s in range(SLOTS)]
        b_landed = [sem(f"weights_b_landed{s}") for s in range(SLOTS)]
        hi_ready = sem("pieces_hi_ready")
        piece_ready = sem("pieces_ready")
        pieces_used = sem("pieces_used")
        ple_used = sem("ple_proj_used")
        up_used = sem("od_up_used")
        gu_landed = [sem(f"experts_gate_up_landed{s}") for s in range(2)]
        down_landed = [sem(f"experts_down_landed{s}") for s in range(2)]
        gu_used, down_used = sem("experts_gate_up_used"), sem("experts_down_used")
        early_landed = sem("early_expert_landed")
        stage_over = sem("stage_over")
        small_landed = sem("small_landed")
        out_landed = sem("out_landed")
        dve_own = sem("dve_own")
        h_ready = sem("h_ready")
        ada_landed = [sem(f"ada_landed{s}") for s in range(ADA_BUFFERS)]
        ada_used = sem("ada_used")
        ends = {}

        def stage_end(eng):
            ends[id(eng)] = ends.get(id(eng), 0) + 1
            eng.drain().then_inc(stage_over, 1)
            eng.wait_ge(stage_over, 4 * ends[id(eng)])

        def per_round(value, it, count):
            return value if it is None else value + count * it

        def part_a(name, i, n=AT_DOWN):
            return ring[(A.first[name] + i) % SLOTS][:, 0:n]

        def part_b(name, i):
            return ring[(B.first[name] + i) % SLOTS][:, AT_DOWN:SLOT]

        def wait_a(eng, name, i, it=None):
            at = A.first[name] + i
            eng.wait_ge(a_landed[at % SLOTS], per_round(A.landed[at], it, 32 * FF_ROUND // SLOTS))

        def wait_b(eng, name, i, it=None):
            at = B.first[name] + i
            eng.wait_ge(b_landed[at % SLOTS], per_round(B.landed[at], it, 16 * FF_ROUND // SLOTS))

        def width(name, i):
            return min(512, ODD_IN - 512 * i) if name == "od_in" else 512

        def piece(name, i, j):
            if j >= 4:
                return part_b(name, i)[:, (j - 4) * PIECE:(j - 3) * PIECE]
            n = width(name, i)
            if name == "ev_in" and i >= 2:
                return part_a(name, i).rearrange("p (k n) -> p k n", k=KC)[:, :, j * P:(j + 1) * P]
            if name == "conv_in":
                ag = part_a(name, i).rearrange("p (k two n) -> p k two n", k=KC, two=2)
                return ag[:, :, j % 2, (j // 2) * P:(j // 2 + 1) * P]
            return part_a(name, i)[:, 2 * n * j:2 * n * (j + 1)]

        def split_view(parts, name, i, j):
            v = parts[:, PIECE_AT[name, i, j] % BUFFERS]
            if (name == "ev_in" and i >= 2) or name == "conv_in":
                return v.rearrange("p (k n) -> p k n", k=KC)
            return v if j >= 4 else v[:, 0:2 * width(name, i)]

        def split_hi(act, name, i, j, it=None):
            at = PIECE_AT[name, i, j]
            if j == 0:
                wait_a(act, name, i, it)
            elif j == 4:
                wait_b(act, name, i, it)
            if at >= BUFFERS:
                act.wait_ge(pieces_used, per_round(at - BUFFERS + 1, it, FF_ROUND * FF_PIECES))
            act.copy(split_view(w_hi, name, i, j), piece(name, i, j)).then_inc(hi_ready, 1)

        def split_lo(dve, name, i, j, it=None):
            dve.wait_ge(hi_ready, per_round(PIECE_AT[name, i, j] + 1, it, FF_ROUND * FF_PIECES))
            dve.tensor_tensor(split_view(w_lo, name, i, j), piece(name, i, j), split_view(w_hi, name, i, j).bitcast(F32),
                              ALU.subtract).then_inc(piece_ready, 1)

        split_done = {}

        def split_upto(eng, split, name, i, j, ahead=BUFFERS - 1):
            for at in range(split_done.get(id(eng), 0), min(PIECE_AT[name, i, j] + ahead + 1, len(PIECES))):
                split(eng, *PIECES[at])
                split_done[id(eng)] = at + 1

        def split_counted(eng, name, i, j):
            split_done[id(eng)] = PIECE_AT[name, i, j] + 1

        def halves(pe, name, i, j, it=None):
            pe.wait_ge(piece_ready, per_round(PIECE_AT[name, i, j] + 1, it, FF_ROUND * FF_PIECES))
            return split_view(w_hi, name, i, j), split_view(w_lo, name, i, j)

        def wait_used(eng, name, i, j, it=None):
            eng.wait_ge(pieces_used, per_round(PIECE_AT[name, i, j] + 1, it, FF_ROUND * FF_PIECES))

        def three_passes(pe, out, left, right, start, stop):
            pe.matmul(out, left[1], right[0], start=start, stop=False)
            pe.matmul(out, left[0], right[1], start=False, stop=False)
            return pe.matmul(out, left[0], right[0], start=False, stop=stop)

        def tokens_by_columns(pe, name, i, banks, n=512, rest=None, chunks=None):
            for j in range(4):
                w = [v.rearrange("p (k n) -> p k n", k=2) for v in halves(pe, name, i, j)]
                if j == 2 and rest is not None:
                    rest()
                if chunks is not None:
                    pe.wait_ge(chunks, 2 * (j + 1))
                for kk in range(2):
                    for t in range(T):
                        x = [v[:, 2 * j + kk, t * P:(t + 1) * P] for v in (xT_hi, xT_lo)]
                        last = three_passes(pe, ps[:, banks[t], 0:n], x, [v[:, kk, :] for v in w],
                                            start=(j == 0 and kk == 0), stop=(j == 3 and kk == 1))
                last.then_inc(pieces_used, 1)

        def columns_by_tokens(pe, out, w):
            for k in range(KC):
                last = three_passes(pe, out, [v[:, k, :] for v in w], (xT_hi[:, k], xT_lo[:, k]),
                                    start=(k == 0), stop=(k == KC - 1))
            return last

        expert_tiles = [dense_weights[:].rearrange("p s f -> p (s f)"), odd_expert[:]]

        def gate_up_of(e):
            return expert_tiles[e % 2][:, 0:KC * 2 * EXPERT_HID].rearrange("p (k two f) -> p k two f", k=KC, two=2)

        def down_of(e):
            return expert_tiles[e % 2][:, KC * 2 * EXPERT_HID:].rearrange("p (c d) -> p c d", d=D)

        def gate_up_chunks(flat):
            return flat.rearrange("p (k two f) -> p k two f", two=2, f=EXPERT_HID)

        early_gate_up = [(early_rows[:], k) for k in range(KC // 2)]
        for memory in (mixT[:].rearrange("p k s -> p (k s)"), wsT[:].rearrange("p h n -> p (h n)"),
                       pT[:].rearrange("p l c s -> p (l c s)")):
            view = gate_up_chunks(memory)
            early_gate_up += [(view, k) for k in range(view.shape[1])]
        first_places = 2
        early_down = [(early_down_rows[:], c) for c in range(EARLY_DOWN_ROWS)] + [(g_bc[:, 0:1], 0)]

        def gate_up_rows(e, k):
            view, k = early_gate_up[k] if e == EARLY else (gate_up_of(e), k)
            return view[:, k]

        def down_rows(e, c):
            view, c = early_down[c] if e == EARLY else (down_of(e), c)
            return view[:, c]

        def tile_turn(e):
            return e // 2 + 1 - (e > EARLY and e % 2 == EARLY % 2)

        def wait_gate_up(eng, e, it=None):
            if e == EARLY:
                eng.wait_ge(early_landed, 16 * EARLY_DMAS)
            else:
                eng.wait_ge(gu_landed[e % 2], per_round(32 * tile_turn(e), it, 32))

        def wait_down(eng, e, it=None):
            if e == EARLY:
                eng.wait_ge(early_landed, 16 * EARLY_DMAS)
            else:
                eng.wait_ge(down_landed[e % 2], per_round(16 * tile_turn(e), it, 16))

        def cols8(tile, n=512):
            return tile[:, 0:KC * n].rearrange("p (k n) -> p k n", k=KC)

        def weight_stream(sp):
            def wait_split(name, i, j, it):
                sp.wait_ge(piece_ready, per_round(PIECE_AT[name, i, j] + 1, it, FF_ROUND * FF_PIECES))

            def before(part, name, i):
                at = part.first[name] + i - SLOTS
                if at < 0:
                    return None, None
                stage = [row[0] for row in ITEMS if row[2 if part is A else 3] and part.first[row[0]] <= at][-1]
                return stage, at - part.first[stage]

            def load_a(name, i, dst, srcs, it=None):
                stage, k = before(A, name, i)
                if stage == "od_up":
                    sp.wait_ge(up_used, 1)
                elif stage is not None:
                    wait_split(stage, k, 3, it)
                for d, src in zip(dst, srcs):
                    sp.dma_start(d, src).then_inc(a_landed[(A.first[name] + i) % SLOTS], 16)

            def load_b(name, i, dst, src, it=None):
                stage, k = before(B, name, i)
                if stage == "od_up":
                    sp.wait_ge(up_used, 1)
                elif stage is not None and stage.startswith("ple"):
                    sp.wait_ge(ple_used, 2 * int(stage[-1]) + k + 1)
                elif stage is not None:
                    wait_split(stage, k, 5, it)
                sp.dma_start(dst, src).then_inc(b_landed[(B.first[name] + i) % SLOTS], 16)

            def columns(name, w, starts):
                wv = w.rearrange("(k p) n -> p k n", p=P)
                for i, c in enumerate(starts):
                    if name == "ev_in" and i == 1:
                        setup.load_rest(sp)
                    n = width(name, i)
                    load_a(name, i, [cols8(part_a(name, i, KC * n), n)], [wv[:, :, c:c + n]])

            def two_sided(name, i):
                ag = part_a(name, i).rearrange("p (k two n) -> p k two n", k=KC, two=2)
                return [ag[:, :, side, :] for side in range(2)]

            def ffn(layer):
                name = f"ffn{layer}"
                g = a["w_gate"][layer].rearrange("(k p) f -> p k f", p=P)
                u = a["w_up"][layer].rearrange("(k p) f -> p k f", p=P)
                d = a["w_down"][layer].rearrange("(n c p) d -> p n c d", p=P, c=2)

                def block(n, it):
                    m = n if it is None else n + FF_ROUND * it
                    cut = bass.ds(m * BLK, BLK)
                    load_a(name, n, two_sided(name, n), [g[:, :, cut], u[:, :, cut]], it)
                    load_b(name, n, part_b(name, n).rearrange("p (c d) -> p c d", c=2), d[:, m], it)
                for n in range(3):
                    block(n, None)
                with sp.Fori(0, (FF_BLOCKS - 3) // FF_ROUND) as it:
                    for n in range(3, 3 + FF_ROUND):
                        block(n, it)

            def ple(layer):
                name = f"ple{layer}"
                w = a["w_ple_gate"][layer].rearrange("(k p) n -> p k n", p=P)
                q = a["w_ple_proj"][layer].rearrange("(k p) n -> p k n", p=P)
                for i in range(2):
                    load_a(name, i, [cols8(part_a(name, i))], [w[:, :, i * 512:(i + 1) * 512]])
                    load_b(name, i, part_b(name, i)[:, 0:2 * 512].rearrange("p (k n) -> p k n", k=2),
                           q[:, :, i * 512:(i + 1) * 512])

            columns("ev_in", a["ev_w_in"][0], [2048, 1536, 512, 1024, 0])
            columns("ev_out", a["ev_w_out"][0], [0, 512])
            ffn(0)
            ple(0)
            columns("od_in", a["od_w_in"][0], range(0, ODD_IN, 512))
            load_a("od_up", 0, [part_a("od_up", 0, 3 * 768).rearrange("p (k n) -> p k n", k=3)],
                   [a["od_w_q_up"][0].rearrange("(k p) n -> p k n", p=P)])
            load_b("od_up", 0, part_b("od_up", 0).rearrange("p (k n) -> p k n", k=2),
                   a["od_w_kv_up"][0].rearrange("(k p) n -> p k n", p=P))
            columns("od_out", a["od_w_out"][0], [0, 512])
            ffn(1)
            ple(1)
            w = a["conv_w_in_2"][0].rearrange("(k p) n -> p k n", p=P)
            for i in range(4):
                load_a("conv_in", i, two_sided("conv_in", i), [w[:, :, j * D + i * BLK:j * D + (i + 1) * BLK] for j in range(2)])
            columns("conv_out", a["conv_w_out_2"][0], [0, 512])

            g = a["moe_w_gate_2"][0].rearrange("e (k p) f -> p e k f", p=P)
            u = a["moe_w_up_2"][0].rearrange("e (k p) f -> p e k f", p=P)
            d = a["moe_w_down_2"][0].rearrange("e (c p) d -> p e c d", p=P)

            def gate_up(e, it):
                for side, w in enumerate((g, u)):
                    sp.dma_start(gate_up_of(e)[:, :, side, :], w[:, per_round(e, it, 2)]).then_inc(gu_landed[e % 2], 16)

            def down(e, it):
                sp.dma_start(down_of(e), d[:, per_round(e, it, 2)]).then_inc(down_landed[e % 2], 16)

            def early_expert(chunks):
                for first in [k for k in chunks if early_gate_up[k][1] == 0]:
                    view = early_gate_up[first][0]
                    for side, w in enumerate((g, u)):
                        sp.dma_start(view[:, :, side, :], w[:, EARLY, first:first + view.shape[1]]).then_inc(early_landed, 16)

            sp.wait_ge(ple_used, 4)
            early_expert(range(KC - first_places, KC))
            wait_split("conv_out", 1, 3, None)
            gate_up(0, None)
            down(0, None)
            sp.wait_ge(h_ready, 14)
            gate_up(1, None)
            down(1, None)
            early_expert(range(0, KC - first_places))
            sp.dma_start(early_down_rows[:], d[:, EARLY, 0:EARLY_DOWN_ROWS]).then_inc(early_landed, 16)
            sp.dma_start(g_bc[:, 0], d[:, EARLY, EARLY_DOWN_ROWS]).then_inc(early_landed, 16)
            assert EARLY == 3
            sp.wait_ge(gu_used, 1)
            gate_up(2, None)
            sp.wait_ge(gu_used, 2)
            gate_up(5, None)
            sp.wait_ge(down_used, 1)
            down(2, None)
            down(5, None)
            sp.wait_ge(gu_used, 3)
            gate_up(4, None)
            sp.wait_ge(down_used, 2)
            down(4, None)
            with sp.Fori(0, EXPERTS // 2 - 3) as it:
                for e in range(2):
                    sp.wait_ge(gu_used, per_round(5 + e, it, 2))
                    gate_up(6 + e, it)
                sp.wait_ge(down_used, it + 3)
                for e in range(2):
                    down(6 + e, it)

        def rsqrt(dve, own, x, y, t0, t1, done=None):
            own(dve.tensor_scalar(x, x, EPS, None, ALU.add))
            own(dve.tensor_scalar(t0.bitcast(I32), x.bitcast(I32), 1, None, ALU.logical_shift_right))
            own(dve.tensor_scalar(y.bitcast(I32), t0.bitcast(I32), -1.0, float(0x5F3759DF), ALU.mult, ALU.add))
            for i in range(3):
                own(dve.tensor_tensor(t0, y, y, ALU.mult))
                own(dve.scalar_tensor_tensor(out=t1, in0=t0, scalar=-0.5, in1=x, op0=ALU.mult, op1=ALU.mult))
                last = dve.scalar_tensor_tensor(out=y, in0=t1, scalar=1.5, in1=y, op0=ALU.add, op1=ALU.mult)
                if i < 2 or done is None:
                    own(last)
            if done is not None:
                last.then_inc(done, 1)

        def rsqrt_ms(dve, own, n, done=None):
            rsqrt(dve, own, ms[:, 0:n], rs[:, 0:n], rtmp[:, 0, 0:n], rtmp[:, 1, 0:n], done)

        class NormStage:
            squares, made, scaled, turned, hi, ready, whole = (sem("norm_" + n) for n in (
                "squares", "made", "scaled", "turned", "hi", "ready", "whole"))

            def __init__(self, index, gain, shift=None, folded=False, split=True):
                self.index, self.gain, self.shift, self.folded, self.split = index, gain, shift, folded, split
                self.scaled_before = T * sum(1 for i in (0, 6, 7) if i < index)

            def source(self, c):
                return ps[:, c // 2, (c % 2) * S:(c % 2 + 1) * S]

            def act(self, act, split_ahead=None, gains=None):
                if not self.folded:
                    self.sum_squares(act)
                    act.wait_ge(self.made, self.index + 1)
                    act.activation(xn[:, 0], h[:, 0], ACT.Copy, scale=rstd[:, 0, 0:1]).then_inc(self.scaled, 1)
                if split_ahead is not None:
                    split_upto(act, split_hi, *split_ahead, ahead=0)
                if gains is not None:
                    gains(act)
                if not self.split:
                    for c in (2, 3, 6, 7):
                        act.wait_ge(self.turned, 4 * self.index + c // 2 + 1)
                        last = act.activation(hnT[:, c], self.source(c), ACT.Identity, scale=self.gain(c), bias=self.shift(c))
                    last.then_inc(self.whole, 1)
                else:
                    for c in range(KC):
                        if c % 2 == 0:
                            act.wait_ge(self.turned, 4 * self.index + c // 2 + 1)
                        bias = 0.0 if self.shift is None else self.shift(c)
                        act.activation(xT_hi[:, c], self.source(c), ACT.Identity, scale=self.gain(c), bias=bias).then_inc(self.hi, 1)
                if self.folded:
                    self.sum_squares(act)

            def sum_squares(self, act):
                if self.index:
                    act.wait_ge(h_ready, 2 * self.index)
                else:
                    act.wait_ge(setup.h_landed, 16)
                for t in range(T):
                    act.activation(xn[:, t], h[:, t], ACT.Square, scale=float(D) ** -0.5,
                                   accum_out=ms[:, t:t + 1]).then_inc(self.squares, 1)

            def dve(self, dve, own, split_ahead=None, gains=None):
                if not self.folded:
                    self.factors(dve, own)
                    dve.wait_ge(self.made, self.index + 1)
                    dve.tensor_scalar(xn[:, 1], h[:, 1], rstd[:, 0, 1:2], None, ALU.mult).then_inc(self.scaled, 1)
                if gains is not None:
                    gains(dve)
                if split_ahead is not None:
                    split_upto(dve, split_lo, *split_ahead, ahead=0)
                for c in range(KC) if self.split else (0, 1, 4, 5):
                    if c % 2 == 0:
                        dve.wait_ge(self.turned, 4 * self.index + c // 2 + 1)
                        if self.split:
                            dve.wait_ge(self.hi, KC * self.index + c + 2)
                    if self.shift is not None:
                        whole = dve.tensor_scalar(hnT[:, c], self.source(c), self.gain(c), self.shift(c), ALU.mult, ALU.add)
                        if self.split:
                            own(whole)
                        elif c == 5:
                            whole.then_inc(self.whole, 1)
                    if self.split:
                        hi = xT_hi[:, c].bitcast(F32)
                        if self.shift is None:
                            ins = dve.scalar_tensor_tensor(out=xT_lo[:, c], in0=self.source(c), scalar=self.gain(c), in1=hi,
                                                           op0=ALU.mult, op1=ALU.subtract)
                        else:
                            ins = dve.tensor_tensor(xT_lo[:, c], hnT[:, c], hi, ALU.subtract)
                        ins.then_inc(self.ready, 1)
                if self.folded:
                    self.factors(dve, own)

            def factors(self, dve, own):
                dve.wait_ge(self.squares, T * (self.index + 1))
                rsqrt(dve, own, ms[:, 0:T], rstd[:, 0], rtmp[:, 0, 0:T], rtmp[:, 1, 0:T], None if self.folded else self.made)
                if not self.folded:
                    return
                own(dve.tensor_scalar(rstd[:, 1], rstd[:, 0], 0.5, None, ALU.mult))
                dve.tensor_tensor(rstd[:, 2], rstd[:, 0], rstd[:, 1], ALU.mult).then_inc(self.made, 1)

            def pe(self, pe, gains=None):
                if not self.folded:
                    pe.wait_ge(self.scaled, self.scaled_before + T)
                if self.index == 0:
                    pe.wait_ge(setup.consts, 1)
                src = h if self.folded else xn
                for b in range(4):
                    if self.folded and b % 2 == 0:
                        pe.wait_ge(h_ready, 2 * self.index - 1 + b // 2)
                    for c in (2 * b, 2 * b + 1):
                        for t in range(T):
                            last = pe.transpose(self.source(c)[:, t * P:(t + 1) * P], src[:, t, c * P:(c + 1) * P], ident[:])
                    last.then_inc(self.turned, 1)
                if gains is not None:
                    gains(pe)
                if self.folded or self.index == 0:
                    pe.wait_ge(self.ready, KC * self.index + KC // 2)
                elif self.split:
                    self.wait_rest(pe)
                else:
                    pe.wait_ge(self.whole, 2)

            def wait_rest(self, pe):
                pe.wait_ge(self.ready, KC * (self.index + 1))

            def wait_factors(self, eng):
                eng.wait_ge(self.made, self.index + 1)

        class FfnStage:
            gate_half_made, hid, turned, hidT_hi, hidT = (sem("ff_" + n) for n in ("half_made", "hid_ready", "turned", "hidT_hi_ready",
                                                                                  "hidT_ready"))
            tanh = sem("ff_tanh")

            def __init__(self, layer, norm, side=None):
                self.name, self.norm = f"ffn{layer}", norm
                self.before = layer * FF_BLOCKS
                self.side = side

            def count(self, blocks, it, per_block=1):
                return per_round(per_block * (self.before + blocks), it, per_block * FF_ROUND)

            def run(self, eng, step):
                step(0, None)
                step(1, None)
                split_counted_at = 2 + FF_ROUND
                with eng.Fori(0, (FF_BLOCKS - 3) // FF_ROUND) as it:
                    for n in range(2, split_counted_at):
                        step(n, it)
                step(FF_BLOCKS - 1, None)

            def pe(self, pe):
                name, last_block = self.name, FF_BLOCKS - 1

                def gate_up(n, it, pieces):
                    for j in pieces:
                        w = [v.rearrange("p (k n) -> p k n", k=2) for v in halves(pe, name, n, j, it)]
                        if n == 0 and j == 2:
                            self.norm.wait_rest(pe)
                        if j == 0 and n >= 1:
                            pe.wait_ge(self.hid, self.count(n, it, T))
                        for kk in range(2):
                            for t in range(T):
                                x = [v[:, 2 * j + kk, t * P:(t + 1) * P] for v in (xT_hi, xT_lo)]
                                last = three_passes(pe, ps[:, t, :], x, [v[:, kk, :] for v in w],
                                                    start=(j == 0 and kk == 0), stop=(j == 3 and kk == 1))
                        last.then_inc(pieces_used, 1)

                def turn(n, it):
                    pe.wait_ge(self.hid, self.count(n + 1, it, T))
                    for c in range(2):
                        for t in range(T):
                            last = pe.transpose(ps[:, 2, c * S + t * P:c * S + (t + 1) * P],
                                                ff_hid[:, t, c * P:(c + 1) * P], ident[:])
                    last.then_inc(self.turned, 1)

                def down(n, it):
                    pe.wait_ge(self.hidT, self.count(n + 1, it))
                    for c in range(2):
                        w = halves(pe, name, n, 4 + c, it)
                        for t in range(T):
                            x = [v[:, c, t * P:(t + 1) * P] for v in (ff_hidT_hi, ff_hidT_lo)]
                            for half in range(2):
                                last = three_passes(pe, ps[:, 4 + 2 * t + half, :], x, [v[:, half * 512:(half + 1) * 512] for v in w],
                                                    start=(n == 0 and c == 0), stop=(n == last_block and c == 1))
                        last.then_inc(pieces_used, 1)

                def step(n, it):
                    gate_up(n, it, (0, 1))
                    if n >= 1:
                        turn(n - 1, it)
                    gate_up(n, it, (2, 3))
                    if n >= 1:
                        down(n - 1, it)

                self.run(pe, step)
                turn(last_block, None)
                down(last_block, None)

            def splits(self, eng, split, n, it, which):
                ahead = [(n, 3), (n - 1, 4), (n - 1, 5), (n + 1, 0), (n + 1, 1), (n + 1, 2)]
                if n == FF_BLOCKS - 1:
                    at = PIECE_AT[self.name, n - 1, 5]
                    ahead[3:] = [PIECES[at + 1], PIECES[at + 2], PIECES[at + 3]]
                for q in which:
                    stage, block, j = ahead[q] if len(ahead[q]) == 3 else (self.name,) + ahead[q]
                    if block >= 0:
                        split(eng, stage, block, j, it)

            def act(self, act):
                split_upto(act, split_hi, self.name, 0, 2, ahead=0)
                self.norm.wait_factors(act)

                def step(n, it):
                    self.splits(act, split_hi, n, it, (0, 1, 2))
                    if n >= 1:
                        copy(n - 1, it)
                    self.splits(act, split_hi, n, it, (3,))
                    wait_used(act, self.name, n, 3, it)
                    for t in range(T):
                        act.activation(ff_th[:, t], ps[:, t, 0:BLK], ACT.Tanh, scale=rstd[:, 1, t:t + 1]).then_inc(self.tanh, 1)
                    self.splits(act, split_hi, n, it, (4, 5))

                def copy(n, it):
                    act.wait_ge(self.turned, self.count(n + 1, it))
                    act.copy(ff_hidT_hi[:], ps[:, 2, :].rearrange("p (c s) -> p c s", c=2)).then_inc(self.hidT_hi, 1)

                self.run(act, step)
                self.rest(act, split_hi, copy)

            def rest(self, eng, split, copy):
                copy(FF_BLOCKS - 1, None)
                at = PIECE_AT[self.name, FF_BLOCKS - 1, 5]
                split_counted(eng, *PIECES[at + 1])
                split_upto(eng, split, *PIECES[at + 3], ahead=0)

            def dve(self, dve, own):
                split_upto(dve, split_lo, self.name, 0, 2, ahead=0)

                def step(n, it):
                    self.splits(dve, split_lo, n, it, (0, 1, 2))
                    if n >= 1:
                        copy(n - 1, it)
                    self.splits(dve, split_lo, n, it, (3,))
                    for t in range(T):
                        dve.wait_ge(self.tanh, self.count(n, it, T) + t + 1)
                        dve.scalar_tensor_tensor(out=ff_a[:, t], in0=ff_th[:, t], scalar=1.0, in1=ps[:, t, 0:BLK],
                                                 op0=ALU.add, op1=ALU.mult).then_inc(self.gate_half_made, 1)
                    for t in range(T):
                        dve.wait_ge(self.gate_half_made, self.count(n, it, T) + t + 1)
                        dve.scalar_tensor_tensor(out=ff_hid[:, t], in0=ff_a[:, t], scalar=rstd[:, 2, t:t + 1],
                                                 in1=ps[:, t, BLK:2 * BLK], op0=ALU.mult, op1=ALU.mult).then_inc(self.hid, 1)
                    self.splits(dve, split_lo, n, it, (4, 5))
                    if self.side is not None and n < FF_BLOCKS - 1:
                        self.side(dve, n, it)

                def copy(n, it):
                    dve.wait_ge(self.hidT_hi, self.count(n + 1, it))
                    dve.tensor_tensor(ff_hidT_lo[:], ps[:, 2, :].rearrange("p (c s) -> p c s", c=2), ff_hidT_hi[:].bitcast(F32),
                                      ALU.subtract).then_inc(self.hidT, 1)

                self.run(dve, step)
                self.rest(dve, split_lo, copy)
                wait_used(dve, self.name, FF_BLOCKS - 1, 5)
                for half in range(2):
                    for t in range(T):
                        o = h[:, t, half * 512:(half + 1) * 512]
                        ins = dve.tensor_tensor(o, o, ps[:, 4 + 2 * t + half, :], ALU.add)
                    ins.then_inc(h_ready, 1)

        class PleStage:
            tanh = sem("ple_tanh")

            def __init__(self, layer, norm, side=None):
                self.layer, self.name, self.norm, self.side = layer, f"ple{layer}", norm, side

            def pe(self, pe):
                for i in range(2):
                    tokens_by_columns(pe, self.name, i, (4 * i, 4 * i + 1), rest=(lambda: self.norm.wait_rest(pe)) if i == 0 else None)
                    wait_b(pe, self.name, i)
                    q = part_b(self.name, i)[:, 0:2 * 512].rearrange("p (k n) -> p k n", k=2)
                    for t in range(T):
                        for k in range(2):
                            last = pe.matmul(ps[:, 4 * i + 2 + t, :], pT[:, self.layer, k, t * P:(t + 1) * P],
                                             q[:, k, :], start=(k == 0), stop=(k == 1))
                    last.then_inc(ple_used, 1)

            def act(self, act):
                split_upto(act, split_hi, self.name, 0, 2, ahead=0)
                self.norm.wait_factors(act)
                for i in range(2):
                    split_upto(act, split_hi, self.name, i, 3)
                    wait_used(act, self.name, i, 3)
                    for t in range(T):
                        if i > 0:
                            act.wait_ge(self.used, 2 * (2 * self.layer + i - 1) + t + 1)
                        act.activation(ple_th[:, t], ps[:, 4 * i + t, :], ACT.Tanh,
                                       scale=rstd[:, 1, t:t + 1]).then_inc(self.tanh, 1)

            used = sem("ple_tanh_used")

            def dve(self, dve, own):
                for i in range(2):
                    split_upto(dve, split_lo, self.name, i, 3)
                    if self.side is not None:
                        self.side(dve, i)
                    dve.wait_ge(ple_used, 2 * self.layer + i + 1)
                    for t in range(T):
                        n = 2 * (2 * self.layer + i) + t + 1
                        dve.wait_ge(self.tanh, n)
                        dve.scalar_tensor_tensor(out=ple_a[:, t], in0=ple_th[:, t], scalar=1.0, in1=ps[:, 4 * i + 2 + t, :],
                                                 op0=ALU.add, op1=ALU.mult).then_inc(self.used, 1)
                        dve.wait_ge(self.used, n)
                        o = h[:, t, i * 512:(i + 1) * 512]
                        ins = dve.scalar_tensor_tensor(out=o, in0=ple_a[:, t], scalar=0.5, in1=o, op0=ALU.mult, op1=ALU.add)
                    ins.then_inc(h_ready, 1)

        class SetupStage:
            def __init__(self):
                self.rows_landed = sem("rows_landed")
                self.columns_made = sem("columns_made")
                self.copied = sem("setup_copied")
                self.consts = sem("consts_made")
                self.own_consts = sem("consts_under_way")
                self.turned = sem("setup_turned")
                self.h_landed = sem("h_landed")

            def loads(self):
                for name, dst in (("ev_g_v", g_v), ("od_g_mh", g_mh)):
                    yield dst[:], a[name][0].rearrange("h d -> (h d)").partition_broadcast(P)
                yield g_q[:], a["od_g_q"][0].partition_broadcast(P)
                yield g_k[:], a["od_g_k"][0].partition_broadcast(P)
                yield b_gate[:], a["od_b_gate"][0].partition_broadcast(P)
                yield b_route[:, 0:GROUPS], a["moe_b_rg_2"][0].partition_broadcast(P)
                yield b_route[:, GROUPS:], a["moe_b_re_2"][0].partition_broadcast(P)
                yield w_route[:, :, 0:GROUPS], a["moe_w_rg_2"][0].rearrange("(k p) n -> p k n", p=P)
                yield w_route[:, :, GROUPS:], a["moe_w_re_2"][0].rearrange("(k p) n -> p k n", p=P)
                yield pos_i[:], a["positions"].rearrange("b (t p) -> p (b t)", p=P)
                yield ws_rows[:], a["ev_w_s"][0].rearrange("h t s -> t h s")
                for layer in range(2):
                    yield p_rows[:, layer], a["p"][layer, 0].rearrange("(t p) d -> p t d", p=P)
                yield dw_rows[:], a["conv_w_dw_2"][0]
                yield from self.rows(ROWS_B, rows_b)

            def rows(self, rows, tile):
                for name, (at, n) in rows.items():
                    v = a[name]
                    flat = v.rearrange(" ".join("abcd"[:len(v.shape)]) + " -> (" + " ".join("abcd"[:len(v.shape)]) + ")")
                    yield tile[at:at + n, :], flat.rearrange("(c p) -> c p", p=P)

            def load_stream(self, sp):
                sp.dma_start(h[:], a["x"][0].rearrange("(t p) d -> p t d", p=P)).then_inc(self.h_landed, 16)

            def load_rest(self, sp):
                for dst, src in self.rows(ROWS_A, rows_a):
                    sp.dma_start(dst, src).then_inc(self.rows_landed, 16)
                for dst, src in self.loads():
                    sp.dma_start(dst, src, allow_slow_non_contiguous=dst.dtype == I32).then_inc(small_landed, 16)

            def act_columns(self, act):
                act.wait_ge(self.turned, 1)
                act.copy(cols_a[:, 0:N_ROWS_A], ps[:, 4, 0:N_ROWS_A]).then_inc(self.columns_made, 1)
                act.wait_ge(self.columns_made, 1)

            def act_rest(self, act):
                act.wait_ge(self.turned, 2)
                act.copy(wsT[:, 0:4], ps[:, 4, :].rearrange("p (h n) -> p h n", h=4)).then_inc(self.copied, 1)
                act.wait_ge(self.turned, 3)
                act.copy(wsT[:, 4:8], ps[:, 5, :].rearrange("p (h n) -> p h n", h=4)).then_inc(self.copied, 1)
                act.wait_ge(self.turned, 4)
                act.copy(pT[:, 0], ps[:, 7, :].rearrange("p (c s) -> p c s", c=2)).then_inc(self.copied, 1)
                act.wait_ge(self.turned, 5)
                act.copy(cols_b[:, 0:N_ROWS_B], ps[:, 6, 0:N_ROWS_B])
                act.copy(w_dw[:], ps[:, 6, P:P + KC * TAPS].rearrange("p (c j) -> p c j", c=KC)).then_inc(self.copied, 1)
                act.wait_ge(self.turned, 6)
                act.copy(pT[:, 1], ps[:, 4, :].rearrange("p (c s) -> p c s", c=2)).then_inc(self.copied, 1)
                act.wait_ge(self.copied, 4)
                act.activation(c_act[:], col("c_2", 0, KC), ACT.Tanh, scale=0.5).then_inc(self.copied, 1)

            def pool(self, pool):
                own = Own(pool, self.own_consts)
                own(pool.memset(ident[:], 0.0))
                own(pool.affine_select(out=ident[:], in_=ident[:], compare_op=ALU.not_equal, fill=1.0, base=0,
                                       pattern=[[-1, P]], channel_multiplier=1))
                own(pool.memset(ones[:], 1.0))
                pool.memset(cmask[:], 0.0).then_inc(self.consts, 1)
                pool.wait_ge(self.consts, 1)
                pool.memset(mean_w[:], 1.0 / D)
                pool.iota(rev_i[:], pattern=[[-1, EXPERTS]], base=EXPERTS, channel_multiplier=0)
                pool.iota(places_i[:], pattern=[[1, PLACES]], base=0, channel_multiplier=0)
                own(pool.affine_select(out=upper[:], in_=ones[:], compare_op=ALU.is_ge, fill=0.0, base=0,
                                       pattern=[[1, P]], channel_multiplier=-1))
                for at in (0, 2 * P):
                    own(pool.affine_select(out=cmask[:, at:at + P], in_=cmask[:, at:at + P], compare_op=ALU.is_ge,
                                           fill=NEG, base=0, pattern=[[-1, P]], channel_multiplier=1))
                pool.tensor_copy(places[:], places_i[:])
                pool.tensor_copy(rev[:], rev_i[:])
                pool.drain().then_inc(self.consts, 1)

            def pe(self, pe):
                pe.wait_ge(self.rows_landed, 16 * len(ROWS_A))
                pe.transpose(ps[:, 4, 0:N_ROWS_A], rows_a[0:N_ROWS_A, :], ident[0:N_ROWS_A, 0:N_ROWS_A]).then_inc(self.turned, 1)

            def pe_rest(self, pe):
                pe.wait_ge(small_landed, SMALL_LANDED)
                for hd in range(GM_HEADS):
                    last = pe.transpose(ps[:, 4 + hd // 4, (hd % 4) * P:(hd % 4 + 1) * P], ws_rows[:, hd], ident[:])
                    if hd % 4 == 3:
                        last.then_inc(self.turned, 1)

                def turn_p(layer, bank):
                    for c in range(2):
                        for t in range(T):
                            last = pe.transpose(ps[:, bank, c * S + t * P:c * S + (t + 1) * P],
                                                p_rows[:, layer, t, c * P:(c + 1) * P], ident[:])
                    last.then_inc(self.turned, 1)

                turn_p(0, 7)
                pe.transpose(ps[:, 6, 0:N_ROWS_B], rows_b[0:N_ROWS_B, :], ident[0:N_ROWS_B, 0:N_ROWS_B])
                for c in range(KC):
                    last = pe.transpose(ps[:, 6, P + c * TAPS:P + (c + 1) * TAPS], dw_rows[:, c * P:(c + 1) * P],
                                        ident[0:TAPS, 0:TAPS])
                last.then_inc(self.turned, 1)
                pe.wait_ge(self.copied, 1)
                turn_p(1, 4)
                pe.wait_ge(self.copied, 5)

            def dve_rest(self, dve, own):
                dve.wait_ge(self.copied, 6)
                dve.wait_ge(self.consts, 2)
                own(dve.tensor_tensor(wsT[:], wsT[:], upper[:].unsqueeze(1).to_broadcast([P, GM_HEADS, P]), ALU.mult))
                own(dve.scalar_tensor_tensor(out=c_act[:], in0=c_act[:], scalar=1.0, in1=col("c_2", 0, KC), op0=ALU.add,
                                             op1=ALU.mult))
                own(dve.tensor_scalar(c_act[:], c_act[:], 0.5, None, ALU.mult))

        class EvenStage:
            def __init__(self):
                self.v_copied = sem("ev_v_copied")
                self.u_copied = sem("ev_u_copied")
                self.x_copied = sem("ev_x_copied")
                self.v_tanh_in = sem("ev_v_tanh_in")
                self.v_tanh = sem("ev_v_tanh")
                self.u_tanh_in = sem("ev_u_tanh_in")
                self.u_tanh = sem("ev_u_tanh")
                self.vn = sem("ev_vn")
                self.mixed = sem("ev_mixed")
                self.y_b = sem("ev_y_b")
                self.y_turned = sem("ev_y_turned")
                self.mixT_ready = sem("ev_mixT_ready")
                self.mix_hi = sem("ev_mix_hi")
                self.mix_split = sem("ev_mix_split")

            def pe(self, pe):
                for i in range(2):
                    tokens_by_columns(pe, "ev_in", i, (2 * i, 2 * i + 1), rest=(lambda: norms[0].wait_rest(pe)) if i == 0 else None)
                setup.pe_rest(pe)
                for i in range(3):
                    if i == 2:
                        pe.wait_ge(self.v_copied, 1)
                    for f in range(4):
                        at = ps[:, (4, 6, 0)[i] + f // 2, (f % 2) * S:(f % 2 + 1) * S]
                        columns_by_tokens(pe, at, halves(pe, "ev_in", 2 + i, f)).then_inc(pieces_used, 1)
                pe.wait_ge(self.vn, 1)
                pe.wait_ge(self.u_copied, 1)
                for t in range(T):
                    for hd in range(GM_HEADS):
                        last = pe.matmul(ps[:, 2 + t, hd * GM_HD:(hd + 1) * GM_HD], wsT[:, hd, :],
                                         gm_v[:, t, hd * GM_HD:(hd + 1) * GM_HD], start=True, stop=True)
                last.then_inc(self.mixed, 1)
                pe.wait_ge(self.y_b, 1)
                for c in range(4):
                    for t in range(T):
                        at = (c % 2) * S + t * P
                        last = pe.transpose(ps[:, 4 + c // 2, at:at + P], gm_s[:, t, c * P:(c + 1) * P], ident[:])
                last.then_inc(self.y_turned, 1)
                pe.wait_ge(self.mix_split, 2)
                for i in range(2):
                    tokens_by_columns(pe, "ev_out", i, (6 - 2 * i, 7 - 2 * i))

            def act(self, act):
                split_upto(act, split_hi, "ev_in", 0, 3)
                wait_used(act, "ev_in", 0, 3)
                act.copy(gm_v[:], ps[:, 0:2, :]).then_inc(self.v_copied, 1)
                split_upto(act, split_hi, "ev_in", 1, 3)
                wait_used(act, "ev_in", 1, 3)
                act.copy(gm_u[:], ps[:, 2:4, :]).then_inc(self.u_copied, 1)
                setup.act_rest(act)
                split_upto(act, split_hi, "ev_in", 2, 3)
                act.wait_ge(self.v_tanh_in, 1)
                act.activation(gm_t[:], gm_t[:], ACT.Tanh, scale=0.7978845608028654).then_inc(self.v_tanh, 1)
                split_upto(act, split_hi, "ev_in", 3, 3)
                wait_used(act, "ev_in", 3, 3)
                act.copy(ev_x[:], ps[:, 6:8, :].rearrange("p b (c s) -> p (b c) s", c=2)).then_inc(self.x_copied, 1)
                act.wait_ge(self.u_tanh_in, 1)
                act.activation(gm_s[:], gm_s[:], ACT.Tanh, scale=0.7978845608028654).then_inc(self.u_tanh, 1)
                split_upto(act, split_hi, "ev_out", 0, 2, ahead=0)
                act.wait_ge(self.mixT_ready, 1)
                act.copy(xT_hi[:, 0:4, :], mixT[:, 0:4, :]).then_inc(self.mix_hi, 1)
                act.wait_ge(self.y_turned, 1)
                act.copy(xT_hi[:, 4:8, :], ps[:, 4:6, :].rearrange("p b (c s) -> p (b c) s", c=2)).then_inc(self.mix_hi, 1)
                split_upto(act, split_hi, "ev_out", 1, 3)

            def dve(self, dve, own):
                def gelu_in(x, t, done):
                    own(dve.tensor_tensor(t, x, x, ALU.mult))
                    own(dve.tensor_scalar(t, t, 0.044715, 1.0, ALU.mult, ALU.add))
                    dve.tensor_tensor(t, t, x, ALU.mult).then_inc(done, 1)

                own(dve.memset(ev_z[:, :, 0:2], 0.0))
                split_upto(dve, split_lo, "ev_in", 0, 3)
                dve.wait_ge(self.v_copied, 1)
                gelu_in(gm_v[:], gm_t[:], self.v_tanh_in)
                split_upto(dve, split_lo, "ev_in", 1, 3)
                dve.wait_ge(self.u_copied, 1)
                gelu_in(gm_u[:], gm_s[:], self.u_tanh_in)
                setup.dve_rest(dve, own)
                split_upto(dve, split_lo, "ev_in", 2, 1)
                dve.wait_ge(self.v_tanh, 1)
                own(dve.scalar_tensor_tensor(out=gm_v[:], in0=gm_t[:], scalar=1.0, in1=gm_v[:], op0=ALU.add, op1=ALU.mult))
                own(dve.tensor_tensor(gm_t[:], gm_v[:], gm_v[:], ALU.mult))
                n = T * GM_HEADS
                split_upto(dve, split_lo, "ev_in", 2, 3)
                own(dve.tensor_reduce(ms[:, 0:n], gm_t[:].rearrange("p t (h d) -> p (t h) d", d=GM_HD), AX.X, ALU.add))
                own(dve.tensor_scalar(ms[:, 0:n], ms[:, 0:n], 0.25 / GM_HD, None, ALU.mult))
                rsqrt_ms(dve, own, n)
                own(dve.tensor_scalar(rs[:, 0:n], rs[:, 0:n], 0.5, None, ALU.mult))
                split_upto(dve, split_lo, "ev_in", 3, 1)
                v3 = gm_v[:].rearrange("p t (h d) -> p (t h) d", d=GM_HD)
                own(dve.tensor_tensor(v3, v3, rs[:, 0:n].unsqueeze(2).to_broadcast([P, n, GM_HD]), ALU.mult))
                dve.tensor_tensor(gm_v[:], gm_v[:], g_v[:].unsqueeze(1).to_broadcast([P, T, 512]),
                                  ALU.mult).then_inc(self.vn, 1)
                split_upto(dve, split_lo, "ev_in", 3, 3)
                dve.wait_ge(self.u_tanh, 1)
                own(dve.scalar_tensor_tensor(out=gm_u[:], in0=gm_s[:], scalar=1.0, in1=gm_u[:], op0=ALU.add, op1=ALU.mult))
                dve.wait_ge(self.x_copied, 1)
                own(dve.tensor_tensor(ev_z[:, :, 2:], ps[:, 4:6, :].rearrange("p b (c s) -> p (b c) s", c=2), ev_x[:],
                                      ALU.mult))
                for j in range(3):
                    for c in range(4):
                        w = col("ev_w_conv", 4 * j + c)
                        if j == 0:
                            own(dve.tensor_scalar(ev_y[:, c], ev_z[:, c, 0:S], w, None, ALU.mult))
                        else:
                            own(dve.scalar_tensor_tensor(out=ev_y[:, c], in0=ev_z[:, c, j:j + S], scalar=w,
                                                         in1=ev_y[:, c], op0=ALU.mult, op1=ALU.add))
                split_upto(dve, split_lo, "ev_out", 0, 2, ahead=0)
                wait_used(dve, "ev_in", 4, 3)
                dve.tensor_tensor(mixT[:, 0:4, :], ps[:, 0:2, :].rearrange("p b (c s) -> p (b c) s", c=2), ev_y[:],
                                  ALU.mult).then_inc(self.mixT_ready, 1)
                dve.wait_ge(self.mixed, 1)
                bias = col("ev_b_s", 0, GM_HEADS).unsqueeze(2).to_broadcast([P, GM_HEADS, GM_HD])
                for t in range(T):
                    own(dve.tensor_tensor(gm_t[:, t].rearrange("p (h d) -> p h d", d=GM_HD),
                                          ps[:, 2 + t, :].rearrange("p (h d) -> p h d", d=GM_HD), bias, ALU.add))
                dve.scalar_tensor_tensor(out=gm_s[:], in0=gm_t[:], scalar=0.5, in1=gm_u[:], op0=ALU.mult,
                                         op1=ALU.mult).then_inc(self.y_b, 1)
                dve.wait_ge(self.mix_hi, 1)
                dve.tensor_tensor(xT_lo[:, 0:4], mixT[:, 0:4], xT_hi[:, 0:4].bitcast(F32), ALU.subtract).then_inc(self.mix_split, 1)
                dve.wait_ge(self.mix_hi, 2)
                dve.tensor_tensor(xT_lo[:, 4:8], ps[:, 4:6, :].rearrange("p b (c s) -> p (b c) s", c=2),
                                  xT_hi[:, 4:8].bitcast(F32), ALU.subtract).then_inc(self.mix_split, 1)
                for i in range(2):
                    split_upto(dve, split_lo, "ev_out", i, 3)
                    wait_used(dve, "ev_out", i, 3)
                    for t in range(T):
                        o = h[:, t, i * 512:(i + 1) * 512]
                        ins = dve.tensor_tensor(o, o, ps[:, 6 - 2 * i + t, :], ALU.add)
                    ins.then_inc(h_ready, 1)

        class OddIn:
            def __init__(self, norm, up):
                self.norm, self.up = norm, up
                self.copied = [sem(f"od_z_copied{t}") for t in range(T)]
                self.freq = sem("od_freq")

            def pe(self, pe):
                for i in range(5):
                    if i == 4:
                        for t in range(T):
                            pe.wait_ge(self.copied[t], 1)
                    tokens_by_columns(pe, "od_in", i, [(2 * i + t) % 8 for t in range(T)], width("od_in", i),
                                      (lambda: self.norm.wait_rest(pe)) if i == 0 else None)

            def wait_z(self, eng, items):
                for t in range(T):
                    eng.wait_ge(self.copied[t], items)

            def act(self, act):
                split_upto(act, split_hi, "od_in", 0, 2, ahead=0)
                self.norm.wait_factors(act)
                for i in range(5):
                    n = width("od_in", i)
                    split_upto(act, split_hi, "od_in", i, 3, BUFFERS - 1 if i < 4 else 0)
                    wait_used(act, "od_in", i, 3)
                    act.activation(od_z[:, 0, 512 * i:512 * i + n], ps[:, (2 * i) % 8, 0:n], ACT.Copy, scale=rstd[:, 0, 0:1]
                                   ).then_inc(self.copied[0], 1)
                    if i == 1:
                        self.wait_z(act, 2)
                        self.up.squares_of(act)
                    if i == 2:
                        self.up.scale_q(act)

            def dve(self, dve, own):
                self.up.turns_of(dve, own, self.freq)
                for i in range(5):
                    n = width("od_in", i)
                    split_upto(dve, split_lo, "od_in", i, 3, BUFFERS - 1 if i < 4 else 0)
                    wait_used(dve, "od_in", i, 3)
                    dve.tensor_scalar(od_z[:, 1, 512 * i:512 * i + n], ps[:, (2 * i + 1) % 8, 0:n], rstd[:, 0, 1:2], None,
                                      ALU.mult).then_inc(self.copied[1], 1)
                    if i == 1:
                        self.wait_z(dve, 2)
                        self.up.factors(dve, own)

            def pool(self, pool):
                pool.wait_ge(h_ready, 6)
                freq = (np.float32(ROPE_THETA) ** (-np.arange(0, ROPE, 2, dtype=np.float32) / np.float32(ROPE))
                        ).astype(np.float32)
                for i in range(ROPE // 2):
                    last = pool.memset(inv_freq[:, i:i + 1], float(freq[i]))
                last.then_inc(self.freq, 1)

        class OddUp:
            def __init__(self):
                self.gate_abs, self.exps, self.logs = sem("od_gate_abs"), sem("od_gate_exp"), sem("od_gate_log")
                self.q_made, self.q_copied, self.kv_copied = sem("od_q_made"), sem("od_q_copied"), sem("od_kv_copied")
                self.squares = sem("od_squares")
                self.rstd = sem("od_rstd")
                self.lat = sem("od_lat")
                self.lat_turned = sem("od_lat_turned")
                self.latT = sem("od_latT")
                self.mqk_turned = sem("od_mqk_turned")
                self.mqk_freed = sem("od_mqk_freed")
                self.angles = sem("od_angles")
                self.trig = sem("od_trig")

            def squares_of(self, act):
                for kind, (at, n) in enumerate(((0, Q_LORA), (Q_LORA, KV_LORA), (AT_KPE, ROPE))):
                    for t in range(T):
                        last = act.activation(xn[:, t, at:at + n], od_z[:, t, at:at + n], ACT.Square, scale=float(n) ** -0.5,
                                              accum_out=ms[:, kind * T + t:kind * T + t + 1])
                last.then_inc(self.squares, 1)

            def scale_q(self, act):
                act.wait_ge(self.rstd, 1)
                for t in range(T):
                    act.activation(lat[:, t, 0:Q_LORA], od_z[:, t, 0:Q_LORA], ACT.Copy,
                                   scale=rs[:, t:t + 1]).then_inc(self.lat, 1)

            def act(self, act):
                act.wait_ge(self.lat_turned, 1)
                for c in range(5):
                    gain = col("od_g_qa", c) if c < 3 else col("od_g_kva", c - 3)
                    last = act.activation(latT[:, c, :], ps[:, 2 + c // 2, (c % 2) * S:(c % 2 + 1) * S], ACT.Copy, scale=gain)
                last.then_inc(self.latT, 1)
                act.wait_ge(self.mqk_turned, 1)
                act.copy(mqkT[:], ps[:, 5:7, :].rearrange("p b (c s) -> p (b c) s", c=2)).then_inc(self.mqk_freed, 1)
                act.wait_ge(self.angles, 1)
                act.activation(cs[:], cs[:], ACT.Sin).then_inc(self.trig, 1)
                act.wait_ge(self.gate_abs, 1)
                act.activation(lf[:, 0], lf[:, 0], ACT.Exp, scale=-1.0).then_inc(self.exps, 1)
                act.wait_ge(self.exps, 1)
                act.activation(lf[:, 1], lf[:, 0], ACT.Ln, bias=1.0).then_inc(self.logs, 1)
                act.wait_ge(self.q_made, 1)
                act.copy(od_q[:].rearrange("p t h d -> p t (h d)").rearrange("p t (a b) -> p (t a) b", a=2),
                         ps[:, 0:4, 0:384]).then_inc(self.q_copied, 1)
                act.wait_ge(up_used, 1)
                act.copy(od_kv[:].rearrange("p t h d -> p t (h d)").rearrange("p t (a b) -> p (t a) b", a=2),
                         ps[:, 4:8, :]).then_inc(self.kv_copied, 1)
                split_upto(act, split_hi, "od_out", 0, 3, ahead=0)

            def turns_of(self, dve, own, freq):
                dve.wait_ge(freq, 1)
                own(dve.tensor_copy(posf[:], pos_i[:]))
                for t in range(T):
                    own(dve.tensor_scalar(ang[:, t], inv_freq[:], posf[:, t:t + 1], None, ALU.mult))
                first_part = 6.25
                second_part = np.floor((2 * np.pi - first_part) * 2.0 ** 19) / 2.0 ** 19
                parts = [first_part, second_part, 2 * np.pi - first_part - second_part]
                big = 1.5 * 2.0 ** 23
                for k, quarter in ((0, 0.25), (1, 0.0)):
                    own(dve.tensor_scalar(turns[:], ang[:], float(1 / (2 * np.pi)), quarter, ALU.mult, ALU.add))
                    own(dve.tensor_scalar(turns[:], turns[:], big, None, ALU.add))
                    own(dve.tensor_scalar(turns[:], turns[:], big, None, ALU.subtract))
                    own(dve.scalar_tensor_tensor(out=cs[:, k], in0=turns[:], scalar=-float(parts[0]), in1=ang[:],
                                                 op0=ALU.mult, op1=ALU.add))
                    for part in parts[1:]:
                        own(dve.scalar_tensor_tensor(out=cs[:, k], in0=turns[:], scalar=-float(part), in1=cs[:, k],
                                                     op0=ALU.mult, op1=ALU.add))
                    if quarter:
                        own(dve.tensor_scalar(cs[:, k], cs[:, k], float(np.pi / 2), None, ALU.add))
                    last = dve.tensor_scalar(cs[:, k], cs[:, k], 3.1415925, -3.1415925, ALU.min, ALU.max)
                    if k == 0:
                        own(last)
                last.then_inc(self.angles, 1)

            def factors(self, dve, own):
                dve.wait_ge(self.squares, 1)
                rsqrt_ms(dve, own, 3 * T, self.rstd)
                dve.wait_ge(self.rstd, 1)
                for t in range(T):
                    dve.tensor_scalar(lat[:, t, Q_LORA:], od_z[:, t, Q_LORA:AT_KPE], rs[:, T + t:T + t + 1], None,
                                      ALU.mult).then_inc(self.lat, 1)
                for t in range(T):
                    kp = od_z[:, t, AT_KPE:AT_KPE + ROPE]
                    own(dve.scalar_tensor_tensor(out=kp, in0=kp, scalar=rs[:, 2 * T + t:2 * T + t + 1], in1=g_k[:, NOPE:],
                                                 op0=ALU.mult, op1=ALU.mult))

            def dve(self, dve, own):
                hr = ROPE // 2
                dve.wait_ge(self.trig, 1)
                for t in range(T):
                    k1, k2 = od_z[:, t, AT_KPE:AT_KPE + hr], od_z[:, t, AT_KPE + hr:AT_KPE + ROPE]
                    r1, r2 = rtmp[:, 0, 0:hr], rtmp[:, 1, 0:hr]
                    cos, sin = cs[:, 0, t], cs[:, 1, t]
                    own(dve.tensor_tensor(r1, k2, sin, ALU.mult))
                    own(dve.tensor_tensor(r2, k1, sin, ALU.mult))
                    own(dve.tensor_tensor(k1, k1, cos, ALU.mult))
                    own(dve.tensor_tensor(k2, k2, cos, ALU.mult))
                    own(dve.tensor_tensor(k1, k1, r1, ALU.subtract))
                    own(dve.tensor_tensor(k2, k2, r2, ALU.add))
                self.z.wait_z(dve, 5)
                own(dve.tensor_tensor(gts[:], od_z[:, :, AT_MI:], b_gate[:].unsqueeze(1).to_broadcast([P, T, 2 * MH]),
                                      ALU.add))
                f = gts[:, :, MH:]
                own(dve.tensor_scalar(lf[:, 2], f, -1.0, None, ALU.mult))
                dve.tensor_tensor(lf[:, 0], f, lf[:, 2], ALU.max).then_inc(self.gate_abs, 1)
                dve.wait_ge(self.logs, 1)
                own(dve.tensor_scalar(lf[:, 2], f, 0.0, None, ALU.min))
                own(dve.tensor_tensor(lf[:, 2], lf[:, 2], lf[:, 1], ALU.subtract))

            def pe(self, pe):
                self.z.wait_z(pe, 5)
                pe.wait_ge(self.lat, 2 * T)
                for c in range(5):
                    for t in range(T):
                        at = (c % 2) * S + t * P
                        last = pe.transpose(ps[:, 2 + c // 2, at:at + P], lat[:, t, c * P:(c + 1) * P], ident[:])
                last.then_inc(self.lat_turned, 1)
                for c in range(4):
                    for t in range(T):
                        at = (c % 2) * S + t * P
                        last = pe.transpose(ps[:, 5 + c // 2, at:at + P], od_z[:, t, AT_MQ + c * P:AT_MQ + (c + 1) * P],
                                            ident[:])
                last.then_inc(self.mqk_turned, 1)
                pe.wait_ge(self.latT, 1)
                pe.wait_ge(self.mqk_freed, 1)
                wait_a(pe, "od_up", 0)
                wait_b(pe, "od_up", 0)
                wq = part_a("od_up", 0, 3 * 768).rearrange("p (k n) -> p k n", k=3)
                wkv = part_b("od_up", 0).rearrange("p (k n) -> p k n", k=2)
                for t in range(T):
                    for half_ in range(2):
                        for k in range(3):
                            last = pe.matmul(ps[:, 2 * t + half_, 0:384], latT[:, k, t * P:(t + 1) * P],
                                             wq[:, k, half_ * 384:(half_ + 1) * 384], start=(k == 0), stop=(k == 2))
                last.then_inc(self.q_made, 1)
                for t in range(T):
                    for half_ in range(2):
                        for k in range(2):
                            last = pe.matmul(ps[:, 4 + 2 * t + half_, :], latT[:, 3 + k, t * P:(t + 1) * P],
                                             wkv[:, k, half_ * 512:(half_ + 1) * 512], start=(k == 0), stop=(k == 1))
                last.then_inc(up_used, 1)

        class OddHeads:

            def __init__(self, up):
                self.up = up
                self.q_ready, self.k_ready = sem("od_q_ready"), sem("od_k_ready")
                self.turned = sem("od_heads_turned")

            def dve(self, dve, own):
                n = T * HEADS
                q3 = od_q[:].rearrange("p t h d -> p (t h) d")
                kv3 = od_kv[:].rearrange("p t h d -> p (t h) d")
                k3 = od_k[:].rearrange("p t h d -> p (t h) d")
                sq = xn[:].rearrange("p t d -> p (t d)")[:, 0:n * QK].rearrange("p (n d) -> p n d", d=QK)

                def per_head(at, width):
                    return rs[:, at:at + n].unsqueeze(2).to_broadcast([P, n, width])

                def root(at, parts):
                    for i, width in enumerate(parts):
                        own(dve.tensor_scalar(ms[:, at + i * n:at + (i + 1) * n], ms[:, at + i * n:at + (i + 1) * n], 1.0 / width,
                                              None, ALU.mult))
                    cut = slice(at, at + len(parts) * n)
                    rsqrt(dve, own, ms[:, cut], rs[:, cut], rtmp[:, 0, cut], rtmp[:, 1, cut])

                dve.wait_ge(self.up.q_copied, 1)
                own(dve.tensor_tensor(sq, q3, q3, ALU.mult))
                dve.tensor_reduce(ms[:, 0:n], sq[:, :, 0:NOPE], AX.X, ALU.add)
                own(dve.tensor_reduce(ms[:, n:2 * n], sq[:, :, NOPE:], AX.X, ALU.add))
                root(0, (NOPE, ROPE))
                dve.tensor_tensor(q3[:, :, 0:NOPE], q3[:, :, 0:NOPE], per_head(0, NOPE), ALU.mult)
                own(dve.tensor_tensor(q3[:, :, NOPE:], q3[:, :, NOPE:], per_head(n, ROPE), ALU.mult))
                own(dve.tensor_tensor(q3, q3, g_q[:].unsqueeze(1).to_broadcast([P, n, QK]), ALU.mult))
                hr = ROPE // 2
                for t in range(T):
                    r1, r2 = sq[:, t * HEADS:(t + 1) * HEADS, 0:hr], sq[:, t * HEADS:(t + 1) * HEADS, hr:2 * hr]
                    cos = cs[:, 0, t].unsqueeze(1).to_broadcast([P, HEADS, hr])
                    sin = cs[:, 1, t].unsqueeze(1).to_broadcast([P, HEADS, hr])
                    x1, x2 = od_q[:, t, :, NOPE:NOPE + hr], od_q[:, t, :, NOPE + hr:]
                    dve.tensor_tensor(r1, x2, sin, ALU.mult)
                    own(dve.tensor_tensor(r2, x1, sin, ALU.mult))
                    dve.tensor_tensor(x1, x1, cos, ALU.mult)
                    own(dve.tensor_tensor(x2, x2, cos, ALU.mult))
                    dve.tensor_tensor(x1, x1, r1, ALU.subtract)
                    dve.tensor_tensor(x2, x2, r2, ALU.add).then_inc(self.q_ready, 1)
                dve.wait_ge(self.q_ready, T)
                dve.wait_ge(self.up.kv_copied, 1)
                for t in range(T):
                    dve.tensor_copy(od_k[:, t, :, NOPE:],
                                    od_z[:, t, AT_KPE:AT_KPE + ROPE].unsqueeze(1).to_broadcast([P, HEADS, ROPE]))
                own(dve.tensor_tensor(sq[:, :, 0:NOPE], kv3[:, :, 0:NOPE], kv3[:, :, 0:NOPE], ALU.mult))
                own(dve.tensor_reduce(ms[:, 2 * n:3 * n], sq[:, :, 0:NOPE], AX.X, ALU.add))
                root(2 * n, (NOPE,))
                own(dve.tensor_tensor(k3[:, :, 0:NOPE], kv3[:, :, 0:NOPE], per_head(2 * n, NOPE), ALU.mult))
                dve.tensor_tensor(k3[:, :, 0:NOPE], k3[:, :, 0:NOPE],
                                  g_k[:, 0:NOPE].unsqueeze(1).to_broadcast([P, n, NOPE]), ALU.mult).then_inc(self.k_ready, T)
                for b in range(0, 8, 2):
                    dve.wait_ge(self.turned, b + 1)
                    dst = (qT if b < 4 else kT)[0:QK, 2 * (b % 4):2 * (b % 4) + 2, :]
                    dve.tensor_copy(dst, ps[0:QK, b, :].rearrange("p (h s) -> p h s", h=2))
                stage_end(dve)

            def act(self, act):
                for b in range(1, 8, 2):
                    act.wait_ge(self.turned, b + 1)
                    dst = (qT if b < 4 else kT)[0:QK, 2 * (b % 4):2 * (b % 4) + 2, :]
                    act.copy(dst, ps[0:QK, b, :].rearrange("p (h s) -> p h s", h=2))
                stage_end(act)

            def pe(self, pe):
                for b in range(8):
                    ready, src = (self.q_ready, od_q) if b < 4 else (self.k_ready, od_k)
                    if b % 4 == 0:
                        pe.wait_ge(ready, T)
                    for hd in range(2):
                        for t in range(T):
                            at = hd * S + t * P
                            last = pe.transpose(ps[0:QK, b, at:at + P], src[:, t, 2 * (b % 4) + hd, :], ident[:])
                    last.then_inc(self.turned, 1)
                stage_end(pe)

        class OddAttend:

            def __init__(self):
                self.cum = sem("oa_cum")
                self.diag = sem("oa_diag")
                self.rows = sem("oa_rows")
                self.rows_freed = sem("oa_rows_freed")
                self.scores = sem("oa_scores")
                self.masked = sem("oa_masked")
                self.prob = sem("oa_prob")
                self.turned = sem("oa_turned")
                self.probT = sem("oa_probT")
                self.valued = sem("oa_valued")
                self.nm = sem("oa_nm")
                self.w_mem = sem("oa_w_mem")
                self.mx = sem("oa_mx")
                self.v_aug_ready = sem("oa_v_aug_ready")
                self.y_freed = sem("oa_y_freed")

            N = HEADS + MH

            def pe(self, pe):
                for t in range(T):
                    o = ps[:, 5, t * MH:(t + 1) * MH]
                    if t:
                        pe.matmul(o, ones[:], lf[:, 2, 0], start=True, stop=False)
                    last = pe.matmul(o, upper[:], lf[:, 2, t], start=(t == 0), stop=True)
                last.then_inc(self.cum, 1)

                def rows(t):
                    pe.wait_ge(self.diag, t + 1)
                    if t:
                        pe.wait_ge(self.rows_freed, t)
                    pe.matmul(ps[:, 5, :], ones[:], diag_b[:, t], start=True, stop=True).then_inc(self.rows, 1)

                def scores(hd):
                    if hd >= 3:
                        pe.wait_ge(self.masked, hd - 2)
                    if hd < HEADS:
                        q, k = qT[0:QK, hd, :], kT[0:QK, hd, :]
                    else:
                        m = hd - HEADS
                        rows = slice((m % 2) * MQK, (m % 2 + 1) * MQK)
                        q, k = mqkT[rows, m // 2, :], mqkT[rows, 2 + m // 2, :]
                    pe.matmul(ps[:, hd % 3, 0:P], q[:, 0:P], k[:, 0:P], start=True, stop=True)
                    pe.matmul(ps[:, hd % 3, P:3 * P], q[:, P:S], k, start=True, stop=True).then_inc(self.scores, 1)

                def turn(hd):
                    if hd < HEADS:
                        pe.wait_ge(self.prob, hd + 1)
                    else:
                        pe.wait_ge(self.masked, hd + 1)
                    if hd >= 2:
                        pe.wait_ge(self.probT, hd - 1)
                    for j in range(3):
                        last = pe.transpose(ps[:, 3 + hd % 2, j * P:(j + 1) * P], prob[:, hd % 2, j * P:(j + 1) * P], ident[:])
                    last.then_inc(self.turned, 1)

                def values(hd):
                    pe.wait_ge(self.probT, hd + 1)
                    if hd == HEADS:
                        pe.wait_ge(self.v_aug_ready, 1)
                        pe.wait_ge(self.y_freed, T)
                    elif hd > HEADS + 1:
                        pe.wait_ge(self.y_freed, T + hd - HEADS - 1)
                    for t in range(T):
                        for j in range(t + 1):
                            w = probT[:, hd % 2, (t + j) * P:(t + j + 1) * P]
                            if hd < HEADS:
                                o, v = ps[:, 6 + t, hd * VD:(hd + 1) * VD], od_kv[:, j, hd, NOPE:]
                            else:
                                m = hd - HEADS
                                o = ps[:, 6 + m % 2, t * (MV + 1):(t + 1) * (MV + 1)]
                                v = v_aug[:, j, m, :]
                            last = pe.matmul(o, w, v, start=(j == 0), stop=(j == t))
                    last.then_inc(self.valued, 1)

                for step in range(self.N + 2):
                    if step < self.N:
                        scores(step)
                    if 1 <= step <= self.N:
                        turn(step - 1)
                    if step >= 2:
                        values(step - 2)
                    if step in (1, 2):
                        rows(step - 1)
                stage_end(pe)

            def act(self, act):
                def copy(hd):
                    act.wait_ge(self.turned, hd + 1)
                    if hd >= 2:
                        act.wait_ge(self.valued, hd - 1)
                    act.copy(probT[:, hd % 2], ps[:, 3 + hd % 2, 0:3 * P]).then_inc(self.probT, 1)

                def memory_weights():
                    act.wait_ge(self.mx, 1)
                    for m in range(MH):
                        for t in range(T):
                            b = b_masked[:, m, 0:P] if t == 0 else b_masked[:, m, P:3 * P]
                            act.activation(b, b, ACT.Exp, bias=nmax[:, HEADS + m, t:t + 1])
                    act.activation(emt[:], emt[:], ACT.Exp, scale=-1.0).then_inc(self.w_mem, 1)

                for hd in range(HEADS):
                    act.wait_ge(self.nm, hd + 1)
                    if hd >= 2:
                        act.wait_ge(self.turned, hd - 1)
                    for t in range(T):
                        cut = slice(0, P) if t == 0 else slice(P, 3 * P)
                        last = act.activation(prob[:, hd % 2, cut], sm[:, hd % 2, cut], ACT.Exp,
                                              bias=nmax[:, hd, t:t + 1], accum_out=rsum[:, t, hd:hd + 1])
                    last.then_inc(self.prob, 1)
                    copy(hd)
                    if hd == HEADS - 2:
                        memory_weights()
                for hd in range(HEADS, self.N):
                    copy(hd)
                stage_end(act)

            def dve(self, dve, own):
                dve.wait_ge(self.cum, 1)
                own(dve.tensor_copy(acum[:], ps[:, 5, 0:T * MH].rearrange("p (t h) -> p t h", t=T)))
                own(dve.tensor_tensor(bcol[:], gts[:, :, 0:MH], acum[:], ALU.subtract))

                def masked(hd):
                    dve.wait_ge(self.scores, hd + 1)
                    if hd < HEADS:
                        if hd >= 2:
                            dve.wait_ge(self.prob, hd - 1)
                        ins = dve.scalar_tensor_tensor(out=sm[:, hd % 2], in0=ps[:, hd % 3, 0:3 * P], scalar=float(QK) ** -0.5,
                                                       in1=cmask[:], op0=ALU.mult, op1=ALU.add)
                        ins.then_inc(self.masked, 1)
                        dve.wait_ge(self.masked, hd + 1)
                        dve.tensor_reduce(nmax[:, hd, 0:1], sm[:, hd % 2, 0:P], AX.X, ALU.max, negate=True)
                        dve.tensor_reduce(nmax[:, hd, 1:2], sm[:, hd % 2, P:3 * P], AX.X, ALU.max,
                                          negate=True).then_inc(self.nm, 1)
                    else:
                        m = hd - HEADS
                        if m == 0:
                            dve.wait_ge(self.w_mem, 1)
                        dve.wait_ge(self.turned, hd - 1)
                        ins = dve.scalar_tensor_tensor(out=prob[:, hd % 2], in0=ps[:, hd % 3, 0:3 * P],
                                                       scalar=float(MQK) ** -0.5, in1=b_masked[:, m, :],
                                                       op0=ALU.mult, op1=ALU.mult)
                        ins.then_inc(self.masked, 1)

                for t in range(T):
                    dve.tensor_tensor(diag_b[:, t], ident[:].unsqueeze(1).to_broadcast([P, MH, P]),
                                      bcol[:, t].unsqueeze(2).to_broadcast([P, MH, P]), ALU.mult).then_inc(self.diag, 1)
                tri = cmask[:, 0:P].unsqueeze(1).to_broadcast([P, MH, P])
                row = ps[:, 5, :].rearrange("p (h n) -> p h n", h=MH)
                top = nmax[:, HEADS:, :].rearrange("p h t -> p t h")

                def rows(t):
                    dve.wait_ge(self.rows, t + 1)
                    if t == 0:
                        dve.tensor_tensor(b_masked[:, :, 0:P], row, tri, ALU.add)
                        dve.tensor_copy(b_masked[:, :, P:2 * P], row).then_inc(self.rows_freed, 1)
                    else:
                        dve.tensor_tensor(b_masked[:, :, 2 * P:3 * P], row, tri, ALU.add).then_inc(self.rows_freed, 1)

                def maxima():
                    dve.wait_ge(self.rows_freed, T)
                    dve.tensor_reduce(nmax[:, HEADS:, 0:1], b_masked[:, :, 0:P], AX.X, ALU.max)
                    own(dve.tensor_reduce(nmax[:, HEADS:, 1:2], b_masked[:, :, P:3 * P], AX.X, ALU.max))
                    own(dve.tensor_scalar(nmax[:, HEADS:, :], nmax[:, HEADS:, :], 0.0, None, ALU.max))
                    own(dve.tensor_tensor(emt[:], acum[:], top, ALU.add))
                    dve.tensor_scalar(nmax[:, HEADS:, :], nmax[:, HEADS:, :], -1.0, None, ALU.mult).then_inc(self.mx, 1)

                def values():
                    own(dve.memset(v_aug[:, :, :, MV:], 1.0))
                    dve.tensor_copy(v_aug[:, :, :, 0:MV], od_z[:, :, AT_MV:AT_MO].rearrange("p t (h d) -> p t h d", h=MH)
                                    ).then_inc(self.v_aug_ready, 1)

                def split(j):
                    split_upto(dve, split_lo, "od_out", 0, j, ahead=0)

                between = {1: lambda: rows(0), 2: lambda: rows(1), 3: maxima, 4: values, 5: lambda: split(0), 6: lambda: split(1),
                           7: lambda: split(2), 9: lambda: split(3)}
                for hd in range(self.N):
                    masked(hd)
                    if hd in between:
                        between[hd]()
                    if hd == HEADS + 1:
                        dve.wait_ge(self.valued, HEADS)
                        own(dve.reciprocal(rsum[:], rsum[:]))
                        for t in range(T):
                            dve.tensor_tensor(mix[:, t, 0:HEADS * VD].rearrange("p (h d) -> p h d", h=HEADS),
                                              ps[:, 6 + t, :].rearrange("p (h d) -> p h d", h=HEADS),
                                              rsum[:, t].unsqueeze(2).to_broadcast([P, HEADS, VD]),
                                              ALU.mult).then_inc(self.y_freed, 1)
                for m in range(MH):
                    dve.wait_ge(self.valued, HEADS + m + 1)
                    dve.wait_ge(self.y_freed, T + m)
                    num = ps[:, 6 + m % 2, 0:T * (MV + 1)].rearrange("p (t d) -> p t d", t=T)
                    own(dve.tensor_copy(den[:, 0], num[:, :, MV]))
                    own(dve.tensor_scalar(den[:, 1], den[:, 0], -1.0, None, ALU.mult))
                    own(dve.tensor_tensor(den[:, 0], den[:, 0], den[:, 1], ALU.max))
                    own(dve.tensor_tensor(den[:, 0], den[:, 0], emt[:, :, m], ALU.max))
                    own(dve.reciprocal(den[:, 0], den[:, 0]))
                    dve.tensor_tensor(y_d[:, :, m, :], num[:, :, 0:MV], den[:, 0].unsqueeze(2).to_broadcast([P, T, MV]),
                                      ALU.mult).then_inc(self.y_freed, 1)
                stage_end(dve)

        class OddOut:
            def __init__(self):
                self.tanh, self.y, self.turned, self.hi, self.lo = (sem("oo_" + n) for n in ("tanh", "y", "turned", "hi", "lo"))

            def act(self, act):
                mo = od_z[:, :, AT_MO:AT_MI]
                act.activation(od_z[:, :, AT_MV:AT_MO], mo, ACT.Tanh, scale=0.5).then_inc(self.tanh, 1)
                split_upto(act, split_hi, "od_out", 0, 3, ahead=0)
                for b in range(4):
                    act.wait_ge(self.turned, b + 1)
                    act.copy(xT_hi[:, 2 * b:2 * b + 2, :], ps[:, b, :].rearrange("p (c s) -> p c s", c=2)).then_inc(self.hi, 1)
                split_upto(act, split_hi, "od_out", 1, 3)

            def dve(self, dve, own):
                def low(b):
                    dve.wait_ge(self.hi, b + 1)
                    dve.tensor_tensor(xT_lo[:, 2 * b:2 * b + 2, :], ps[:, b, :].rearrange("p (c s) -> p c s", c=2),
                                      xT_hi[:, 2 * b:2 * b + 2, :].bitcast(F32), ALU.subtract).then_inc(self.lo, 1)

                for b in range(2):
                    low(b)
                split_upto(dve, split_lo, "od_out", 0, 1, ahead=0)
                n = T * MH
                sq = od_kv[:].rearrange("p t h d -> p t (h d)")[:, :, 0:MH * MV].rearrange("p t (h d) -> p t h d", h=MH)
                own(dve.tensor_tensor(sq, y_d, y_d, ALU.mult))
                own(dve.tensor_reduce(ms[:, 0:n].rearrange("p (t h) -> p t h", t=T), sq, AX.X, ALU.add))
                own(dve.tensor_scalar(ms[:, 0:n], ms[:, 0:n], 1.0 / MV, None, ALU.mult))
                rsqrt_ms(dve, own, n)
                own(dve.tensor_scalar(rs[:, 0:n], rs[:, 0:n], 0.5, None, ALU.mult))
                for t in range(T):
                    own(dve.tensor_tensor(y_d[:, t], y_d[:, t],
                                          rs[:, t * MH:(t + 1) * MH].unsqueeze(2).to_broadcast([P, MH, MV]), ALU.mult))
                flat = mix[:, :, HEADS * VD:]
                own(dve.tensor_tensor(flat, flat, g_mh[:].unsqueeze(1).to_broadcast([P, T, MH * MV]), ALU.mult))
                dve.wait_ge(self.tanh, 1)
                dve.scalar_tensor_tensor(out=flat, in0=od_z[:, :, AT_MV:AT_MO], scalar=1.0, in1=flat, op0=ALU.add,
                                         op1=ALU.mult).then_inc(self.y, 1)
                split_upto(dve, split_lo, "od_out", 0, 3, ahead=0)
                for b in (2, 3):
                    low(b)
                for i in range(2):
                    split_upto(dve, split_lo, "od_out", i, 3)
                    wait_used(dve, "od_out", i, 3)
                    for t in range(T):
                        o = h[:, t, i * 512:(i + 1) * 512]
                        ins = dve.tensor_tensor(o, o, ps[:, 4 + 2 * i + t, :], ALU.add)
                    ins.then_inc(h_ready, 1)

            def pe(self, pe):
                def turn(banks):
                    for b in banks:
                        for c in (2 * b, 2 * b + 1):
                            for t in range(T):
                                at = (c % 2) * S + t * P
                                last = pe.transpose(ps[:, b, at:at + P], mix[:, t, c * P:(c + 1) * P], ident[:])
                        last.then_inc(self.turned, 1)

                def rest():
                    pe.wait_ge(self.y, 1)
                    turn((2, 3))
                    pe.wait_ge(self.lo, 4)

                turn((0, 1))
                pe.wait_ge(self.lo, 2)
                for i in range(2):
                    tokens_by_columns(pe, "od_out", i, (4 + 2 * i, 5 + 2 * i), rest=rest if i == 0 else None)

        ADA_ITEMS = 2 * 6 * D // BLK
        HALF_ROWS = KC // 2
        ada_steps = sem("ada_steps")

        def ada_loads(pool):
            w = a["ada_w_2"][0].rearrange("(s k p) n -> p s k n", p=P, s=2)

            def load(q, it):
                cut = bass.ds(per_round(q % 2 * BLK, it, 2 * BLK), BLK)
                pool.dma_start(ada_w[:, q], w[:, q // 2, :, cut]).then_inc(ada_landed[q], 16)

            pool.wait_ge(h_ready, 8)
            for q in range(ADA_BUFFERS):
                load(q, None)
            with pool.Fori(1, ADA_ITEMS // ADA_BUFFERS) as it:
                for q in range(ADA_BUFFERS):
                    pool.wait_ge(ada_used, ADA_BUFFERS * it + q // 2 * 2 - 2)
                    load(q, it)

        def ada_products(dve, block, it):
            j = block
            for second in range(2):
                for q in range(2):
                    dve.wait_ge(ada_landed[2 * second + q], per_round(16 * (j + 1), it, 16 * FF_ROUND))
                if second:
                    dve.wait_ge(ada_used, per_round(4 * j + 2, it, 4 * FF_ROUND))
                steps = 4 * (HALF_ROWS - 1) * j + 2 * (HALF_ROWS - 1) * second
                for k in range(HALF_ROWS):
                    for q in range(2):
                        acc = ada_acc[:, bass.ds(per_round((2 * j + q) * BLK, it, 2 * FF_ROUND * BLK), BLK)]
                        c = second * HALF_ROWS + k
                        w, c_col = ada_w[:, 2 * second + q, k], c_act[:, c:c + 1]
                        if c == 0:
                            ins = dve.tensor_scalar(acc, w, c_col, None, ALU.mult)
                        else:
                            if k > 0:
                                dve.wait_ge(ada_steps, per_round(steps + 2 * (k - 1) + q + 1, it, 4 * (HALF_ROWS - 1) * FF_ROUND))
                            ins = dve.scalar_tensor_tensor(out=acc, in0=w, scalar=c_col, in1=acc, op0=ALU.mult, op1=ALU.add)
                        ins.then_inc(ada_steps if k < HALF_ROWS - 1 else ada_used, 1)

        class ModStage:
            COLS, ROWS = (0, 1, 3, 4), (2, 5)

            def __init__(self):
                self.summed = sem("mod_summed")
                self.cols, self.rows = sem("mod_cols_made"), sem("mod_rows_made")
                self.b_landed = sem("mod_b_landed")

            def load(self, act):
                for i, v in enumerate(self.ROWS):
                    act.dma_start(g_bc[:, i], a["ada_b_2"][0, v * D:(v + 1) * D].partition_broadcast(P)
                                  ).then_inc(self.b_landed, 16)

            def pe(self, pe):
                pe.wait_ge(h_ready, 12)
                pe.wait_ge(ada_used, ADA_ITEMS)
                for i, v in enumerate(self.COLS):
                    for c in range(KC):
                        last = pe.matmul(ps[:, 0, i * KC + c:i * KC + c + 1], ada_acc[:, v * D + c * P:v * D + (c + 1) * P],
                                         ones[:, 0:1], start=True, stop=True)
                last.then_inc(self.summed, 1)
                for i, v in enumerate(self.ROWS):
                    for j in range(2):
                        last = pe.matmul(ps[:, 4 + 2 * i + j, :], ones[:], ada_acc[:, v * D + j * 512:v * D + (j + 1) * 512],
                                         start=True, stop=True)
                last.then_inc(self.summed, 1)
                pe.wait_ge(self.cols, 1)

            def dve_cols(self, dve, own):
                dve.wait_ge(self.summed, 1)
                for i, v in enumerate(self.COLS):
                    own(dve.tensor_tensor(mod_cols[:, i], ps[:, 0, i * KC:(i + 1) * KC], col("ada_b_2", v * KC, KC), ALU.add))
                for i, name in ((1, "norm_mix_g_2"), (3, "norm_ffn_g_2")):
                    last = dve.scalar_tensor_tensor(out=mod_cols[:, i], in0=mod_cols[:, i], scalar=1.0, in1=col(name, 0, KC),
                                                    op0=ALU.add, op1=ALU.mult)
                last.then_inc(self.cols, 1)
                dve.wait_ge(self.cols, 1)

            def dve_rows(self, dve):
                dve.wait_ge(self.summed, 2)
                dve.wait_ge(self.b_landed, 32)
                for i in range(2):
                    last = dve.tensor_tensor(g_bc[:, i].rearrange("p (j n) -> p j n", j=2), ps[:, 4 + 2 * i:6 + 2 * i, :],
                                             g_bc[:, i].rearrange("p (j n) -> p j n", j=2), ALU.add)
                last.then_inc(self.rows, 1)
                dve.wait_ge(self.rows, 1)

        class ConformerStage:
            def __init__(self):
                self.hi = sem("cf_hi")
                self.lo = sem("cf_lo")
                self.cols = sem("cf_cols")
                self.tanh = sem("cf_tanh")
                self.u = sem("cf_u")
                self.conv = sem("cf_conv")
                self.mean = sem("cf_mean")
                self.centred = sem("cf_centred")
                self.squares = sem("cf_squares")
                self.var = sem("cf_var")
                self.normed = sem("cf_normed")
                self.tanh2 = sem("cf_tanh2")
                self.y = sem("cf_y")
                self.taps = sem("cf_taps")
                self.shifted = sem("cf_shifted")
                self.diag_ready, self.diag_used, self.conv_pe = sem("cf_diag_ready"), sem("cf_diag_used"), sem("cf_conv_pe")
                self.y_view = xn[:].rearrange("p t d -> p (t d)").rearrange("p (c s) -> p c s", c=KC)

            def pe(self, pe):
                for c in range(KC):
                    for g in range(2):
                        w = halves(pe, "conv_in", c // 2, 2 * (c % 2) + g)
                        columns_by_tokens(pe, ps[:, c, g * S:(g + 1) * S], w).then_inc(pieces_used, 1)
                for i, c in enumerate(CONV_PE):
                    pe.wait_ge(self.u, c + 1)
                    for j in range(TAPS):
                        pe.wait_ge(self.diag_ready, i * TAPS + j + 1)
                        pe.matmul(ps[:, i, 0:S], diag[:, (i * TAPS + j) % DIAGS], u_pad[:, c, j:j + S],
                                  start=(j == 0), stop=(j == TAPS - 1)).then_inc(self.diag_used, 1)
                y = self.y_view
                pe.wait_ge(self.conv, KC - len(CONV_PE))
                pe.wait_ge(self.conv_pe, len(CONV_PE))
                for c in range(KC):
                    last = pe.matmul(ps[:, 6, 0:S], mean_w[:], y[:, c], start=(c == 0), stop=(c == KC - 1))
                last.then_inc(self.mean, 1)
                for c in range(KC):
                    pe.wait_ge(self.squares, c + 1)
                    last = pe.matmul(ps[:, 7, 0:S], mean_w[:], mixT[:, c], start=(c == 0), stop=(c == KC - 1))
                last.then_inc(self.var, 1)
                for i in range(2):
                    tokens_by_columns(pe, "conv_out", i, (2 + 2 * i, 3 + 2 * i), chunks=self.lo)

            def act(self, act):
                def high(c):
                    act.wait_ge(self.y, c + 1)
                    act.copy(xT_hi[:, c], mixT[:, c]).then_inc(self.hi, 1)

                made = [0]

                def diagonals(act, upto):
                    for n in range(made[0], min(upto, len(CONV_PE) * TAPS)):
                        c, j = CONV_PE[n // TAPS], n % TAPS
                        if n >= DIAGS:
                            act.wait_ge(self.diag_used, n - DIAGS + 1)
                        act.activation(diag[:, n % DIAGS], ident[:], ACT.Copy, scale=w_dw[:, c, j:j + 1]).then_inc(self.diag_ready, 1)
                        made[0] = n + 1

                act.wait_ge(self.cols, 1)
                for c in range(KC):
                    split_upto(act, split_hi, "conv_in", c // 2, 2 * (c % 2) + 1)
                    wait_used(act, "conv_in", c // 2, 2 * (c % 2) + 1)
                    if c >= 2:
                        act.wait_ge(self.u, c - 1)
                    act.activation(cf_th[:, c % 2], ps[:, c, S:2 * S], ACT.Tanh, bias=half[:, c:c + 1],
                                   scale=0.5).then_inc(self.tanh, 1)
                    diagonals(act, DIAGS // KC * (c + 1))
                for i, c in enumerate(CONV_PE):
                    diagonals(act, (i + 1) * TAPS + DIAGS - TAPS)
                    act.wait_ge(self.diag_used, (i + 1) * TAPS)
                    act.activation(self.y_view[:, c], ps[:, i, 0:S], ACT.Identity, bias=col("conv_b_dw_2", c)).then_inc(self.conv_pe, 1)
                for c in range(KC):
                    act.wait_ge(self.centred, c + 1)
                    act.activation(mixT[:, c], self.y_view[:, c], ACT.Square).then_inc(self.squares, 1)
                for c in range(KC):
                    act.wait_ge(self.normed, c + 1)
                    act.activation(hnT[:, c], self.y_view[:, c], ACT.Tanh, bias=half[:, 2 * KC + c:2 * KC + c + 1],
                                   scale=half[:, KC + c:KC + c + 1]).then_inc(self.tanh2, 1)
                    if c >= 2:
                        high(c - 2)
                high(KC - 2)
                high(KC - 1)
                split_upto(act, split_hi, "conv_out", 1, 3)

            def dve(self, dve, own):
                for i, (name, at) in enumerate((("conv_b_in_2", KC), ("conv_ln_g_2", 0), ("conv_ln_b_2", 0))):
                    last = dve.tensor_scalar(half[:, i * KC:(i + 1) * KC], col(name, at, KC), 0.5, None, ALU.mult)
                last.then_inc(self.cols, 1)
                own(dve.memset(u_pad[:, :, 0:TAPS - 1], 0.0))
                y = self.y_view
                def gated(c):
                    dve.wait_ge(self.tanh, c + 1)
                    own(dve.tensor_scalar(cf_a[:, c % 2], ps[:, c, 0:S], col("conv_b_in_2", c), 0.5, ALU.add, ALU.mult))
                    dve.scalar_tensor_tensor(out=u_pad[:, c, TAPS - 1:], in0=cf_th[:, c % 2], scalar=1.0, in1=cf_a[:, c % 2],
                                             op0=ALU.add, op1=ALU.mult).then_inc(self.u, 1)

                def convolve(chunks, before, first, last):
                    for j in range(first, last):
                        for at, c in enumerate(chunks):
                            w, src = w_dw[:, c, j:j + 1], u_pad[:, c, j:j + S]
                            if j == 0:
                                dve.wait_ge(self.u, c + 1)
                                ins = dve.tensor_scalar(y[:, c], src, w, col("conv_b_dw_2", c), ALU.mult, ALU.add)
                            else:
                                dve.wait_ge(self.taps, before + len(chunks) * (j - 1) + at + 1)
                                ins = dve.scalar_tensor_tensor(out=y[:, c], in0=src, scalar=w, in1=y[:, c], op0=ALU.mult,
                                                               op1=ALU.add)
                            ins.then_inc(self.taps if j < TAPS - 1 else self.conv, 1)

                early, late = (0, 1), tuple(range(2, CONV_PE[0]))
                beside = 6
                for c in range(KC):
                    split_upto(dve, split_lo, "conv_in", c // 2, 2 * (c % 2) + 1)
                    gated(c)
                    if c >= 2:
                        convolve(early, 0, min(beside * (c - 2), TAPS), min(beside * (c - 1), TAPS))
                convolve(late, len(early) * (TAPS - 1), 0, TAPS)
                dve.wait_ge(self.conv, KC - len(CONV_PE))
                dve.wait_ge(self.conv_pe, len(CONV_PE))
                dve.wait_ge(self.mean, 1)
                for c in range(KC):
                    dve.tensor_tensor(y[:, c], y[:, c], ps[:, 6, 0:S], ALU.subtract).then_inc(self.centred, 1)
                split_upto(dve, split_lo, "conv_out", 0, 2, ahead=0)
                dve.wait_ge(self.var, 1)
                own(dve.tensor_copy(cf_r[:, 0], ps[:, 7, 0:S]))
                rsqrt(dve, own, cf_r[:, 0], cf_r[:, 1], cf_r[:, 2], cf_r[:, 3])
                dve.wait_ge(self.centred, KC)

                def finish(c):
                    dve.wait_ge(self.tanh2, c + 1)
                    dve.tensor_scalar(y[:, c], y[:, c], half[:, KC + c:KC + c + 1], half[:, 2 * KC + c:2 * KC + c + 1],
                                      ALU.mult, ALU.add).then_inc(self.shifted, 1)
                    dve.wait_ge(self.shifted, c + 1)
                    dve.scalar_tensor_tensor(out=mixT[:, c], in0=hnT[:, c], scalar=1.0, in1=y[:, c], op0=ALU.add,
                                             op1=ALU.mult).then_inc(self.y, 1)

                def low(c):
                    dve.wait_ge(self.hi, c + 1)
                    dve.tensor_tensor(xT_lo[:, c], mixT[:, c], xT_hi[:, c].bitcast(F32), ALU.subtract).then_inc(self.lo, 1)

                for c in range(KC + 4):
                    if c < KC:
                        dve.tensor_tensor(y[:, c], y[:, c], cf_r[:, 1], ALU.mult).then_inc(self.normed, 1)
                    if 1 <= c <= KC:
                        finish(c - 1)
                    if c >= 4:
                        low(c - 4)
                dve.wait_ge(mod.rows, 1)
                for i in range(2):
                    split_upto(dve, split_lo, "conv_out", i, 3)
                    wait_used(dve, "conv_out", i, 3)
                    for t in range(T):
                        o, g = h[:, t, i * 512:(i + 1) * 512], g_bc[:, 0, i * 512:(i + 1) * 512]
                        tmp = xn[:, t, i * 512:(i + 1) * 512]
                        own(dve.tensor_tensor(tmp, ps[:, 2 + 2 * i + t, :], g, ALU.mult))
                        ins = dve.tensor_tensor(o, o, tmp, ALU.add)
                    ins.then_inc(h_ready, 1)

        class RouteStage:
            def __init__(self):
                self.made, self.gmax, self.gexp, self.diff, self.dexp = (sem("rt_" + n) for n in
                                                                        ("made", "gmax", "gexp", "diff", "dexp"))
                self.turned, self.chosen, self.counted = sem("rt_turned"), sem("rt_chosen"), sem("rt_counted")

            def pe(self, pe):
                for t in range(T):
                    for k in range(KC):
                        last = pe.matmul(ps[:, t, 0:GROUPS + EXPERTS], hnT[:, k, t * P:(t + 1) * P], w_route[:, k, :],
                                         start=(k == 0), stop=(k == KC - 1))
                last.then_inc(self.made, 1)
                for b in range(4):
                    for c in range(4):
                        k = (b % 2) * 4 + c
                        last = pe.transpose(ps[:, 4 + b, c * P:(c + 1) * P], hnT[:, k, (b // 2) * P:(b // 2 + 1) * P], ident[:])
                    last.then_inc(self.turned, 1)
                pe.wait_ge(self.chosen, 1)
                pe.matmul(ps[:, 2, 0:EXPERTS], upper[:], rt[:, 8, 0], start=True, stop=True)
                pe.matmul(ps[:, 2, EXPERTS:2 * EXPERTS], ones[:], rt[:, 8, 0], start=True, stop=False)
                pe.matmul(ps[:, 2, EXPERTS:2 * EXPERTS], upper[:], rt[:, 8, 1], start=False, stop=True)
                pe.matmul(ps[:, 3, 0:EXPERTS], ones[:], rt[:, 8, 0], start=True, stop=False)
                pe.matmul(ps[:, 3, 0:EXPERTS], ones[:], rt[:, 8, 1], start=False, stop=True).then_inc(self.counted, 1)
                stage_end(pe)

            def act(self, act):
                for b in range(4):
                    act.wait_ge(self.turned, b + 1)
                    act.copy(xn[:, b // 2, (b % 2) * 512:(b % 2 + 1) * 512], ps[:, 4 + b, :])
                act.wait_ge(self.gmax, 1)
                for t in range(T):
                    last = act.activation(rt[:, 1, t, 0:GROUPS], rt[:, 0, t, 0:GROUPS], ACT.Exp, bias=rts[:, 0, t:t + 1],
                                          accum_out=rts[:, 1, t:t + 1])
                last.then_inc(self.gexp, 1)
                act.wait_ge(self.diff, 1)
                act.activation(rts[:, 5], rts[:, 4], ACT.Exp).then_inc(self.dexp, 1)
                stage_end(act)

            def dve(self, dve, own):
                def wide(x, n=EXPERTS):
                    return x.unsqueeze(2).to_broadcast([P, T, n])

                def first_max(hot, x, top, key, key_top, n):
                    own(dve.tensor_tensor(key, x, wide(top, n), ALU.is_equal))
                    own(dve.tensor_tensor(key, key, rev[:, 0:n].unsqueeze(1).to_broadcast([P, T, n]), ALU.mult))
                    own(dve.tensor_reduce(key_top, key, AX.X, ALU.max))
                    own(dve.tensor_tensor(hot, key, wide(key_top, n), ALU.is_equal))

                grp, eg, key, hot1, hot2 = (rt[:, i] for i in (0, 2, 3, 4, 5))
                exp_l = rt[:, 6]
                g4 = grp[:, :, 0:GROUPS]
                dve.wait_ge(self.made, 1)
                own(dve.tensor_tensor(g4, ps[:, 0:T, 0:GROUPS], b_route[:, 0:GROUPS].unsqueeze(1).to_broadcast([P, T, GROUPS]),
                                      ALU.add))
                own(dve.tensor_tensor(exp_l, ps[:, 0:T, GROUPS:GROUPS + EXPERTS],
                                      b_route[:, GROUPS:].unsqueeze(1).to_broadcast([P, T, EXPERTS]), ALU.add))
                own(dve.tensor_reduce(rts[:, 2], g4, AX.X, ALU.max))
                dve.tensor_scalar(rts[:, 0], rts[:, 2], -1.0, None, ALU.mult).then_inc(self.gmax, 1)
                first_max(eg[:, :, 0:GROUPS], g4, rts[:, 2], key[:, :, 0:GROUPS], rts[:, 3], GROUPS)
                own(dve.tensor_scalar(eg[:, :, 0:GROUPS], eg[:, :, 0:GROUPS], -1.0, -NEG, ALU.add, ALU.mult))
                for t in range(T):
                    e3 = exp_l[:, t].rearrange("p (g e) -> p g e", g=GROUPS)
                    own(dve.tensor_tensor(e3, e3, eg[:, t, 0:GROUPS].unsqueeze(2).to_broadcast([P, GROUPS, PER_GROUP]), ALU.add))
                own(dve.tensor_reduce(rts[:, 6], exp_l, AX.X, ALU.max))
                first_max(hot1, exp_l, rts[:, 6], key, rts[:, 3], EXPERTS)
                own(dve.scalar_tensor_tensor(out=rt[:, 7], in0=hot1, scalar=3 * NEG, in1=exp_l, op0=ALU.mult, op1=ALU.add))
                own(dve.tensor_reduce(rts[:, 7], rt[:, 7], AX.X, ALU.max))
                first_max(hot2, rt[:, 7], rts[:, 7], key, rts[:, 3], EXPERTS)
                dve.tensor_tensor(rts[:, 4], rts[:, 7], rts[:, 6], ALU.subtract).then_inc(self.diff, 1)
                dve.tensor_tensor(rt[:, 8], hot1, hot2, ALU.add).then_inc(self.chosen, 1)
                dve.wait_ge(self.gexp, 1)
                own(dve.reciprocal(rts[:, 8], rts[:, 1]))
                dve.wait_ge(self.dexp, 1)
                own(dve.tensor_scalar(rts[:, 9], rts[:, 5], 1.0, None, ALU.add))
                own(dve.reciprocal(rts[:, 9], rts[:, 9]))
                own(dve.tensor_tensor(rts[:, 10], rts[:, 5], rts[:, 9], ALU.mult))
                for i in (9, 10):
                    own(dve.scalar_tensor_tensor(out=rts[:, i], in0=rts[:, i], scalar=0.5, in1=rts[:, 8], op0=ALU.mult,
                                                 op1=ALU.mult))
                own(dve.tensor_tensor(hot1, hot1, wide(rts[:, 9]), ALU.mult))
                own(dve.tensor_tensor(hot2, hot2, wide(rts[:, 10]), ALU.mult))
                own(dve.tensor_tensor(gate_half[:], hot1, hot2, ALU.add))
                dve.wait_ge(self.counted, 1)
                own(dve.tensor_tensor(place[:], ps[:, 2, 0:T * EXPERTS].rearrange("p (t e) -> p t e", t=T), rt[:, 8], ALU.mult))
                own(dve.tensor_scalar(place[:], place[:], -1.0, None, ALU.add))
                own(dve.tensor_reduce(rts[:, 0, 0:1], ps[:, 3, 0:EXPERTS], AX.X, ALU.max))
                own(dve.tensor_scalar(rts[:, 1, 0:1], rts[:, 0, 0:1], PLACES + 0.5, None, ALU.is_ge))
                own(dve.tensor_copy(crowded[:], rts[:, 1, 0:1]))
                stage_end(dve)

        class AllTokens:

            def __init__(self, other):
                self.blocks = MOE_BLOCKS
                self.gate_up = other.gathered
                self.tanh = other.tanh
                self.half = other.half
                self.hid = other.hid
                self.turned = other.turned
                self.hidT = other.copied
                self.first_looped = 2 * HALVES * (EARLY // 2 + 1) + 2
                self.loops = (self.blocks - self.first_looped) // 4

            def blocks_in_loop(self, eng, step):
                for n in range(2, self.first_looped):
                    step(n, None)
                with eng.Fori(0, self.loops) as it:
                    for j in range(4):
                        step(self.first_looped + j, it)
                for n in range(self.first_looped + 4 * self.loops, self.blocks):
                    step(n, None)

            @staticmethod
            def at(value, per_block, it):
                return value if it is None else value + 4 * per_block * it

            def pe(self, pe):
                at = self.at

                def gate_up(n, it, t):
                    if t == 0:
                        wait_gate_up(pe, n // HALVES, it)
                    if n >= 1:
                        pe.wait_ge(self.hid, at(2 * (n - 1) + t + 1, 2, it))
                    cut = slice(n % HALVES * BLK, (n % HALVES + 1) * BLK)
                    for k in range(KC):
                        last = pe.matmul(ps[:, t, :].rearrange("p (two f) -> p two f", two=2), hnT[:, k, t * P:(t + 1) * P],
                                         gate_up_rows(n // HALVES, k)[:, :, cut], start=(k == 0), stop=(k == KC - 1))
                    last.then_inc(self.gate_up, 1)
                    if n % HALVES == 1 and t == 1:
                        pe.drain().then_inc(gu_used, 1)

                def turn(n, it):
                    pe.wait_ge(self.hid, at(2 * n + 2, 2, it))
                    if n >= 1:
                        pe.wait_ge(self.hidT, at(n, 1, it))
                    for c in range(2):
                        for t in range(T):
                            last = pe.transpose(ps[:, 2, c * S + t * P:c * S + (t + 1) * P],
                                                all_hid[:, n % 2, t, c * P:(c + 1) * P], ident[:])
                    last.then_inc(self.turned, 1)

                def down(n, it):
                    pe.wait_ge(self.hidT, at(n + 1, 1, it))
                    wait_down(pe, n // HALVES, it)
                    for t in range(T):
                        for half in range(2):
                            for c in range(2):
                                last = pe.matmul(ps[:, 4 + 2 * t + half, :], all_hidT[:, c, t * P:(t + 1) * P],
                                                 down_rows(n // HALVES, n % HALVES * 2 + c)[:, half * 512:(half + 1) * 512],
                                                 start=(n == 0 and c == 0), stop=(n == self.blocks - 1 and c == 1))
                    if n % (2 * HALVES) == 2 * HALVES - 1:
                        last.then_inc(down_used, 1)

                def step(n, it):
                    gate_up(n, it, 0)
                    turn(n - 1, it)
                    gate_up(n, it, 1)
                    down(n - 1, it)

                gate_up(0, None, 0)
                gate_up(0, None, 1)
                step(1, None)
                self.blocks_in_loop(pe, step)
                turn(self.blocks - 1, None)
                down(self.blocks - 1, None)

            def act(self, act):
                at = self.at

                def tanh(n, it, t):
                    act.wait_ge(self.gate_up, at(2 * n + t + 1, 2, it))
                    act.activation(all_th[:, t], ps[:, t, 0:BLK], ACT.Tanh, scale=0.5).then_inc(self.tanh, 1)

                def copy(n, it):
                    act.wait_ge(self.turned, at(n + 1, 1, it))
                    act.copy(all_hidT[:], ps[:, 2, :].rearrange("p (c s) -> p c s", c=2)).then_inc(self.hidT, 1)

                def step(n, it):
                    tanh(n, it, 0)
                    copy(n - 1, it)
                    tanh(n, it, 1)

                tanh(0, None, 0)
                tanh(0, None, 1)
                step(1, None)
                self.blocks_in_loop(act, step)
                copy(self.blocks - 1, None)

            def dve(self, dve):
                at = self.at

                def step(n, it):
                    for t in range(T):
                        dve.wait_ge(self.tanh, at(2 * n + t + 1, 2, it))
                        dve.scalar_tensor_tensor(out=all_a[:, t], in0=all_th[:, t], scalar=1.0, in1=ps[:, t, 0:BLK],
                                                 op0=ALU.add, op1=ALU.mult).then_inc(self.half, 1)
                        if n >= 2:
                            dve.wait_ge(self.turned, at(n - 1, 1, it))
                        dve.wait_ge(self.half, at(2 * n + t + 1, 2, it))
                        e = n // HALVES if it is None else n // HALVES + it * (4 // HALVES)
                        share = gate_half[:, t, bass.ds(e, 1)]
                        dve.scalar_tensor_tensor(out=all_hid[:, n % 2, t], in0=all_a[:, t], scalar=share,
                                                 in1=ps[:, t, BLK:2 * BLK], op0=ALU.mult,
                                                 op1=ALU.mult).then_inc(self.hid, 1)

                step(0, None)
                step(1, None)
                self.blocks_in_loop(dve, step)
                dve.wait_ge(down_used, EXPERTS // 2)

        class ExpertsStage:
            PAIRS = EXPERTS // 2

            def __init__(self):
                self.sel = sem("ge_sel_ready")
                self.share = sem("ge_share_ready")
                self.gathered = sem("ge_gathered")
                self.xT = sem("ge_xT_ready")
                self.tanh = sem("ge_tanh_ready")
                self.half = sem("ge_half")
                self.hid = sem("ge_hid_ready")
                self.share_turned = sem("ge_share_turned")
                self.turned = sem("ge_hid_turned")
                self.copied = sem("ge_turned_copied")
                self.half_down = sem("ge_half_down")
                self.y = sem("ge_y_ready")
                self.given = sem("ge_given_back")
                self.half_given = sem("ge_half_given")
                self.gated = sem("ge_gated")
                self.over = sem("ge_over")
                self.all_tokens = AllTokens(self)

            def either(self, eng, gathered, dense):
                many = eng.value_load(crowded[0:1, 0:1], min_val=0, max_val=1)
                with eng.If(many == 0):
                    gathered()
                with eng.Else():
                    dense()

            def pairs(self, eng, step):
                step(0, None)
                step(1, None)
                with eng.Fori(0, self.PAIRS - 3) as it:
                    step(2, it)
                step(self.PAIRS - 1, None)

            def pe(self, pe):
                at = per_round

                def gather(p, it):
                    pe.wait_ge(self.sel, at(p + 1, it, 1))
                    for k in range(KC):
                        for t in range(T):
                            last = pe.matmul(ps[:, 2 + k // 4, (k % 4) * P:(k % 4 + 1) * P], xn[:, t, k * P:(k + 1) * P], ge_sel[:, t],
                                             start=(t == 0), stop=(t == T - 1))
                    last.then_inc(self.gathered, 1)

                def gate_up(p, it, e):
                    wait_gate_up(pe, 2 * p + e, it)
                    if e == 0:
                        pe.wait_ge(self.xT, at(p + 1, it, 1))
                    for k in range(KC):
                        for f in range(HALVES):
                            out = ps[f * PLACES:(f + 1) * PLACES, 2 + e, :].rearrange("p (two f) -> p two f", two=2)
                            last = pe.matmul(out, ge_xT[:, k, e * PLACES:(e + 1) * PLACES],
                                             gate_up_rows(2 * p + e, k)[:, :, f * BLK:(f + 1) * BLK],
                                             start=(k == 0), stop=(k == KC - 1))
                    last.then_inc(gu_used, 1)

                def turn_shares(p, it):
                    pe.wait_ge(self.share, at(p + 1, it, 1))
                    if p >= 1:
                        pe.wait_ge(self.y, at(2 * p, it, 2))
                    for t in range(T):
                        last = pe.transpose(ps[:, 1, t * P:(t + 1) * P], ge_share[:, t], ident[:])
                    last.then_inc(self.share_turned, 1)

                def turn(p, it):
                    pe.wait_ge(self.hid, at(2 * p + 2, it, 2))
                    for e in range(2):
                        for c in range(2):
                            n = (2 * e + c) * P
                            last = pe.transpose(ps[:, 0, n:n + P], ge_hid[:, e, c * P:(c + 1) * P], ident[:])
                    last.then_inc(self.turned, 1)

                def down(p, it):
                    for e in range(2):
                        wait_down(pe, 2 * p + e, it)
                    pe.wait_ge(self.copied, at(2 * p + 2, it, 2))
                    for n in range(2):
                        for f in range(HALVES):
                            for c in range(2):
                                for e in range(2):
                                    last = pe.matmul(ps[e * PLACES:(e + 1) * PLACES, n, :], ge_hidT[:, e, c, f * PLACES:(f + 1) * PLACES],
                                                     down_rows(2 * p + e, 2 * f + c)[:, n * 512:(n + 1) * 512],
                                                     start=(f == 0 and c == 0), stop=(f == HALVES - 1 and c == 1))
                        last.then_inc(self.half_down if n == 0 else down_used, 1)

                def give_back(p, it):
                    for n in range(2):
                        pe.wait_ge(self.y, at(2 * p + n + 1, it, 2))
                        for t in range(T):
                            last = pe.matmul(ps[:, 4 + 2 * t + n, :], ge_shareT[:, t], ge_y[:, n],
                                             start=(p == 0), stop=(p == self.PAIRS - 1))
                        if n == 0 and p == self.PAIRS - 1:
                            last.then_inc(self.half_given, 1)
                    last.then_inc(self.given, 1)

                def step(p, it):
                    final_pair = p == self.PAIRS - 1
                    if final_pair:
                        give_back(p - 1, it)
                    gate_up(p, it, 0)
                    turn_shares(p, it)
                    gate_up(p, it, 1)
                    if p > 0 and not final_pair:
                        give_back(p - 1, it)
                    turn(p, it)
                    if p < self.PAIRS - 1:
                        gather(p + 1, it)
                    down(p, it)

                def gathered():
                    gather(0, None)
                    self.pairs(pe, step)
                    give_back(self.PAIRS - 1, None)

                self.either(pe, gathered, lambda: self.all_tokens.pe(pe))

            def act(self, act):
                at = per_round

                def copy_x(p, it):
                    act.wait_ge(self.gathered, at(p + 1, it, 1))
                    act.copy(ge_xT[:], ps[:, 2:4, :].rearrange("p b (k n) -> p (b k) n", k=4)).then_inc(self.xT, 1)

                def step(p, it):
                    for e in range(2):
                        act.wait_ge(gu_used, at(2 * p + e + 1, it, 2))
                        act.activation(ge_th[:, e], ps[:, 2 + e, 0:BLK], ACT.Tanh, scale=0.5).then_inc(self.tanh, 1)
                    act.wait_ge(self.share_turned, at(p + 1, it, 1))
                    if p > 0:
                        act.wait_ge(self.given, at(p, it, 1))
                    act.copy(ge_shareT[:], ps[:, 1, 0:T * P].rearrange("p (t n) -> p t n", t=T)).then_inc(self.copied, 1)
                    act.wait_ge(self.turned, at(p + 1, it, 1))
                    act.copy(ge_hidT[:], ps[:, 0, :].rearrange("p (e c n) -> p e c n", e=2, c=2)).then_inc(self.copied, 1)
                    if p < self.PAIRS - 1:
                        copy_x(p + 1, it)

                def gathered():
                    copy_x(0, None)
                    self.pairs(act, step)

                self.either(act, gathered, lambda: self.all_tokens.act(act))

            def dve(self, dve, own):
                at = per_round

                def columns(p, it):
                    for e in range(2):
                        for t in range(T):
                            c = bass.ds(at(2 * p + e, it, 2), 1)
                            yield t, slice(e * PLACES, (e + 1) * PLACES), place[:, t, c], gate_half[:, t, c]

                def select(p, it):
                    for t, cut, where, _ in columns(p, it):
                        last = dve.tensor_scalar(ge_sel[:, t, cut], places[:], where, None, ALU.is_equal)
                    last.then_inc(self.sel, 1)

                def shares(p, it):
                    if p >= 1:
                        dve.wait_ge(self.share_turned, at(p, it, 1))
                    for t, cut, where, share in columns(p, it):
                        last = dve.tensor_scalar(ge_share[:, t, cut], places[:], where, share, ALU.is_equal, ALU.mult)
                    last.then_inc(self.share, 1)

                def copy_y(p, it):
                    for n, made in enumerate((self.half_down, down_used)):
                        dve.wait_ge(made, at(p + 1, it, 1))
                        dve.tensor_copy(ge_y[:, n], ps[:, n, :]).then_inc(self.y, 1)

                def hidden(p, it, e):
                    n = at(2 * p + e + 1, it, 2)
                    dve.wait_ge(self.tanh, n)
                    dve.scalar_tensor_tensor(out=ge_a[:], in0=ge_th[:, e], scalar=1.0, in1=ps[:, 2 + e, 0:BLK], op0=ALU.add,
                                             op1=ALU.mult).then_inc(self.half, 1)
                    dve.wait_ge(self.half, n)
                    dve.tensor_tensor(ge_hid[:, e], ge_a[:], ps[:, 2 + e, BLK:2 * BLK], ALU.mult).then_inc(self.hid, 1)
                    dve.wait_ge(self.hid, n)

                def step(p, it):
                    if p > 0:
                        copy_y(p - 1, it)
                    else:
                        dve.wait_ge(self.gathered, 1)
                    if p < self.PAIRS - 1:
                        select(p + 1, it)
                    hidden(p, it, 0)
                    if p < self.PAIRS - 1:
                        shares(p + 1, it)
                    hidden(p, it, 1)

                def gathered():
                    select(0, None)
                    shares(0, None)
                    self.pairs(dve, step)
                    copy_y(self.PAIRS - 1, None)
                    dve.wait_ge(self.half_given, 1)
                    through_gate(lambda: dve.wait_ge(self.given, self.PAIRS))

                def through_gate(wait_rest=None):
                    for half in range(2):
                        cut = slice(half * 512, (half + 1) * 512)
                        if half == 1 and wait_rest is not None:
                            wait_rest()
                        for t in range(T):
                            dve.tensor_tensor(xn[:, t, cut], ps[:, 4 + 2 * t + half, :], g_bc[:, 1, cut], ALU.mult).then_inc(self.gated, 1)
                            dve.wait_ge(self.gated, T * half + t + 1)
                            ins = dve.tensor_tensor(h[:, t, cut], h[:, t, cut], xn[:, t, cut], ALU.add)
                            if half == 1:
                                ins.then_inc(self.over, 1)

                def dense():
                    self.all_tokens.dve(dve)
                    through_gate()

                self.either(dve, gathered, dense)

        class FinalStage:
            def __init__(self):
                self.squares, self.rstd, self.gained = sem("fin_squares"), sem("fin_rstd"), sem("fin_gained")
                self.made = [sem(f"fin_made{t}") for t in range(T)]
                self.f_landed = sem("fin_gain_landed")

            def load(self, act):
                act.dma_start(f_bc[:], a["final_g_2"].partition_broadcast(P)).then_inc(self.f_landed, 16)

            def act(self, act):
                for t in range(T):
                    act.wait_ge(moe.over, t + 1)
                    act.activation(xn[:, t], h[:, t], ACT.Square, scale=float(D) ** -0.5,
                                   accum_out=ms[:, t:t + 1]).then_inc(self.squares, 1)

                act.wait_ge(self.rstd, 1)
                act.wait_ge(self.gained, 1)
                act.activation(xn[:, 0], xn[:, 0], ACT.Copy, scale=rs[:, 0:1]).then_inc(self.made[0], 1)

            def dve(self, dve, own):
                dve.wait_ge(self.f_landed, 16)
                dve.wait_ge(self.squares, 1)
                dve.tensor_tensor(xn[:, 0], h[:, 0], f_bc[:], ALU.mult).then_inc(self.gained, 1)
                dve.wait_ge(self.squares, T)
                rsqrt_ms(dve, own, T, self.rstd)
                dve.wait_ge(self.rstd, 1)
                dve.scalar_tensor_tensor(out=xn[:, 1], in0=h[:, 1], scalar=rs[:, 1:2], in1=f_bc[:], op0=ALU.mult,
                                         op1=ALU.mult).then_inc(self.made[1], 1)

            def store(self, sp):
                o = out[0].rearrange("(t p) d -> p t d", p=P)
                for t in range(T):
                    sp.wait_ge(self.made[t], 1)
                    sp.dma_start(o[:, t], xn[:, t]).then_inc(out_landed, 16)
                sp.wait_ge(out_landed, 16 * T)

        setup = SetupStage()
        norms = [NormStage(0, lambda c: col("g_mix", c)),
                 NormStage(1, lambda c: col("g_ffn", c), folded=True),
                 NormStage(2, lambda c: col("g_ple", c), folded=True),
                 NormStage(3, lambda c: col("g_mix", KC + c), folded=True),
                 NormStage(4, lambda c: col("g_ffn", KC + c), folded=True),
                 NormStage(5, lambda c: col("g_ple", KC + c), folded=True),
                 NormStage(6, lambda c: mod_cols[:, 1, c:c + 1], lambda c: mod_cols[:, 0, c:c + 1]),
                 NormStage(7, lambda c: mod_cols[:, 3, c:c + 1], lambda c: mod_cols[:, 2, c:c + 1], split=False)]
        even = EvenStage()
        ffn = [FfnStage(0, norms[1]), FfnStage(1, norms[4], ada_products)]
        ple = [PleStage(0, norms[2]), PleStage(1, norms[5], lambda dve, i: ada_products(dve, FF_BLOCKS - 1 + i, None))]
        odd_up = OddUp()
        odd_in = odd_up.z = OddIn(norms[3], odd_up)
        odd_heads, odd_attend, odd_out = OddHeads(odd_up), OddAttend(), OddOut()
        mod, conformer, route, final = ModStage(), ConformerStage(), RouteStage(), FinalStage()
        moe = ExpertsStage()

        block = ctx.enter_context(nc.Block())

        @block.scalar
        def _(act):
            norms[0].act(act, ("ev_in", 0, 3), setup.act_columns)
            even.act(act)
            norms[1].act(act, ("ffn0", 0, 2))
            ffn[0].act(act)
            norms[2].act(act)
            ple[0].act(act)
            norms[3].act(act, ("od_in", 0, 2))
            odd_in.act(act)
            odd_up.act(act)
            odd_heads.act(act)
            odd_attend.act(act)
            odd_out.act(act)
            norms[4].act(act, ("ffn1", 0, 2))
            mod.load(act)
            ffn[1].act(act)
            norms[5].act(act)
            ple[1].act(act)
            norms[6].act(act, ("conv_in", 0, 3), lambda eng: eng.wait_ge(mod.cols, 1))
            conformer.act(act)
            norms[7].act(act)
            final.load(act)
            route.act(act)
            moe.act(act)
            final.act(act)

        @block.gpsimd
        def _(pool):
            setup.pool(pool)
            odd_in.pool(pool)
            for _ in range(2):
                stage_end(pool)
            ada_loads(pool)
            stage_end(pool)

        @block.tensor
        def _(pe):
            norms[0].pe(pe, setup.pe)
            even.pe(pe)
            norms[1].pe(pe)
            ffn[0].pe(pe)
            norms[2].pe(pe)
            ple[0].pe(pe)
            norms[3].pe(pe)
            odd_in.pe(pe)
            odd_up.pe(pe)
            odd_heads.pe(pe)
            odd_attend.pe(pe)
            odd_out.pe(pe)
            norms[4].pe(pe)
            ffn[1].pe(pe)
            norms[5].pe(pe)
            ple[1].pe(pe)
            mod.pe(pe)
            norms[6].pe(pe)
            conformer.pe(pe)
            norms[7].pe(pe)
            route.pe(pe)
            moe.pe(pe)

        @block.vector
        def _(dve):
            own = Own(dve, dve_own)
            norms[0].dve(dve, own, ("ev_in", 0, 3))
            even.dve(dve, own)
            norms[1].dve(dve, own, ("ffn0", 0, 2))
            ffn[0].dve(dve, own)
            norms[2].dve(dve, own)
            ple[0].dve(dve, own)
            norms[3].dve(dve, own, ("od_in", 0, 2))
            odd_in.dve(dve, own)
            odd_up.dve(dve, own)
            odd_heads.dve(dve, own)
            odd_attend.dve(dve, own)
            odd_out.dve(dve, own)
            norms[4].dve(dve, own, ("ffn1", 0, 2))
            ffn[1].dve(dve, own)
            norms[5].dve(dve, own)
            ple[1].dve(dve, own)
            norms[6].dve(dve, own, ("conv_in", 0, 3), lambda eng: mod.dve_cols(eng, own))
            mod.dve_rows(dve)
            conformer.dve(dve, own)
            norms[7].dve(dve, own)
            route.dve(dve, own)
            moe.dve(dve, own)
            final.dve(dve, own)

        @block.sync
        def _(sp):
            setup.load_stream(sp)
            weight_stream(sp)
            final.store(sp)


_INS = ["x", "p", "positions", "g_mix", "g_ffn", "g_ple", "ev_w_in", "ev_w_conv", "ev_g_v", "ev_w_s", "ev_b_s", "ev_w_out",
        "od_w_in", "od_b_gate", "od_g_qa", "od_g_kva", "od_w_q_up", "od_w_kv_up", "od_g_q", "od_g_k", "od_g_mh", "od_w_out",
        "w_gate", "w_up", "w_down", "w_ple_proj", "w_ple_gate", "c_2", "ada_w_2", "ada_b_2", "norm_mix_g_2",
        "norm_ffn_g_2", "final_g_2", "conv_w_in_2", "conv_b_in_2", "conv_w_dw_2", "conv_b_dw_2", "conv_ln_g_2",
        "conv_ln_b_2", "conv_w_out_2", "moe_w_rg_2", "moe_b_rg_2", "moe_w_re_2", "moe_b_re_2", "moe_w_gate_2",
        "moe_w_up_2", "moe_w_down_2"]


def kernel(**inputs):
    import numpy as _np
    import concourse.bacc as _bacc
    from concourse import mybir as _mybir
    from concourse.bass_utils import run_bass_kernel_spmd as _run

    nc = _bacc.Bacc("TRN2", target_bir_lowering=False, num_devices=1)
    arrays, args = {}, {}
    for name in _INS:
        v = _np.ascontiguousarray(inputs[name])
        arrays[f"in_{name}"] = v
        args[name] = nc.dram_tensor(f"in_{name}", v.shape, _mybir.dt.from_np(v.dtype), kind="ExternalInput").ap()
    out = nc.dram_tensor("out", (1, S, D), F32, kind="ExternalOutput").ap()
    build(nc, args, out)
    r = _run(nc, [arrays], core_ids=[0])
    return r.results[0]["out"]
```
